# Optimizing a Trainium2 kernel written in Bass

```python
import jax, jax.numpy as jnp
from jax import lax
import numpy as np

D_MODEL = 1024
BATCH = 1
SEQ = 512
DEPTH = 1

CONV_WIDTH = 512
CONV_KERNEL = 31
N_HEADS = 8
HEAD_K = 64
HEAD_V = 64
KEY_DIM = N_HEADS * HEAD_K
VAL_DIM = N_HEADS * HEAD_V
SHORT_CONV = 4
CHUNK = 64
N_GROUPS = 4
EXPERTS_PER_GROUP = 8
N_EXPERTS = N_GROUPS * EXPERTS_PER_GROUP
TOP_K = 2
D_EXPERT = 256
EPS = 1e-6

IN_SPLITS = (2 * CONV_WIDTH, KEY_DIM, KEY_DIM, VAL_DIM, VAL_DIM, N_HEADS, N_HEADS, D_MODEL, D_MODEL)
D_IN = 2 * CONV_WIDTH + 2 * KEY_DIM + 2 * VAL_DIM + 2 * N_HEADS + 2 * D_MODEL

kernel_name = 'hybrid_conformer_gdn_hiermoe'

def split_cols(z, sizes):
    offs = [int(o) for o in np.cumsum(sizes)[:-1]]
    return jnp.split(z, offs, axis=-1)

def rms_norm(x, gain):
    x32 = x.astype(jnp.float32)
    y = x32 * lax.rsqrt(jnp.mean(x32 * x32, axis=-1, keepdims=True) + EPS)
    return (y * gain.astype(jnp.float32)).astype(x.dtype)

def layer_norm(x, gain, bias):
    x32 = x.astype(jnp.float32)
    mu = jnp.mean(x32, axis=-1, keepdims=True)
    xc = x32 - mu
    y = xc * lax.rsqrt(jnp.mean(xc * xc, axis=-1, keepdims=True) + EPS)
    return (y * gain.astype(jnp.float32) + bias.astype(jnp.float32)).astype(x.dtype)

def l2_normalize(x):
    x32 = x.astype(jnp.float32)
    return x32 * lax.rsqrt(jnp.sum(x32 * x32, axis=-1, keepdims=True) + EPS)

def causal_depthwise_conv(x, w):
    k, c = w.shape
    return lax.conv_general_dilated(
        x, w.reshape(k, 1, c).astype(x.dtype), window_strides=(1,),
        padding=((k - 1, 0),), dimension_numbers=('NWC', 'WIO', 'NWC'),
        feature_group_count=c)

def to_chunks(t):
    b, t_len, h, d = t.shape
    return t.reshape(b, t_len // CHUNK, CHUNK, h, d).transpose(1, 0, 3, 2, 4)

def gated_delta_rule(q, k, v, beta, g):
    b, t_len, h, dk = q.shape
    dv = v.shape[-1]
    qc, kc, vc = to_chunks(q), to_chunks(k), to_chunks(v)
    bc = to_chunks(beta[..., None])[..., 0]
    gcum = jnp.cumsum(to_chunks(g[..., None])[..., 0], axis=-1)
    causal = jnp.tril(jnp.ones((CHUNK, CHUNK), dtype=bool))
    strict = jnp.tril(jnp.ones((CHUNK, CHUNK), dtype=bool), -1)
    decay = jnp.exp(jnp.where(causal, gcum[..., :, None] - gcum[..., None, :], -jnp.inf))
    kk = jnp.einsum('nbhid,nbhjd->nbhij', kc, kc)
    lower = jnp.where(strict, bc[..., :, None] * kk * decay, 0.0)
    eye = jnp.eye(CHUNK, dtype=jnp.float32)
    rhs = jnp.concatenate([vc * bc[..., None], kc * (bc * jnp.exp(gcum))[..., None]], axis=-1)
    sol = lax.linalg.triangular_solve(lower + eye, rhs, left_side=True, lower=True, unit_diagonal=True)
    u, w = sol[..., :dv], sol[..., dv:]
    qk = jnp.einsum('nbhid,nbhjd->nbhij', qc, kc) * decay
    q_dec = qc * jnp.exp(gcum)[..., None]
    k_dec = kc * jnp.exp(gcum[..., -1:] - gcum)[..., None]
    g_last = jnp.exp(gcum[..., -1])

    def step(state, xs):
        qk_i, q_i, k_i, u_i, w_i, gl = xs
        v_new = u_i - jnp.einsum('bhck,bhkv->bhcv', w_i, state)
        o = jnp.einsum('bhck,bhkv->bhcv', q_i, state) + jnp.einsum('bhij,bhjv->bhiv', qk_i, v_new)
        state = state * gl[..., None, None] + jnp.einsum('bhck,bhcv->bhkv', k_i, v_new)
        return state, o

    s0 = jnp.zeros((b, h, dk, dv), dtype=jnp.float32)
    _, o = lax.scan(step, s0, (qk, q_dec, k_dec, u, w, g_last))
    return o.transpose(1, 0, 3, 2, 4).reshape(b, t_len, h, dv)

def hybrid_mixer(h, w_in, conv_dw_w, conv_dw_b, conv_ln_gain, conv_ln_bias, w_conv_out,
                 gdn_conv_w, gdn_a_log, gdn_dt_bias, gdn_norm_gain, w_gdn_out, w_out):
    bsz, t_len, _ = h.shape
    z = h @ w_in
    c_in, q, k, v, zg, b_raw, a_raw, gate_c, gate_d = split_cols(z, IN_SPLITS)

    u = c_in[..., :CONV_WIDTH] * jax.nn.sigmoid(c_in[..., CONV_WIDTH:])
    u = causal_depthwise_conv(u, conv_dw_w) + conv_dw_b.astype(u.dtype)
    u = jax.nn.silu(layer_norm(u, conv_ln_gain, conv_ln_bias))
    y_conv = u @ w_conv_out

    qkv = jax.nn.silu(causal_depthwise_conv(jnp.concatenate([q, k, v], axis=-1), gdn_conv_w))
    q, k, v = split_cols(qkv, (KEY_DIM, KEY_DIM, VAL_DIM))
    q = l2_normalize(q.reshape(bsz, t_len, N_HEADS, HEAD_K)) * (HEAD_K ** -0.5)
    k = l2_normalize(k.reshape(bsz, t_len, N_HEADS, HEAD_K))
    v = v.reshape(bsz, t_len, N_HEADS, HEAD_V).astype(jnp.float32)
    beta = jax.nn.sigmoid(b_raw.astype(jnp.float32))
    g = -jnp.exp(gdn_a_log.astype(jnp.float32)) * jax.nn.softplus(
        a_raw.astype(jnp.float32) + gdn_dt_bias.astype(jnp.float32))
    o = gated_delta_rule(q, k, v, beta, g)
    o = rms_norm(o, gdn_norm_gain) * jax.nn.silu(zg.reshape(bsz, t_len, N_HEADS, HEAD_V).astype(jnp.float32))
    y_delta = o.reshape(bsz, t_len, VAL_DIM).astype(h.dtype) @ w_gdn_out

    y = jax.nn.sigmoid(gate_c) * y_conv + jax.nn.sigmoid(gate_d) * y_delta
    return y @ w_out

def hierarchical_moe(h, w_router_group, b_router_group, w_router_expert, b_router_expert,
                     w_expert_gate, w_expert_up, w_expert_down):
    bsz, t_len, d = h.shape
    t = h.reshape(-1, d)
    n_tok = t.shape[0]
    group_p = jax.nn.softmax((t @ w_router_group).astype(jnp.float32) + b_router_group.astype(jnp.float32), axis=-1)
    gp, gi = lax.top_k(group_p, 1)
    exp_logits = ((t @ w_router_expert).astype(jnp.float32) + b_router_expert.astype(jnp.float32)
                  ).reshape(n_tok, N_GROUPS, EXPERTS_PER_GROUP)
    sel = jnp.take_along_axis(exp_logits, gi[:, :, None], axis=1)[:, 0]
    ep = jax.nn.softmax(sel, axis=-1)
    ev, ei = lax.top_k(ep, TOP_K)
    ev = ev / jnp.sum(ev, axis=-1, keepdims=True)
    weights = gp * ev
    expert_id = gi * EXPERTS_PER_GROUP + ei
    combine = jnp.sum(jax.nn.one_hot(expert_id, N_EXPERTS, dtype=jnp.float32) * weights[..., None], axis=1)
    combine = combine.astype(t.dtype)
    out = jnp.zeros_like(t)
    for e in range(N_EXPERTS):
        hid = jax.nn.silu(t @ w_expert_gate[e]) * (t @ w_expert_up[e])
        out = out + combine[:, e:e + 1] * (hid @ w_expert_down[e])
    return out.reshape(bsz, t_len, d)

def setup_inputs(seed: int = 0) -> dict:
    key = jax.random.key(seed)
    ks = jax.random.split(key, 24)
    L = DEPTH

    def nrm(k, shape, scale):
        return jax.random.normal(k, shape, dtype=jnp.float32) * scale

    def gain(k, shape):
        return 1.0 + 0.01 * jax.random.normal(k, shape, dtype=jnp.float32)

    dt = jnp.exp(jax.random.uniform(ks[12], (L, N_HEADS), minval=np.log(1e-3), maxval=np.log(1e-1)))
    return {
        'x': nrm(ks[0], (BATCH, SEQ, D_MODEL), 1.0),
        'norm_mix_gain': gain(ks[1], (L, D_MODEL)),
        'w_in': nrm(ks[2], (L, D_MODEL, D_IN), D_MODEL ** -0.5),
        'conv_dw_w': nrm(ks[3], (L, CONV_KERNEL, CONV_WIDTH), CONV_KERNEL ** -0.5),
        'conv_dw_b': nrm(ks[4], (L, CONV_WIDTH), 0.01),
        'conv_ln_gain': gain(ks[5], (L, CONV_WIDTH)),
        'conv_ln_bias': nrm(ks[6], (L, CONV_WIDTH), 0.01),
        'w_conv_out': nrm(ks[7], (L, CONV_WIDTH, D_MODEL), CONV_WIDTH ** -0.5),
        'gdn_conv_w': nrm(ks[8], (L, SHORT_CONV, 2 * KEY_DIM + VAL_DIM), SHORT_CONV ** -0.5),
        'gdn_a_log': jnp.log(jax.random.uniform(ks[9], (L, N_HEADS), minval=1.0, maxval=16.0)),
        'gdn_dt_bias': jnp.log(jnp.expm1(dt)),
        'gdn_norm_gain': gain(ks[10], (L, HEAD_V)),
        'w_gdn_out': nrm(ks[11], (L, VAL_DIM, D_MODEL), VAL_DIM ** -0.5),
        'w_out': nrm(ks[13], (L, D_MODEL, D_MODEL), D_MODEL ** -0.5),
        'norm_ffn_gain': gain(ks[14], (L, D_MODEL)),
        'w_router_group': nrm(ks[15], (L, D_MODEL, N_GROUPS), D_MODEL ** -0.5),
        'b_router_group': nrm(ks[16], (L, N_GROUPS), 0.01),
        'w_router_expert': nrm(ks[17], (L, D_MODEL, N_EXPERTS), D_MODEL ** -0.5),
        'b_router_expert': nrm(ks[18], (L, N_EXPERTS), 0.01),
        'w_expert_gate': nrm(ks[19], (L, N_EXPERTS, D_MODEL, D_EXPERT), D_MODEL ** -0.5),
        'w_expert_up': nrm(ks[20], (L, N_EXPERTS, D_MODEL, D_EXPERT), D_MODEL ** -0.5),
        'w_expert_down': nrm(ks[21], (L, N_EXPERTS, D_EXPERT, D_MODEL), D_EXPERT ** -0.5),
        'final_norm_gain': gain(ks[22], (D_MODEL,)),
    }

def reference(x, norm_mix_gain, w_in, conv_dw_w, conv_dw_b, conv_ln_gain, conv_ln_bias, w_conv_out,
              gdn_conv_w, gdn_a_log, gdn_dt_bias, gdn_norm_gain, w_gdn_out, w_out,
              norm_ffn_gain, w_router_group, b_router_group, w_router_expert, b_router_expert,
              w_expert_gate, w_expert_up, w_expert_down, final_norm_gain):
    for l in range(DEPTH):
        h = rms_norm(x, norm_mix_gain[l])
        x = x + hybrid_mixer(h, w_in[l], conv_dw_w[l], conv_dw_b[l], conv_ln_gain[l], conv_ln_bias[l],
                             w_conv_out[l], gdn_conv_w[l], gdn_a_log[l], gdn_dt_bias[l], gdn_norm_gain[l],
                             w_gdn_out[l], w_out[l])
        h = rms_norm(x, norm_ffn_gain[l])
        x = x + hierarchical_moe(h, w_router_group[l], b_router_group[l], w_router_expert[l],
                                 b_router_expert[l], w_expert_gate[l], w_expert_up[l], w_expert_down[l])
    return rms_norm(x, final_norm_gain)


_drawn_inputs = setup_inputs


def setup_inputs(seed=0):
    import zlib

    import numpy as np

    out = dict(_drawn_inputs(seed))
    spreads = {}
    factors = {'norm_mix_gain': 3.958,
     'conv_dw_b': 3.702,
     'conv_ln_gain': 5.928,
     'conv_ln_bias': 6.505,
     'gdn_norm_gain': 3.866,
     'norm_ffn_gain': 3.301,
     'b_router_group': 5.264,
     'b_router_expert': 3.43,
     'final_norm_gain': 5.655}
    for name, (base, spread) in spreads.items():
        noise = np.random.default_rng([zlib.crc32(name.encode()), seed]).standard_normal(out[name].shape)
        drawn = base * np.exp(spread * noise) if base else spread * noise
        out[name] = __import__('jax').numpy.asarray(drawn.astype(out[name].dtype))
    for name, factor in factors.items():
        out[name] = (out[name] * factor).astype(out[name].dtype)
    return out
```

```python
from contextlib import ExitStack

import concourse.bass as bass
from concourse import mybir

F32 = mybir.dt.float32
I32 = mybir.dt.int32
ACT = mybir.ActivationFunctionType
ALU = mybir.AluOpType
AX = mybir.AxisListType

P = 128
EPS = 1e-6
NEG = -1e30


class Signals:

    def __init__(self, nc, ctx):
        self.nc, self.ctx, self.sems, self.count = nc, ctx, {}, {}

    def __getitem__(self, name):
        if name not in self.sems:
            self.sems[name] = self.ctx.enter_context(self.nc.semaphore(name))
        return self.sems[name]

    def tell(self, ins, name, by=1):
        ins.then_inc(self[name], by)
        self.count[name] = self.count.get(name, 0) + by
        return self.count[name]


def hybrid_layer(nc, a, out, sorted_h, sorted_y, CAP):
    _, T, D = a["x"].shape
    KT = D // P
    NT = T // P
    CW = a["w_conv_out"].shape[1]
    TAPS = a["conv_dw_w"].shape[1]
    CF = CW // P
    H = a["gdn_a_log"].shape[1]
    VD = a["w_gdn_out"].shape[1]
    DK = VD // H
    NP = H // 2
    ST = a["gdn_conv_w"].shape[1]
    NG = a["w_router_group"].shape[2]
    NE = a["w_router_expert"].shape[2]
    EG = NE // NG
    DE = a["w_expert_gate"].shape[3]
    JE = DE // P
    HALF = 512
    NH2 = D // HALF
    WSLOT = KT * HALF
    ESLOT = 3 * KT * DE
    UN = 4
    LV = 7
    GRP = 4
    NR = NG + NE

    C_CONV, C_Q = 0, 2 * CW
    C_K, C_V, C_ZG = C_Q + VD, C_Q + 2 * VD, C_Q + 3 * VD
    C_AB = C_Q + 4 * VD
    C_GC, C_GD = C_AB + 2 * H, C_AB + 2 * H + D

    with ExitStack() as ctx:
        S = Signals(nc, ctx)
        tell = S.tell

        def wait(eng, name, n):
            if not isinstance(n, int) or n > 0:
                eng.wait_ge(S[name], n)

        top = [0]
        ARENA = 52800
        arena = ctx.enter_context(nc.sbuf_tensor("arena", [P, ARENA], F32))
        slot_idx = ctx.enter_context(nc.sbuf_tensor("slot_idx", [P, NT, 2, 2], I32))
        flag_i = ctx.enter_context(nc.sbuf_tensor("flag_i", [1, 1], I32))

        def take(n):
            top[0] += n
            assert top[0] <= ARENA, top[0]
            return top[0] - n

        def at(off, *shape):
            n = 1
            for s in shape:
                n *= s
            v = arena[:, off:off + n]
            if len(shape) == 1:
                return v
            names = "abcd"[:len(shape)]
            return v.rearrange(f"p ({' '.join(names)}) -> p {' '.join(names)}", **dict(zip(names[1:], shape[1:])))

        R_HT = take(KT * T)
        R_RING = take(3 * WSLOT)
        R_SIG = take(2 * KT * T)
        R_EXP = take(0)
        R_QK = take(2 * NP * T)
        R_VTOK = take(NT * VD)
        R_KDEC = take(NT * VD)
        R_QKT = take(H * T)
        R_U = take(H * T)
        R_ZG = take(NT * VD)
        assert top[0] - R_EXP >= 3 * ESLOT
        R_UP = take(CF * (T + TAPS - 1))
        R_ACC = take(CF * T)
        R_TMP = take(4 * T)

        hT = at(R_HT, KT, T)
        x1 = at(R_HT, NT, D)
        wring = [at(R_RING + i * WSLOT, KT, HALF) for i in range(3)]
        xs = at(R_SIG, NT, D)
        dwstage = at(R_SIG + NT * D, CW)
        gcstage = at(R_SIG + NT * D + CW, 3 * VD)
        vT = at(R_SIG, NP, T)
        Tm = at(R_SIG, GRP, NT, P)
        Xm = at(R_SIG + GRP * T, GRP, NT, P)
        MT = at(R_SIG + 2 * GRP * T, GRP, NT, P)
        BT = at(R_SIG + 3 * GRP * T, GRP, NT, P)
        sig = [at(R_SIG, KT, T), at(R_SIG + KT * T, KT, T)]
        yT = sig[0]
        kT = at(R_QK, NP, T)
        qT = at(R_QK + NP * T, NP, T)
        vtok = at(R_VTOK, NT, VD)
        kdec = at(R_KDEC, NT, VD)
        qkT = at(R_QKT, H, NT, P)
        NPAD = T + ST - 1
        pad = [at(R_QKT + i * NPAD, NPAD) for i in range(3)]
        cacc = [at(R_QKT + 3 * NPAD + i * T, T) for i in range(3)]
        U = at(R_U, H, NT, P)
        zgs = at(R_ZG, NT, VD)
        upad = at(R_UP, CF, T + TAPS - 1)
        oTc = [at(R_VTOK + c * VD, NP, P) for c in range(NT)]
        oT = vtok.rearrange("p c (f n) -> p f c n", f=NP)
        acc = at(R_ACC, CF, T)
        gb = [at(R_TMP + i * T, NT, P) for i in range(2)]
        dec = [at(R_TMP + (2 + i) * T, NT, P) for i in range(2)]
        sq = [at(R_TMP + i * T, NT, 2, DK) for i in range(2)]
        sgl = [at(R_TMP + (2 + i) * T, T) for i in range(2)]
        rbuf, vn, o_t, o_s = (at(R_TMP + i * T, T) for i in range(4))
        lnm, lnv = at(R_TMP, T), at(R_TMP + T, T)
        lsq = [at(R_TMP + (2 + i) * T, T) for i in range(2)]

        ident = at(take(P), P)
        triu = at(take(P), P)
        triu_s = at(take(P), P)
        negm = at(take(P), P)
        ones = at(take(P), P)
        mean_w = at(take(P), P)
        lmask = at(take(LV * P), LV, P)
        Sst = at(take(NP * P), NP, P)
        par = at(take(CF * (TAPS + 3) + 3 * NP * ST), CF * (TAPS + 3) + 3 * NP * ST)
        g1 = at(take(KT), KT)
        wab = at(take(KT * 2 * H), KT, 2 * H)
        absb = at(take(NT * 2 * H), NT, 2 * H)
        alog = at(take(H), H)
        dtb = at(take(H), H)
        gng = at(take(DK), DK)
        SC = NT * H

        def tok(n=1):
            return at(take(SC), NT, H)

        beta, gt, y_sp, sp_a, sp_b, gcum, glast, eg, egl, kds, nk, nq, rk, rq, brk, brk2 = (tok() for _ in range(16))
        gls = at(take(NT * NP), NT, NP)
        epsb = at(take(1), 1)
        epsb64 = at(take(1), 1)
        ssk = tok()
        ssq = tok()
        oss = at(take(NT * H), NT, H)
        ors = at(take(NT * H), NT, H)
        sm = {n: at(take(NT), NT) for n in ("ss1", "r1", "ss2", "r2", "ss3", "r3", "gm", "gs", "gp", "m1", "m2", "w1",
                                            "w2", "tt", "p1", "p2", "s1", "s2", "v1", "v2", "ix", "mx")}

        eslot = [R_EXP + i * ESLOT for i in (1, 2, 0)] + [R_RING]
        wg = [at(o, KT, DE) for o in eslot]
        wu = [at(o + KT * DE, KT, DE) for o in eslot]
        wd = [at(o + 2 * KT * DE, JE, D) for o in eslot]
        ysb = [at(R_RING + ESLOT + i * D, D) for i in range(2)]
        R_S2 = R_RING + 2 * WSLOT
        gain2 = at(R_S2, D)
        gain3 = at(R_S2 + D, D)
        wr = at(R_S2 + 2 * D, KT, NR)
        o2 = R_S2 + 2 * D + KT * NR
        heT = [at(o2 + i * KT * CAP, KT, CAP) for i in range(2)]
        assert o2 + 2 * KT * CAP <= R_RING + 3 * WSLOT
        hs = [at(R_SIG + i * D, D) for i in range(UN)]
        h2T = at(R_SIG + KT * T, KT, T)
        h2 = at(R_UP, NT, D)
        rt = R_TMP
        NRT = NT * NE

        def rte(i):
            return at(rt + i * NRT, NT, NE)

        lg = at(rt + 10 * NRT, NT, NR)
        le, oh1, oh2, pos, Mx, cov, rtmp, desc, iota_c = (rte(i) for i in range(9))
        rtmp2 = rte(9)
        ohg = at(rt + 10 * NRT + NT * NR, NT, NG)
        dg = at(rt + 10 * NRT + NT * NR + NT * NG, NT, NG)
        rbias = at(rt + 10 * NRT + NT * NR + 2 * NT * NG, NR)
        descg = at(rt + 10 * NRT + NT * NR + 2 * NT * NG + NR, NT, NG)
        ovf = at(rt + 10 * NRT + NT * NR + 3 * NT * NG + NR, 2)
        e0 = rt + 10 * NRT + NT * NR + 3 * NT * NG + NR + 2
        sil = at(rt, 2, JE * CAP)
        hid = at(e0, 2, JE * CAP)
        assert e0 + 2 * JE * CAP <= rt + 4 * T and 2 * JE * CAP <= 3 * NRT * 2, (e0 + 2 * JE * CAP - rt)
        osil = at(R_RING + ESLOT, T)
        ohid = at(R_SIG, JE, T)
        zero = at(R_ZG, D)
        gath = [at(R_EXP + i * D, D) for i in range(2 * NT)]

        bank = [ctx.enter_context(nc.psum_tensor(f"bank{i}", [P, 512], F32))[:, :] for i in range(8)]

        def bc(ap, shape):
            return ap.to_broadcast(shape)

        def heads(v):
            return v.rearrange("p (h d) -> p h d", h=H)

        def per_head(s, c):
            return bc(s[:, c, :].unsqueeze(2), [P, H, DK])

        jobs = {}

        win = a["w_in"][0].rearrange("(p k) n -> p k n", k=KT)
        chunks = [("k", win[:, :, C_K:C_K + VD]), ("q", win[:, :, C_Q:C_Q + VD]), ("v", win[:, :, C_V:C_V + VD]),
                  ("cb", win[:, :, CW:2 * CW]), ("ca", win[:, :, 0:CW]), ("zg", win[:, :, C_ZG:C_ZG + VD]),
                  ("gc0", win[:, :, C_GC:C_GC + HALF]), ("gc1", win[:, :, C_GC + HALF:C_GC + D]),
                  ("gd0", win[:, :, C_GD:C_GD + HALF]), ("gd1", win[:, :, C_GD + HALF:C_GD + D]),
                  ("wco", a["w_conv_out"][0].rearrange("(f p) n -> p f n", p=P)),
                  ("wgo", a["w_gdn_out"][0].rearrange("(f p) n -> p f n", p=P)),
                  ("wo0", a["w_out"][0].rearrange("(k p) n -> p k n", p=P)[:, :, 0:HALF]),
                  ("wo1", a["w_out"][0].rearrange("(k p) n -> p k n", p=P)[:, :, HALF:D])]
        cidx = {n: i for i, (n, _) in enumerate(chunks)}

        block = ctx.enter_context(nc.Block())

        @block.tensor
        def _(pe):
            used = [None] * 8
            nxt = [0]

            def begin(name, freed_by, b=None):
                if b is None:
                    b = nxt[0] % 8
                    nxt[0] += 1
                if used[b] is not None:
                    wait(pe, *used[b])
                used[b] = freed_by
                jobs[name] = [b, None, None]
                return bank[b]

            def end(ins, name, fam):
                n = tell(ins, fam)
                jobs[name][1:] = [fam, n]

            wait(pe, "consts", 2)
            for k in range(KT):
                b = begin(("hT", k), ("hT_act" if k % 2 == 0 else "hT_dve", k // 2 + 1))
                for c in range(NT):
                    if k == 0:
                        wait(pe, "xs_ready", c + 1)
                    ins = pe.transpose(b[:, c * P:(c + 1) * P], xs[:, c, :].rearrange("p (q k) -> p k q", k=KT)[:, k, :],
                                       ident)
                end(ins, ("hT", k), "setup_mm")
            b = begin("par", ("setup_ready", 1))
            wait(pe, "ld_stage", 80)
            NS = TAPS + 3
            for i in range(CF):
                pe.transpose(b[:, i * NS:(i + 1) * NS], dwstage[0:NS, i * P:(i + 1) * P], ident[0:NS, 0:NS])
            for f in range(3 * NP):
                o = CF * NS + f * ST
                ins = pe.transpose(b[:, o:o + ST], gcstage[0:ST, f * P:(f + 1) * P], ident[0:ST, 0:ST])
            end(ins, "par", "setup_mm")
            wait(pe, "hT_act", KT // 2)
            wait(pe, "hT_dve", KT // 2)
            b = begin("ab", ("setup_ready", 2))
            wait(pe, "ld_ab", 16)
            for c in range(NT):
                for k in range(KT):
                    ins = pe.matmul(b[:, c * 2 * H:(c + 1) * 2 * H], hT[:, k, c * P:(c + 1) * P], wab[:, k, :],
                                    start=(k == 0), stop=(k == KT - 1))
            end(ins, "ab", "setup_mm")

            def proj(chunk, f, name, freed_by, fam):
                b = begin(name, freed_by)
                n = cidx[chunk]
                wait(pe, f"ld_w{n % 3}", 16 * (n // 3 + 1))
                for k in range(KT):
                    ins = pe.matmul(b[:], wring[n % 3][:, k, f * P:(f + 1) * P], hT[:, k, :], start=(k == 0),
                                    stop=(k == KT - 1))
                end(ins, name, fam)
                if f == NP - 1:
                    jobs[("w", n)] = (fam, S.count[fam])

            def tok_tr(src, p, name, freed_by, fam):
                b = begin(name, freed_by)
                for c in range(NT):
                    ins = pe.transpose(b[:, c * P:(c + 1) * P], src[:, p, c * P:(c + 1) * P], ident)
                end(ins, name, fam)

            for f in range(NP):
                proj("k", f, ("qkv", f), ("pad_ready", f + 1), "qkv_mm")
            b = begin("gcum", ("gcum_ready", 2))
            wait(pe, "g_ready", 1)
            wait(pe, "consts", 7)
            pe.matmul(b[:, 0:SC], triu, gt.rearrange("p a b -> p (a b)"), start=True, stop=True)
            ins = pe.matmul(b[:, SC:2 * SC], ones, gt.rearrange("p a b -> p (a b)"), start=True, stop=True)
            end(ins, "gcum", "setup_mm")
            for f in range(NP):
                proj("q", f, ("qkv", NP + f), ("pad_ready", NP + f + 1), "qkv_mm")
            for p in range(NP):
                wait(pe, "silu_ready", p + 1)
                tok_tr(kT, p, ("ktok", p), ("ktok_copied", p + 1), "tok_tr")
            for f in range(NP):
                proj("v", f, ("qkv", 2 * NP + f), ("pad_ready", 2 * NP + f + 1), "qkv_mm")
            for p in range(NP):
                wait(pe, "silu_ready", NP + p + 1)
                tok_tr(qT, p, ("qtok", p), ("sq_ready", NP + p + 1), "tok_tr")
            for f in range(CF):
                proj("cb", f, ("cb", f), ("glu_sig", f + 1), "glu_mm")
                proj("ca", f, ("ca", f), ("glu_ready", f + 1), "glu_mm")
            for p in range(NP):
                wait(pe, "silu_ready", 2 * NP + p + 1)
                tok_tr(vT, p, ("vtok", p), ("vtok_ready", p + 1), "vtok_tr")
            n = cidx["zg"]
            wait(pe, f"ld_w{n % 3}", 16 * (n // 3 + 1))
            for c in range(NT):
                b = begin(("zg", c), ("zg_silu", c + 1))
                for k in range(KT):
                    ins = pe.matmul(b[:], hT[:, k, c * P:(c + 1) * P], wring[n % 3][:, k, :], start=(k == 0),
                                    stop=(k == KT - 1))
                end(ins, ("zg", c), "zg_mm")
            jobs[("w", n)] = ("zg_mm", NT)

            def prep(h):
                t, r = h // 2, slice(DK * (h % 2), DK * (h % 2) + DK)
                b = begin(("G", h), ("diff_ready", NT * (h + 1)))
                wait(pe, "gb_ready", h + 1)
                for c in range(NT):
                    ins = pe.matmul(b[:, c * P:(c + 1) * P], gb[h % 2][:, c, :], triu, start=True, stop=True)
                end(ins, ("G", h), "G_mm")
                b = begin(("KK", h), ("M_ready", NT * (h + 1)))
                for c in range(NT):
                    kc = kT[r, t, c * P:(c + 1) * P]
                    ins = pe.matmul(b[:, c * P:(c + 1) * P], kc, kc, start=True, stop=True)
                end(ins, ("KK", h), "gram_mm")
                b = begin(("QK", h), ("qk_ready", NT * (h + 1)))
                for c in range(NT):
                    ins = pe.matmul(b[:, c * P:(c + 1) * P], kT[r, t, c * P:(c + 1) * P], qT[r, t, c * P:(c + 1) * P],
                                    start=True, stop=True)
                end(ins, ("QK", h), "gram_mm")

            for grp in range(H // GRP):
                hh = range(grp * GRP, (grp + 1) * GRP)
                for h in hh:
                    prep(h)
                for h in hh:
                    b = begin(("T0", h), ("T_init", h + 1))
                    wait(pe, "U0_ready", h + 1)
                    for c in range(NT):
                        ins = pe.transpose(b[:, c * P:(c + 1) * P], U[:, h, c, :], ident)
                    end(ins, ("T0", h), "gram_mm")
                for lv in range(1, LV):
                    for h in hh:
                        q = h % GRP
                        n_lv = (grp * (LV - 1) + lv - 1) * GRP + q
                        b = begin(("X", h, lv), ("X_ready", n_lv + 1))
                        wait(pe, "BT_ready", n_lv + 1)
                        if lv == 1:
                            wait(pe, "T_init", h + 1)
                        else:
                            wait(pe, "T_ready", (grp * (LV - 2) + lv - 2) * GRP + q + 1)
                        for c in range(NT):
                            ins = pe.matmul(b[:, c * P:(c + 1) * P], BT[:, q, c, :], Tm[:, q, c, :], start=True,
                                            stop=True)
                        end(ins, ("X", h, lv), "X_mm")
                    for h in hh:
                        q = h % GRP
                        n_lv = (grp * (LV - 1) + lv - 1) * GRP + q
                        n_t = (grp * (LV - 2) + lv - 1) * GRP + q
                        last = lv == LV - 1
                        fb = ("U_ready", h + 1) if last else ("T_ready", n_t + 1)
                        b = begin(("D", h, lv), fb)
                        wait(pe, "X_ready", n_lv + 1)
                        if lv > 1:
                            wait(pe, "U_tr_ready", (grp * (LV - 2) + lv - 2) * GRP + q + 1)
                        for c in range(NT):
                            if last:
                                ins = pe.matmul(b[:, c * P:(c + 1) * P], Xm[:, q, c, :], U[:, h, c, :], start=True,
                                                stop=True)
                            else:
                                ins = pe.matmul(b[:, c * P:(c + 1) * P], U[:, h, c, :], Xm[:, q, c, :], start=True,
                                                stop=True)
                        end(ins, ("D", h, lv), "D_mm")
                    if lv == LV - 1:
                        continue
                    for h in hh:
                        q = h % GRP
                        n_t = (grp * (LV - 2) + lv - 1) * GRP + q
                        b = begin(("TT", h, lv), ("U_tr_ready", n_t + 1))
                        wait(pe, "T_ready", n_t + 1)
                        for c in range(NT):
                            ins = pe.transpose(b[:, c * P:(c + 1) * P], Tm[:, q, c, :], ident)
                        end(ins, ("TT", h, lv), "gram_mm")

            gates = [(g, m) for g in range(2) for m in range(KT)]

            def gate():
                if not gates:
                    return
                g, m = gates.pop(0)
                proj(f"g{'cd'[g]}{m // NP}", m % NP, ("gate", g, m), ("gate_ready", g * KT + m + 1), "gate_mm")

            for c in range(NT):
                cs = slice(c * P, (c + 1) * P)
                if c > 0:
                    b = begin(("KS", c), ("st_ready", 2 * c - 1))
                    wait(pe, "S_ready", 2 * c)
                    for p in range(NP):
                        ins = pe.matmul(b[:, p * P:(p + 1) * P], kT[:, p, cs], Sst[:, p, :], start=True, stop=True)
                    end(ins, ("KS", c), "scan_mm")
                    gate()
                b = begin(("VN", c), ("vn_ready", c + 1))
                wait(pe, "U_ready", H)
                wait(pe, "vtok_ready", NP)
                wait(pe, "r_ready", c)
                for h in range(H):
                    rr = vtok[:, 0, :] if c == 0 else rbuf
                    ins = pe.matmul(b[:, h * DK:(h + 1) * DK], U[:, h, c, :], rr[:, h * DK:(h + 1) * DK], start=True,
                                    stop=True)
                end(ins, ("VN", c), "scan_mm")
                gate()
                if c > 0:
                    b = begin(("QS", c), ("st_ready", 2 * c))
                    for p in range(NP):
                        ins = pe.matmul(b[:, p * P:(p + 1) * P], qT[:, p, cs], Sst[:, p, :], start=True, stop=True)
                    end(ins, ("QS", c), "QS_mm")
                wait(pe, "vn_ready", c + 1)
                if c < NT - 1:
                    b = begin(("DS", c), ("S_ready", 2 * c + 2))
                    wait(pe, "kdec_ready", c + 1)
                    for p in range(NP):
                        ins = pe.matmul(b[:, p * P:(p + 1) * P], kdec[:, c, p * P:(p + 1) * P], vn[:, p * P:(p + 1) * P],
                                        start=True, stop=True)
                    end(ins, ("DS", c), "scan_mm")
                b = begin(("OV", c), ("ov_read", c + 1))
                wait(pe, "qk_ready", NT * H)
                for h in range(H):
                    ins = pe.matmul(b[:, h * DK:(h + 1) * DK], qkT[:, h, c, :], vn[:, h * DK:(h + 1) * DK], start=True,
                                    stop=True)
                end(ins, ("OV", c), "OV_mm")
                gate()
                if c > 0:
                    gate()
                b = begin(("oT", c), ("oT_ready", c + 1))
                wait(pe, "og_ready", c + 1)
                for p in range(NP):
                    ins = pe.transpose(b[:, p * P:(p + 1) * P], o_s[:, p * P:(p + 1) * P], ident)
                end(ins, ("oT", c), "oT_tr")
            b = begin("mean", ("xc_ready", CF))
            wait(pe, "dw_done", CF)
            for i in range(CF):
                ins = pe.matmul(b[:], mean_w, acc[:, i, :], start=(i == 0), stop=(i == CF - 1))
            end(ins, "mean", "scan_mm")
            while gates:
                gate()
            b = begin("var", ("sd_ready", 1))
            for i in range(CF):
                wait(pe, "lsq_ready", i + 1)
                ins = pe.matmul(b[:], mean_w, lsq[i % 2], start=(i == 0), stop=(i == CF - 1))
                tell(ins, "var_mm")
            jobs["var"][1:] = ["var_mm", CF]

            n = cidx["wco"]
            wait(pe, f"ld_w{n % 3}", 16 * (n // 3 + 1))
            wait(pe, "u_ready", CF)
            wco = at(R_RING + (n % 3) * WSLOT, CF, D)
            for m in range(KT):
                b = begin(("yc", m), ("yc_ready", m + 1))
                for f in range(CF):
                    ins = pe.matmul(b[:], wco[:, f, m * P:(m + 1) * P], acc[:, f, :], start=(f == 0), stop=(f == CF - 1))
                end(ins, ("yc", m), "yc_mm")
            jobs[("w", n)] = ("yc_mm", KT)
            n = cidx["wgo"]
            wait(pe, f"ld_w{n % 3}", 16 * (n // 3 + 1))
            wait(pe, "oT_ready", NT)
            wgo = at(R_RING + (n % 3) * WSLOT, NP, D)
            for m in range(KT):
                b = begin(("yd", m), ("yd_ready", m + 1))
                for f in range(NP):
                    ins = pe.matmul(b[:], wgo[:, f, m * P:(m + 1) * P], oT[:, f, :, :], start=(f == 0), stop=(f == NP - 1))
                end(ins, ("yd", m), "yd_mm")
            jobs[("w", n)] = ("yd_mm", KT)
            for c in range(NT):
                for hf in range(NH2):
                    n = cidx[f"wo{hf}"]
                    if c == 0:
                        wait(pe, f"ld_w{n % 3}", 16 * (n // 3 + 1))
                    b = begin(("wo", c, hf), ("x1_ready", c * NH2 + hf + 1))
                    for m in range(KT):
                        if hf == 0 and c == 0:
                            wait(pe, "y_ready", m + 1)
                        ins = pe.matmul(b[:], yT[:, m, c * P:(c + 1) * P], wring[n % 3][:, m, :], start=(m == 0),
                                        stop=(m == KT - 1))
                    end(ins, ("wo", c, hf), "wo_mm")

            for k in range(KT):
                b = begin(("h2T", k), ("h2T_ready", k + 1))
                for c in range(NT):
                    if k == 0:
                        wait(pe, "h2_ready", c + 1)
                    ins = pe.transpose(b[:, c * P:(c + 1) * P], h2[:, c, :].rearrange("p (q k) -> p k q", k=KT)[:, k, :],
                                       ident)
                end(ins, ("h2T", k), "route_mm")
            b = begin("logits", ("routed", 1))
            wait(pe, "ld_part2", 64)
            wait(pe, "h2T_ready", KT)
            for c in range(NT):
                for k in range(KT):
                    ins = pe.matmul(b[:, c * NR:(c + 1) * NR], h2T[:, k, c * P:(c + 1) * P], wr[:, k, :],
                                    start=(k == 0), stop=(k == KT - 1))
            end(ins, "logits", "route_mm")
            b = begin("rank", ("routed", 2))
            wait(pe, "M_onehot", 1)
            for c in range(NT):
                for cc in range(c + 1):
                    ins = pe.matmul(b[:, c * NE:(c + 1) * NE], triu_s if cc == c else ones, Mx[:, cc, :],
                                    start=(cc == 0), stop=(cc == c))
            end(ins, "rank", "route_mm")
            b = begin("flag", ("flag_ready", 1))
            wait(pe, "ovf_ready", 1)
            ins = pe.matmul(b[0:1, 0:1], ones[:, 0:1], ovf[:, 0:1], start=True, stop=True)
            end(ins, "flag", "route_mm")
            for b in range(8):
                wait(pe, *used[b])

            def ex_tr(e, g, j):
                wait(pe, f"ld_h{j}", 16 * (g + 1))
                wait(pe, "heT_a", e)
                wait(pe, "heT_d", e)
                for k in range(KT):
                    o = bank[k // 4][:, (k % 4) * CAP:(k % 4 + 1) * CAP]
                    ins = pe.transpose(o, hs[j][0:CAP, :].rearrange("p (q k) -> p k q", k=KT)[:, k, :],
                                       ident[0:CAP, 0:CAP])
                    if k % 4 == 3:
                        ins.then_inc(S["ex_tr"], 1)

            def ex_gu(e, g, j):
                wait(pe, f"ld_e{j}", 48 * (g + 1))
                wait(pe, "heT_a", e + 1)
                wait(pe, "heT_d", e + 1)
                wait(pe, "ex_sil", e - 1)
                wait(pe, "ex_hid", e - 1)
                for w, bk in ((wg, 2 + 2 * (j % 2)), (wu, 3 + 2 * (j % 2))):
                    for m in range(JE):
                        for k in range(KT):
                            ins = pe.matmul(bank[bk][:, m * CAP:(m + 1) * CAP], w[j][:, k, m * P:(m + 1) * P],
                                            heT[j % 2][:, k, :], start=(k == 0), stop=(k == KT - 1))
                    ins.then_inc(S["ex_g" if w is wg else "ex_u"], 1)

            def ex_dn(e, g, j):
                wait(pe, "ex_hid", e + 1)
                wait(pe, "ex_ya", e)
                wait(pe, "ex_yd", e)
                for hf in range(NH2):
                    for m in range(JE):
                        ins = pe.matmul(bank[6 + hf][0:CAP, :], hid[:, j % 2, m * CAP:(m + 1) * CAP],
                                        wd[j][:, m, hf * HALF:(hf + 1) * HALF], start=(m == 0), stop=(m == JE - 1))
                    ins.then_inc(S["ex_d0" if hf == 0 else "ex_d1"], 1)

            def trip(g, first=False, last=False):
                for j in range(UN):
                    e = g * UN + j
                    ex_gu(e, g, j)
                    if not (first and j == 0):
                        ex_dn(e - 1, g if j else g - 1, (j - 1) % UN)
                    if not (last and j == UN - 1):
                        ex_tr(e + 1, g if j < UN - 1 else g + 1, (j + 1) % UN)
                if last:
                    ex_dn(e, g, UN - 1)

            NTRIP = NE // UN
            ex_tr(0, 0, 0)
            trip(0, first=True)
            with pe.Fori(1, NTRIP - 1) as g:
                trip(g)
            trip(NTRIP - 1, last=True)

            wait(pe, "flag_ready", 1)
            wait(pe, "ex_ya", NE)
            wait(pe, "ex_yd", NE)
            fv = pe.value_load(flag_i[0:1, 0:1], min_val=0, max_val=2 * T)
            with pe.If(fv > 0):
                with pe.Fori(0, NE) as e:
                    wait(pe, "ov_ld", 48 * e + 48)
                    for m in range(JE):
                        pe.wait_ge(S["ov_hid"], e * JE + m + 1)
                        for w, bk in ((wg, 0), (wu, 1)):
                            for k in range(KT):
                                ins = pe.matmul(bank[bk][:], w[0][:, k, m * P:(m + 1) * P], h2T[:, k, :],
                                                start=(k == 0), stop=(k == KT - 1))
                            ins.then_inc(S["ov_gu"], 1)
                    for c in range(NT):
                        for hf in range(NH2):
                            if c == 0 and hf == 0:
                                pe.wait_ge(S["ov_hid"], e * JE + JE + 1)
                            pe.wait_ge(S["ov_acc"], e * 2 * NT + c * NH2 + hf + 1)
                            for m in range(JE):
                                ins = pe.matmul(bank[2][:], ohid[:, m, c * P:(c + 1) * P],
                                                wd[0][:, m, hf * HALF:(hf + 1) * HALF], start=(m == 0),
                                                stop=(m == JE - 1))
                            ins.then_inc(S["ov_d"], 1)

        def ready(eng, name):
            b, fam, n = jobs[name]
            wait(eng, fam, n)
            return bank[b]

        @block.sync
        def _(sp):
            xv = a["x"][0].rearrange("(c p) d -> c p d", p=P)
            for c in range(NT):
                sp.dma_start(xs[:, c, :], xv[c]).then_inc(S[f"ld_x{c}"], 16)
            sp.dma_start(g1, a["norm_mix_gain"][0].rearrange("(p k) -> p k", k=KT)).then_inc(S["ld_small"], 16)
            sp.dma_start(dwstage[0:TAPS, :], a["conv_dw_w"][0]).then_inc(S["ld_stage"], 16)
            for i, n in enumerate(("conv_dw_b", "conv_ln_gain", "conv_ln_bias")):
                sp.dma_start(dwstage[TAPS + i:TAPS + i + 1, :], a[n]).then_inc(S["ld_stage"], 16)
            sp.dma_start(gcstage[0:ST, :], a["gdn_conv_w"][0]).then_inc(S["ld_stage"], 16)
            sp.dma_start(wab, win[:, :, C_AB:C_AB + 2 * H]).then_inc(S["ld_ab"], 16)

            def load(n):
                src = chunks[n][1]
                dst = at(R_RING + (n % 3) * WSLOT, src.shape[1], src.shape[2])
                if n >= 3:
                    wait(sp, *jobs[("w", n - 3)])
                sp.dma_start(dst, src).then_inc(S[f"ld_w{n % 3}"], 16)

            load(0)
            sp.dma_start(alog, a["gdn_a_log"][0].partition_broadcast(P)).then_inc(S["ld_small"], 16)
            sp.dma_start(dtb, a["gdn_dt_bias"][0].partition_broadcast(P)).then_inc(S["ld_small"], 16)
            sp.dma_start(gng, a["gdn_norm_gain"][0].partition_broadcast(P)).then_inc(S["ld_small"], 16)
            for n in range(1, 12):
                load(n)
            wait(sp, "gate_mm", 2 * KT)
            for c in range(NT):
                sp.dma_start(x1[:, c, :], xv[c]).then_inc(S[f"ld_x{c}"], 16)
            wgd = a["w_expert_gate"][0].rearrange("(g j) (p k) n -> g j p k n", j=UN, k=KT)
            wud = a["w_expert_up"][0].rearrange("(g j) (p k) n -> g j p k n", j=UN, k=KT)
            wdd = a["w_expert_down"][0].rearrange("(g j) (m p) n -> g j p m n", j=UN, p=P)
            shv = sorted_h.rearrange("(g j s) n -> g j s n", j=UN, s=CAP)

            def expert(g, j):
                sp.dma_start(wg[j], wgd[g, j]).then_inc(S[f"ld_e{j}"], 16)
                sp.dma_start(wu[j], wud[g, j]).then_inc(S[f"ld_e{j}"], 16)
                sp.dma_start(wd[j], wdd[g, j]).then_inc(S[f"ld_e{j}"], 16)

            for n in (12, 13):
                load(n)
            wait(sp, "OV_mm", NT)
            wait(sp, "og_ready", NT)
            wait(sp, "S_ready", 2 * (NT - 1))
            for j in range(2):
                expert(0, j)
            wait(sp, *jobs[("w", cidx["wgo"])])
            sp.dma_start(gain2, a["norm_ffn_gain"][0].partition_broadcast(P)).then_inc(S["ld_part2"], 16)
            sp.dma_start(gain3, a["final_norm_gain"].partition_broadcast(P)).then_inc(S["ld_part2"], 16)
            sp.dma_start(wr[:, :, 0:NG], a["w_router_group"][0].rearrange("(p k) n -> p k n", k=KT)).then_inc(S["ld_part2"], 16)
            sp.dma_start(wr[:, :, NG:NR], a["w_router_expert"][0].rearrange("(p k) n -> p k n", k=KT)).then_inc(S["ld_part2"], 16)
            expert(0, 2)
            wait(sp, "wo_mm", 2 * NT)
            expert(0, 3)
            wait(sp, "scattered", 16 * 2 * NT)
            for j in range(UN):
                sp.dma_start(hs[j][0:CAP, :], shv[0, j]).then_inc(S[f"ld_h{j}"], 16)
            with sp.Fori(1, NE // UN) as g:
                for j in range(UN):
                    e = g * UN + j
                    sp.wait_ge(S["ex_tr"], 2 * (e - UN) + 2)
                    sp.dma_start(hs[j][0:CAP, :], shv[g, j]).then_inc(S[f"ld_h{j}"], 16)
                    sp.wait_ge(S["ex_d1"], e - UN + 1)
                    expert(g, j)

            wait(sp, "flag_ready", 1)
            fv = sp.value_load(flag_i[0:1, 0:1], min_val=0, max_val=2 * T)
            with sp.If(fv > 0):
                wait(sp, "ex_d1", NE)
                with sp.Fori(0, NE) as e:
                    sp.wait_ge(S["ov_shift"], 2 * e + 1)
                    sp.dma_start(wg[0], a["w_expert_gate"][0].rearrange("e (p k) n -> e p k n", k=KT)[e]).then_inc(S["ov_ld"], 16)
                    sp.dma_start(wu[0], a["w_expert_up"][0].rearrange("e (p k) n -> e p k n", k=KT)[e]).then_inc(S["ov_ld"], 16)
                    sp.dma_start(wd[0], a["w_expert_down"][0].rearrange("e (m p) n -> e p m n", p=P)[e]).then_inc(S["ov_ld"], 16)
            ov = out[0].rearrange("(c p) d -> c p d", p=P)
            for c in range(NT):
                wait(sp, "out_ready", c + 1)
                sp.dma_start(ov[c], x1[:, c, :]).then_inc(S["st_out"], 16)
            wait(sp, "st_out", 16 * NT)

        @block.gpsimd
        def _(gp):
            n_chain = [0]

            def link(ins):
                n_chain[0] += 1
                ins.then_inc(S["pool_chain"], 1)
                gp.wait_ge(S["pool_chain"], n_chain[0])

            link(gp.memset(ones, 1.0))
            gp.memset(mean_w, 1.0 / CW).then_inc(S["consts"], 1)

            def sel(dst, src, pattern, base, cm, op=ALU.is_ge, fill=0.0):
                return gp.affine_select(out=dst, in_=src, compare_op=op, fill=fill, base=base, pattern=pattern,
                                        channel_multiplier=cm)

            sel(ident, ones, [[1, P]], 0, -1, ALU.is_equal).then_inc(S["consts"], 1)
            sel(triu, ones, [[1, P]], 0, -1).then_inc(S["consts"], 1)
            sel(triu_s, ones, [[1, P]], -1, -1).then_inc(S["consts"], 1)
            link(gp.memset(negm, 0.0))
            sel(negm, negm, [[1, P]], 0, -1, fill=NEG).then_inc(S["consts"], 1)
            for lv in range(LV):
                s = 2 ** lv
                if 2 * s == P:
                    link(gp.tensor_copy(lmask[:, lv, :], ones))
                    continue
                s2 = 2 * s
                v = lmask[:, lv, :].rearrange("p (b s) -> p b s", s=s2)
                link(sel(v, ones.rearrange("p (b s) -> p b s", s=s2), [[-s2, P // s2], [0, s2]], 0, 1))
                link(sel(v, v, [[s2, P // s2], [0, s2]], s2 - 1, -1))
            gp.wait_ge(S["consts"], 5)
            for lv in range(LV - 1, 0, -1):
                link(gp.tensor_tensor(lmask[:, lv, :], lmask[:, lv, :], lmask[:, lv - 1, :], ALU.subtract))
            link(gp.tensor_tensor(lmask[:, 0, :], lmask[:, 0, :], ident, ALU.subtract))
            for lv in range(LV):
                link(gp.tensor_tensor(lmask[:, lv, :], lmask[:, lv, :], triu_s, ALU.mult))
            gp.memset(Sst, 0.0).then_inc(S["consts"], 1)
            for i in range(3):
                link(gp.memset(pad[i][:, 0:ST - 1], 0.0))
            gp.memset(zero, 0.0).then_inc(S["consts"], 1)
            gp.wait_ge(S["consts"], 7)
            for i in range(CF):
                gp.memset(upad[:, i, 0:TAPS - 1], 0.0).then_inc(S["upad_zero"], 1)
            gp.wait_ge(S["g_ready"], 1)
            for i in range(NE * CAP // P):
                gp.dma_start(sorted_h[i * P:(i + 1) * P, :], zero).then_inc(S["zeroed"], 16)
            gp.wait_ge(S["g_ready"], 1)

            def gbc(h):
                if h >= 2:
                    wait(gp, "G_mm", h - 1)
                gp.tensor_copy(gb[h % 2], bc(gt[:, :, h:h + 1], [P, NT, P])).then_inc(S["gb_ready"], 1)

            wait(gp, "ktok_copied", NP)
            wait(gp, "kds_ready", 1)
            for c in range(NT):
                gp.tensor_tensor(heads(kdec[:, c, :]), heads(kdec[:, c, :]), per_head(kds, c), ALU.mult)\
                    .then_inc(S["kdec_ready"], 1)
            gp.wait_ge(S["ss_done"], 2 * NP)
            gp.wait_ge(S["glu_ready"], CF)
            gbc(0)
            gbc(1)
            gp.wait_ge(S["ld_small"], 64)
            for c in range(NT):
                wait(gp, "zg_silu", c + 1)
                gp.tensor_tensor(heads(zgs[:, c, :]), heads(zgs[:, c, :]),
                                 bc(gng.unsqueeze(1), [P, H, DK]), ALU.mult).then_inc(S["zg_ready"], 1)

            def masked(h, lv, q, buf):
                return gp.tensor_tensor(buf, MT[:, q, :, :], bc(lmask[:, lv, :].unsqueeze(1), [P, NT, P]), ALU.mult)

            for grp in range(H // GRP):
                for q in range(GRP):
                    h = grp * GRP + q
                    if h + 2 < H:
                        gbc(h + 2)
                    wait(gp, "M_ready", NT * (h + 1))
                    if grp > 0:
                        wait(gp, "X_mm", grp * (LV - 1) * GRP)
                    link(masked(h, 0, q, U[:, h, :, :]))
                    gp.tensor_tensor(U[:, h, :, :], bc(ident.unsqueeze(1), [P, NT, P]), U[:, h, :, :],
                                     ALU.subtract).then_inc(S["U0_ready"], 1)
                for lv in range(1, LV):
                    for q in range(GRP):
                        h = grp * GRP + q
                        wait(gp, "X_mm", (grp * (LV - 1) + lv - 2) * GRP + q + 1 if lv > 1 else grp * (LV - 1) * GRP)
                        masked(h, lv, q, BT[:, q, :, :]).then_inc(S["BT_ready"], 1)

            gp.wait_ge(S["u_ready"], CF)
            gp.wait_ge(S["og_ready"], NT)
            gp.wait_ge(S["oT_tr"], NT)
            gp.dma_start(rbias[:, 0:NG], a["b_router_group"][0].partition_broadcast(P)).then_inc(S["ld_rbias"], 16)
            gp.dma_start(rbias[:, NG:NR], a["b_router_expert"][0].partition_broadcast(P)).then_inc(S["ld_rbias"], 16)
            gp.iota(desc, [[0, NT], [-1, NE]], NE, 0, allow_small_or_imprecise_dtypes=True).then_inc(S["rconst"], 1)
            gp.iota(descg, [[0, NT], [-1, NG]], NG, 0, allow_small_or_imprecise_dtypes=True).then_inc(S["rconst"], 1)
            gp.iota(iota_c, [[0, NT], [CAP, NE]], 0, 0, allow_small_or_imprecise_dtypes=True).then_inc(S["rconst"], 1)
            gp.wait_ge(S["idx_ready"], 1)
            gp.wait_ge(S["zeroed"], 16 * (NE * CAP // P))
            for c in range(NT):
                for r in range(2):
                    gp.indirect_dma_start(out=sorted_h, out_offset=bass.IndirectOffsetOnAxis(ap=slot_idx[:, c, r, 0:1], axis=0),
                                          in_=h2[:, c, :], in_offset=None, bounds_check=NE * CAP - 1,
                                          oob_is_err=False).then_inc(S["scattered"], 16)
            syv = sorted_y.rearrange("(g j s) n -> g j s n", j=UN, s=CAP)
            with gp.Fori(0, NE // UN) as g:
                for j in range(UN):
                    e = g * UN + j
                    gp.wait_ge(S["ex_ya"], e + 1)
                    gp.wait_ge(S["ex_yd"], e + 1)
                    gp.dma_start(syv[g, j], ysb[j % 2][0:CAP, :]).then_inc(S[f"st_y{j % 2}"], 16)
            gp.wait_ge(S["st_y0"], 16 * NE // 2)
            gp.wait_ge(S["st_y1"], 16 * NE // 2)
            wait(gp, "ex_d1", NE)
            wait(gp, "ov_over", 1)
            for c in range(NT):
                for r in range(2):
                    gp.indirect_dma_start(out=gath[2 * c + r], out_offset=None, in_=sorted_y,
                                          in_offset=bass.IndirectOffsetOnAxis(ap=slot_idx[:, c, r, 1:2], axis=0),
                                          bounds_check=NE * CAP - 1, oob_is_err=False).then_inc(S[f"ld_y{c}"], 16)

        @block.scalar
        def _(act):
            def copy(dst, src, fam, **kw):
                return tell(act.activation(dst, src, ACT.Copy, **kw), fam)

            for c in range(NT):
                act.wait_ge(S[f"ld_x{c}"], 16)
                act.activation(at(R_QK + c * D, D), xs[:, c, :], ACT.Square,
                               accum_out=sm["ss1"][:, c:c + 1]).then_inc(S["ss"], 1)
            act.wait_ge(S["ss"], NT)
            act.wait_ge(S["eps_ready"], 1)
            act.activation(sm["ss1"], sm["ss1"], ACT.Sqrt, scale=1.0 / D, bias=epsb).then_inc(S["norms"], 1)
            act.wait_ge(S["ld_small"], 64)
            for k in range(0, KT, 2):
                tell(act.activation(hT[:, k, :], ready(act, ("hT", k))[:], ACT.Copy, scale=g1[:, k:k + 1]), "hT_act")

            act.wait_ge(S["ld_small"], 64)
            act.activation(alog, alog, ACT.Exp).then_inc(S["sp"], 1)
            act.wait_ge(S["y_sp"], 1)
            act.activation(sp_a, y_sp, ACT.Abs).then_inc(S["sp"], 1)
            act.wait_ge(S["sp"], 2)
            act.activation(sp_a, sp_a, ACT.Exp, scale=-1.0).then_inc(S["sp"], 1)
            act.wait_ge(S["sp"], 3)
            act.activation(sp_a, sp_a, ACT.Ln, bias=1.0).then_inc(S["sp"], 1)
            act.activation(beta, absb[:, :, 0:H], ACT.Sigmoid).then_inc(S["beta_ready"], 1)

            def pad_copy(f):
                src = ready(act, ("qkv", f))
                if f >= 3:
                    act.wait_ge(S["tap_done"], f - 2)
                tell(act.activation(pad[f % 3][:, ST - 1:], src[:], ACT.Copy), "pad_ready")

            def silu_out(f):
                dst = (kT, qT, vT)[f // NP][:, f % NP, :]
                act.wait_ge(S["tap_done"], f + 1)
                tell(act.activation(dst, cacc[f % 3], ACT.Silu), "silu_ready")

            def squares(name, n):
                src = ready(act, name)
                if n >= 2:
                    act.wait_ge(S["ss_done"], n - 1)
                tell(act.activation(sq[n % 2], src.rearrange("p (c h d) -> p c h d", c=NT, h=2), ACT.Square), "sq_ready")
                return src

            for f in range(NP + 1):
                if f < NP + 1:
                    pad_copy(f)
                if f > 0:
                    silu_out(f - 1)
            act.wait_ge(S["gcum_ready"], 2)
            act.wait_ge(S["gdiff"], 1)
            act.activation(eg, gcum, ACT.Exp).then_inc(S["exps"], 1)
            act.activation(kds, kds, ACT.Exp).then_inc(S["exps"], 1)
            act.activation(egl, glast, ACT.Exp).then_inc(S["exps"], 1)
            for f in range(NP + 1, 2 * NP):
                pad_copy(f)
                silu_out(f - 1)
            for p in range(NP):
                src = squares(("ktok", p), p)
                tell(act.activation(kdec[:, :, p * P:(p + 1) * P], src.rearrange("p (c n) -> p c n", c=NT), ACT.Copy),
                     "ktok_copied")
            act.wait_ge(S["ss_done"], NP)
            act.activation(nk, ssk, ACT.Sqrt, bias=epsb).then_inc(S["norms"], 1)
            for f in range(2 * NP, 3 * NP):
                pad_copy(f)
                silu_out(f - 1)
            silu_out(3 * NP - 1)
            for p in range(NP):
                squares(("qtok", p), NP + p)
            act.wait_ge(S["ss_done"], 2 * NP)
            act.activation(nq, ssq, ACT.Sqrt, scale=float(DK), bias=epsb64).then_inc(S["norms"], 1)
            for i in range(CF):
                src = ready(act, ("cb", i))
                if i >= 2:
                    act.wait_ge(S["glu_ready"], i - 1)
                tell(act.activation(sgl[i % 2], src[:], ACT.Sigmoid), "glu_sig")
            act.wait_ge(S["zeroed"], 16 * (NE * CAP // P))
            for c in range(NT):
                tell(act.activation(zgs[:, c, :], ready(act, ("zg", c))[:], ACT.Silu), "zg_silu")

            for grp in range(H // GRP):
                hh = range(grp * GRP, (grp + 1) * GRP)
                for h in hh:
                    act.wait_ge(S["diff_ready"], NT * (h + 1))
                    act.activation(dec[h % 2], dec[h % 2], ACT.Exp).then_inc(S["dec_ready"], 1)
                for h in hh:
                    tell(act.activation(Tm[:, h % GRP, :, :], ready(act, ("T0", h)).rearrange("p (c n) -> p c n", c=NT),
                                        ACT.Copy), "T_init")
                for lv in range(1, LV):
                    for h in hh:
                        tell(act.activation(Xm[:, h % GRP, :, :],
                                            ready(act, ("X", h, lv)).rearrange("p (c n) -> p c n", c=NT), ACT.Copy),
                             "X_ready")
                    if lv < LV - 1:
                        for h in hh:
                            tell(act.activation(U[:, h, :, :],
                                                ready(act, ("TT", h, lv)).rearrange("p (c n) -> p c n", c=NT), ACT.Copy),
                                 "U_tr_ready")

            act.wait_ge(S["U_ready"], H)
            act.wait_ge(S["D_mm"], H * (LV - 1))
            gates = [(g, m) for g in range(2) for m in range(KT)]

            def gate(upto):
                while gates and len(gates) > 2 * KT - upto:
                    g, m = gates.pop(0)
                    tell(act.activation(sig[g][:, m, :], ready(act, ("gate", g, m))[:], ACT.Sigmoid), "gate_ready")

            done = [0]

            def more(n):
                done[0] += n
                gate(done[0])

            for c in range(NT):
                if c > 0:
                    more(1)
                more(2)
                if c > 0:
                    more(1)
                act.wait_ge(S["o_ready"], c + 1)
                act.activation(rbuf, o_t, ACT.Square).then_inc(S["osq"], 1)
                act.wait_ge(S["oss"], c + 1)
                act.activation(ors[:, c, :], oss[:, c, :], ACT.Sqrt, scale=1.0 / DK, bias=epsb).then_inc(S["ors"], 1)
                src = ready(act, ("oT", c))
                tell(act.activation(oTc[c], src.rearrange("p (f n) -> p f n", f=NP), ACT.Copy),
                     "oT_ready")
            more(2 * KT)

            for i in range(CF):
                act.wait_ge(S["xc_ready"], i + 1)
                if i >= 2:
                    act.wait_ge(S["var_mm"], i - 1)
                act.activation(lsq[i % 2], acc[:, i, :], ACT.Square).then_inc(S["lsq_ready"], 1)
            tell(act.activation(lnv, ready(act, "var")[:], ACT.Sqrt, bias=epsb), "sd_ready")
            for i in range(CF):
                act.wait_ge(S["xn_ready"], i + 1)
                o = i * (TAPS + 3)
                act.activation(acc[:, i, :], acc[:, i, :], ACT.Silu, scale=par[:, o + TAPS + 1:o + TAPS + 2],
                               bias=par[:, o + TAPS + 2:o + TAPS + 3]).then_inc(S["u_ready"], 1)
            junk = at(R_ACC, D)
            act.wait_ge(S["yc_mm"], KT)
            for c in range(NT):
                act.wait_ge(S["x1_ready"], NH2 * (c + 1))
                if c > 0:
                    act.wait_ge(S["ss"], NT + c)
                act.activation(junk, x1[:, c, :], ACT.Square, accum_out=sm["ss2"][:, c:c + 1]).then_inc(S["ss"], 1)
            act.wait_ge(S["ss"], 2 * NT)
            act.activation(sm["ss2"], sm["ss2"], ACT.Sqrt, scale=1.0 / D, bias=epsb).then_inc(S["norms"], 1)
            act.wait_ge(S["yd_ready"], KT)
            for k in range(KT):
                tell(act.activation(h2T[:, k, :], ready(act, ("h2T", k))[:], ACT.Copy), "h2T_ready")
            act.wait_ge(S["route_dif"], 1)
            act.activation(dg, dg, ACT.Exp).then_inc(S["route_exp"], 1)
            act.wait_ge(S["route_dif"], 2)
            act.activation(sm["tt"], sm["tt"], ACT.Exp).then_inc(S["route_exp"], 1)

            def ex_act(e, g, j):
                wait(act, "ex_tr", 2 * e + 1)
                wait(act, "ex_u", e - 1)
                act.activation(heT[j % 2][:, 0:KT // 2, :], bank[0][:, 0:4 * CAP].rearrange("p (k n) -> p k n", k=4),
                               ACT.Copy).then_inc(S["heT_a"], 1)

            def ex_silu(e, g, j):
                wait(act, "ex_g", e + 1)
                wait(act, "ex_hid", e - 1)
                act.activation(sil[:, j % 2, :], bank[2 + 2 * (j % 2)][:, 0:JE * CAP], ACT.Silu).then_inc(S["ex_sil"], 1)

            def ex_y(e, g, j):
                wait(act, "ex_d0", e + 1)
                wait(act, f"st_y{j % 2}", 32 * g + 16 * (j // 2))
                act.activation(ysb[j % 2][0:CAP, 0:HALF], bank[6][0:CAP, :], ACT.Copy).then_inc(S["ex_ya"], 1)

            def trip(g, first=False, last=False):
                for j in range(UN):
                    e = g * UN + j
                    ex_silu(e, g, j)
                    if not (first and j == 0):
                        ex_y(e - 1, g if j else g - 1, (j - 1) % UN)
                    if not (last and j == UN - 1):
                        ex_act(e + 1, g if j < UN - 1 else g + 1, (j + 1) % UN)
                if last:
                    ex_y(e, g, UN - 1)

            act.wait_ge(S["idx_ready"], 1)
            ex_act(0, 0, 0)
            trip(0, first=True)
            with act.Fori(1, NE // UN - 1) as g:
                trip(g)
            trip(NE // UN - 1, last=True)

            act.wait_ge(S["flag_ready"], 1)
            fv = act.value_load(flag_i[0:1, 0:1], min_val=0, max_val=2 * T)
            with act.If(fv > 0):
                with act.Fori(0, NE) as e:
                    for m in range(JE):
                        act.wait_ge(S["ov_gu"], 2 * (e * JE + m) + 1)
                        act.wait_ge(S["ov_hid"], e * JE + m + 1)
                        act.activation(osil, bank[0][:], ACT.Silu).then_inc(S["ov_sil"], 1)
            for c in range(NT):
                act.wait_ge(S["x2_ready"], c + 1)
                if c > 0:
                    act.wait_ge(S["ss"], 2 * NT + c)
                act.activation(at(R_UP, D), x1[:, c, :], ACT.Square, accum_out=sm["ss3"][:, c:c + 1]).then_inc(S["ss"], 1)
                act.wait_ge(S["ss"], 2 * NT + c + 1)
                act.activation(sm["r3"][:, c:c + 1], sm["ss3"][:, c:c + 1], ACT.Sqrt, scale=1.0 / D,
                               bias=epsb).then_inc(S["rms3"], 1)

        @block.vector
        def _(v):
            n_chain = [0]

            def link(ins):
                n_chain[0] += 1
                ins.then_inc(S["dve_chain"], 1)
                v.wait_ge(S["dve_chain"], n_chain[0])

            TT, TS, STT = v.tensor_tensor, v.tensor_scalar, v.scalar_tensor_tensor
            link(v.memset(epsb, EPS))
            v.memset(epsb64, EPS * DK).then_inc(S["eps_ready"], 1)
            v.wait_ge(S["norms"], 1)
            link(v.reciprocal(sm["r1"], sm["ss1"]))
            for c in range(NT):
                TS(xs[:, c, :], xs[:, c, :], sm["r1"][:, c:c + 1], None, ALU.mult).then_inc(S["xs_ready"], 1)
            v.wait_ge(S["ld_small"], 64)
            for k in range(1, KT, 2):
                tell(TS(hT[:, k, :], ready(v, ("hT", k))[:], g1[:, k:k + 1], None, ALU.mult), "hT_dve")
            NS = TAPS + 3
            tell(v.tensor_copy(par, ready(v, "par")[:, 0:par.shape[1]]), "setup_ready")
            tell(v.tensor_copy(absb.rearrange("p a b -> p (a b)"), ready(v, "ab")[:, 0:NT * 2 * H]), "setup_ready")
            v.wait_ge(S["setup_ready"], 2)
            v.wait_ge(S["ld_small"], 64)
            tell(TT(y_sp, absb[:, :, H:2 * H], bc(dtb.unsqueeze(1), [P, NT, H]), ALU.add), "y_sp")
            v.wait_ge(S["y_sp"], 1)
            link(TS(sp_b, y_sp, 0.0, None, ALU.max))
            v.wait_ge(S["sp"], 4)
            link(TT(sp_b, sp_b, sp_a, ALU.add))
            v.wait_ge(S["sp"], 1)
            link(TS(sp_b, sp_b, -1.0, None, ALU.mult))
            TT(gt, sp_b, bc(alog.unsqueeze(1), [P, NT, H]), ALU.mult).then_inc(S["g_ready"], 1)

            def conv(f):
                ff = (NP, 0, 2 * NP)[f // NP] + f % NP
                w0 = CF * NS + ff * ST
                v.wait_ge(S["pad_ready"], f + 1)
                if f >= 3:
                    v.wait_ge(S["silu_ready"], f - 2)
                link(TS(cacc[f % 3], pad[f % 3][:, 0:T], par[:, w0:w0 + 1], None, ALU.mult))
                for t in range(1, ST):
                    ins = STT(out=cacc[f % 3], in0=pad[f % 3][:, t:t + T], scalar=par[:, w0 + t:w0 + t + 1],
                              in1=cacc[f % 3], op0=ALU.mult, op1=ALU.add)
                    if t < ST - 1:
                        link(ins)
                    else:
                        tell(ins, "tap_done")

            def sumsq(n, dst, p):
                v.wait_ge(S["sq_ready"], n + 1)
                tell(v.tensor_reduce(dst[:, :, 2 * p:2 * p + 2], sq[n % 2], AX.X, ALU.add), "ss_done")

            v.wait_ge(S["consts"], 7)
            for f in range(NP):
                conv(f)
            b = ready(v, "gcum")
            tell(v.tensor_copy(gcum.rearrange("p a b -> p (a b)"), b[:, 0:SC]), "gcum_ready")
            tell(v.tensor_copy(glast.rearrange("p a b -> p (a b)"), b[:, SC:2 * SC]), "gcum_ready")
            v.wait_ge(S["gcum_ready"], 2)
            tell(TT(kds, glast, gcum, ALU.subtract), "gdiff")
            for f in range(NP, 2 * NP):
                conv(f)
            for p in range(NP):
                sumsq(p, ssk, p)
            v.wait_ge(S["norms"], 2)
            v.wait_ge(S["exps"], 3)
            v.wait_ge(S["beta_ready"], 1)
            link(v.reciprocal(rk, nk))
            link(TT(brk, beta, rk, ALU.mult))
            TT(brk2, brk, rk, ALU.mult).then_inc(S["brk2"], 1)
            tell(TT(kds, kds, rk, ALU.mult), "kds_ready")
            for r in range(2):
                rs = slice(DK * r, DK * r + DK)
                link(v.tensor_copy(gls[rs, :, :], egl[rs, :, :].rearrange("p c (a r) -> p c r a", r=2)[:, :, r, :]))
            for f in range(2 * NP, 3 * NP):
                conv(f)
            for p in range(NP):
                sumsq(NP + p, ssq, p)
            v.wait_ge(S["norms"], 3)
            link(v.reciprocal(rq, nq))
            v.wait_ge(S["upad_zero"], CF)
            for i in range(CF):
                src = ready(v, ("ca", i))
                v.wait_ge(S["glu_sig"], i + 1)
                tell(TT(upad[:, i, TAPS - 1:], src[:], sgl[i % 2], ALU.mult), "glu_ready")
            for p in range(NP):
                src = ready(v, ("vtok", p))
                tell(TT(vtok[:, :, p * P:(p + 1) * P].rearrange("p c (h d) -> p c h d", h=2),
                        src.rearrange("p (c h d) -> p c h d", c=NT, h=2),
                        bc(nk[:, :, 2 * p:2 * p + 2].unsqueeze(3), [P, NT, 2, DK]), ALU.mult), "vtok_ready")

            taps = [(t, i) for t in range(TAPS) for i in range(CF)]
            n_tap = [0]

            def dw(n):
                for _ in range(n):
                    if not taps:
                        return
                    t, i = taps.pop(0)
                    o = i * NS
                    if t == 0:
                        ins = TS(acc[:, i, :], upad[:, i, 0:T], par[:, o:o + 1], par[:, o + TAPS:o + TAPS + 1], ALU.mult,
                                 ALU.add)
                    else:
                        v.wait_ge(S["dw_step"], n_tap[0] - CF + 1 if t < TAPS - 1 else n_tap[0])
                        ins = STT(out=acc[:, i, :], in0=upad[:, i, t:t + T], scalar=par[:, o + t:o + t + 1],
                                  in1=acc[:, i, :], op0=ALU.mult, op1=ALU.add)
                    if t == TAPS - 1:
                        ins.then_inc(S["dw_done"], 1)
                    else:
                        ins.then_inc(S["dw_step"], 1)
                        n_tap[0] += 1

            for grp in range(H // GRP):
                hh = range(grp * GRP, (grp + 1) * GRP)
                for h in hh:
                    g = ready(v, ("G", h))
                    if h >= 2:
                        v.wait_ge(S["M_ready"], NT * (h - 1))
                        v.wait_ge(S["qk_ready"], NT * (h - 1))
                    for c in range(NT):
                        tell(STT(out=dec[h % 2][:, c, :], in0=g[:, c * P:(c + 1) * P], scalar=gcum[:, c, h:h + 1], in1=negm,
                                 op0=ALU.subtract, op1=ALU.add), "diff_ready")
                    kk = ready(v, ("KK", h))
                    v.wait_ge(S["dec_ready"], h + 1)
                    v.wait_ge(S["brk2"], 1)
                    if grp > 0 and h % GRP == 0:
                        v.wait_ge(S["BT_ready"], (LV - 1) * GRP * grp)
                    if grp == 0 and h == 0:
                        v.wait_ge(S["vtok_tr"], NP)
                    for c in range(NT):
                        tell(STT(out=MT[:, h % GRP, c, :], in0=kk[:, c * P:(c + 1) * P], scalar=brk2[:, c, h:h + 1],
                                 in1=dec[h % 2][:, c, :], op0=ALU.mult, op1=ALU.mult), "M_ready")
                    qk = ready(v, ("QK", h))
                    for c in range(NT):
                        tell(STT(out=qkT[:, h, c, :], in0=qk[:, c * P:(c + 1) * P], scalar=rk[:, c, h:h + 1],
                                 in1=dec[h % 2][:, c, :], op0=ALU.mult, op1=ALU.mult), "qk_ready")
                for lv in range(1, LV):
                    for h in hh:
                        src = ready(v, ("D", h, lv)).rearrange("p (c n) -> p c n", c=NT)
                        if lv < LV - 1:
                            tell(TT(Tm[:, h % GRP, :, :], Tm[:, h % GRP, :, :], src, ALU.subtract), "T_ready")
                        else:
                            tell(TT(U[:, h, :, :], U[:, h, :, :], src, ALU.subtract), "U_ready")
                    dw(11)

            for c in range(NT):
                if c > 0:
                    src = ready(v, ("KS", c))
                    v.wait_ge(S["osq"], c)
                    v.wait_ge(S["oss"], c)
                    tell(TT(heads(rbuf), heads(src), per_head(eg, c), ALU.mult), "st_ready")
                    v.wait_ge(S["st_ready"], 2 * c - 1)
                    TT(rbuf, vtok[:, c, :], rbuf, ALU.subtract).then_inc(S["r_ready"], 1)
                src = ready(v, ("VN", c))
                if c > 0:
                    v.wait_ge(S["OV_mm"], c)
                tell(TT(heads(vn), heads(src), per_head(brk, c), ALU.mult), "vn_ready")
                if c > 0:
                    src = ready(v, ("QS", c))
                    tell(TT(heads(o_t), heads(src), per_head(eg, c), ALU.mult), "st_ready")
                if c < NT - 1:
                    src = ready(v, ("DS", c)).rearrange("p (a n) -> p a n", a=NP)
                    if c > 0:
                        v.wait_ge(S["QS_mm"], c)
                    for r in range(2):
                        rs = slice(DK * r, DK * r + DK)
                        dst = Sst[rs, :, DK * r:DK * r + DK]
                        if c > 0:
                            link(TT(dst, dst, bc(gls[rs, c, :].unsqueeze(2), [DK, NP, DK]), ALU.mult))
                            tell(TT(dst, dst, src[rs, :, DK * r:DK * r + DK], ALU.add), "S_ready")
                        else:
                            v.wait_ge(S["consts"], 7)
                            tell(v.tensor_copy(dst, src[rs, :, DK * r:DK * r + DK]), "S_ready")
                src = ready(v, ("OV", c))
                if c > 0:
                    v.wait_ge(S["st_ready"], 2 * c)
                    tell(TT(o_t, o_t, src[:], ALU.add), "ov_read")
                    v.wait_ge(S["ov_read"], c + 1)
                    ins = TT(heads(o_t), heads(o_t), per_head(rq, c), ALU.mult)
                    ins.then_inc(S["o_ready"], 1)
                else:
                    ins = TT(heads(o_t), heads(src), per_head(rq, c), ALU.mult)
                    tell(ins, "ov_read")
                    v.wait_ge(S["ov_read"], 1)
                    v.engine_nop().then_inc(S["o_ready"], 1)
                v.wait_ge(S["osq"], c + 1)
                v.tensor_reduce(oss[:, c, :], heads(rbuf), AX.X, ALU.add).then_inc(S["oss"], 1)
                v.wait_ge(S["ors"], c + 1)
                link(v.reciprocal(ors[:, c, :], ors[:, c, :]))
                v.wait_ge(S["zg_ready"], c + 1)
                v.wait_ge(S["o_ready"], c + 1)
                if c > 0:
                    v.wait_ge(S["oT_tr"], c)
                link(TT(heads(o_s), heads(o_t), per_head(ors, c), ALU.mult))
                TT(o_s, o_s, zgs[:, c, :], ALU.mult).then_inc(S["og_ready"], 1)

            m = ready(v, "mean")
            for i in range(CF):
                tell(TT(acc[:, i, :], acc[:, i, :], m[:], ALU.subtract), "xc_ready")
            for g in (0,):
                v.wait_ge(S["sd_ready"], 1)
                link(v.reciprocal(lnm, lnv))
                v.wait_ge(S["lsq_ready"], CF)
                for i in range(CF):
                    TT(acc[:, i, :], acc[:, i, :], lnm, ALU.mult).then_inc(S["xn_ready"], 1)
            v.wait_ge(S["gate_ready"], 2 * KT)
            for m_ in range(KT):
                src = ready(v, ("yc", m_))
                tell(TT(yT[:, m_, :], yT[:, m_, :], src[:], ALU.mult), "yc_ready")
            for m_ in range(KT):
                src = ready(v, ("yd", m_))
                tell(TT(sig[1][:, m_, :], sig[1][:, m_, :], src[:], ALU.mult), "yd_ready")
                v.wait_ge(S["yc_ready"], m_ + 1)
                v.wait_ge(S["yd_ready"], m_ + 1)
                TT(yT[:, m_, :], yT[:, m_, :], sig[1][:, m_, :], ALU.add).then_inc(S["y_ready"], 1)
            for c in range(NT):
                v.wait_ge(S[f"ld_x{c}"], 32)
                for hf in range(NH2):
                    src = ready(v, ("wo", c, hf))
                    xx = x1[:, c, hf * HALF:(hf + 1) * HALF]
                    tell(TT(xx, xx, src[:], ALU.add), "x1_ready")
            v.wait_ge(S["norms"], 4)
            link(v.reciprocal(sm["r2"], sm["ss2"]))
            v.wait_ge(S["ld_part2"], 64)
            v.wait_ge(S["x1_ready"], NT * NH2)
            v.wait_ge(S["yc_mm"], KT)
            for c in range(NT):
                STT(out=h2[:, c, :], in0=x1[:, c, :], scalar=sm["r2"][:, c:c + 1], in1=gain2, op0=ALU.mult,
                    op1=ALU.mult).then_inc(S["h2_ready"], 1)

            v.wait_ge(S["ld_rbias"], 32)
            v.wait_ge(S["rconst"], 3)
            src = ready(v, "logits")
            tell(TT(lg, src[:, 0:NT * NR].rearrange("p (c n) -> p c n", c=NT), bc(rbias.unsqueeze(1), [P, NT, NR]),
                    ALU.add), "routed")
            v.wait_ge(S["routed"], 1)

            def col(s, n):
                return bc(sm[s].unsqueeze(2), [P, NT, n])

            def first_max(dst, x, n, dsc, mx):
                link(v.tensor_reduce(sm[mx], x, AX.X, ALU.max))
                link(TT(dst, x, col(mx, n), ALU.is_equal))
                link(TT(dst, dst, dsc, ALU.mult))
                link(v.tensor_reduce(sm["ix"], dst, AX.X, ALU.max))
                link(TT(dst, dst, col("ix", n), ALU.is_equal))

            glog, elog = lg[:, :, 0:NG], lg[:, :, NG:NR]
            first_max(ohg, glog, NG, descg, "gm")
            TT(dg, glog, col("gm", NG), ALU.subtract).then_inc(S["route_dif"], 1)
            link(TS(ohg, ohg, -NEG, NEG, ALU.mult, ALU.add))
            link(TT(le.rearrange("p c (g e) -> p c g e", g=NG), elog.rearrange("p c (g e) -> p c g e", g=NG),
                    bc(ohg.unsqueeze(3), [P, NT, NG, EG]), ALU.add))
            first_max(oh1, le, NE, desc, "m1")
            link(STT(out=rtmp, in0=oh1, scalar=4 * NEG, in1=le, op0=ALU.mult, op1=ALU.add))
            first_max(oh2, rtmp, NE, desc, "m2")
            TT(Mx, oh1, oh2, ALU.add).then_inc(S["M_onehot"], 1)
            TT(sm["tt"], sm["m2"], sm["m1"], ALU.subtract).then_inc(S["route_dif"], 1)
            v.wait_ge(S["route_exp"], 1)
            link(v.tensor_reduce(sm["gs"], dg, AX.X, ALU.add))
            v.wait_ge(S["route_exp"], 2)
            link(TS(sm["gp"], sm["tt"], 1.0, None, ALU.add))
            link(TT(sm["gp"], sm["gp"], sm["gs"], ALU.mult))
            link(v.reciprocal(sm["w1"], sm["gp"]))
            link(TT(sm["w2"], sm["w1"], sm["tt"], ALU.mult))
            src = ready(v, "rank")
            tell(v.tensor_copy(pos.rearrange("p a b -> p (a b)"), src[:, 0:NT * NE]), "routed")
            v.wait_ge(S["routed"], 2)
            v.wait_ge(S["M_onehot"], 1)
            for r, (oh, w) in enumerate(((oh1, "w1"), (oh2, "w2"))):
                pr, sr, vr = f"p{r + 1}", f"s{r + 1}", f"v{r + 1}"
                link(TT(rtmp, oh, pos, ALU.mult))
                link(v.tensor_reduce(sm[pr], rtmp, AX.X, ALU.add))
                link(TT(rtmp, oh, iota_c, ALU.mult))
                link(v.tensor_reduce(sm[sr], rtmp, AX.X, ALU.add))
                link(TS(sm[vr], sm[pr], float(CAP), None, ALU.is_lt))
                link(TT(sm[sr], sm[sr], sm[pr], ALU.add))
                link(TT(rtmp2[:, :, 0], sm[sr], sm[vr], ALU.mult))
                link(v.tensor_copy(slot_idx[:, :, r, 1], rtmp2[:, :, 0]))
                link(TS(rtmp2[:, :, 1], sm[vr], -1.0 * NE * CAP, 1.0 * NE * CAP, ALU.mult, ALU.add))
                link(TT(rtmp2[:, :, 1], rtmp2[:, :, 1], sm[sr], ALU.add))
                link(v.tensor_copy(slot_idx[:, :, r, 0], rtmp2[:, :, 1]))
            v.tensor_copy(ovf[:, 1:2], ones[:, 0:1]).then_inc(S["idx_ready"], 1)
            for r, (oh, w) in enumerate(((oh1, "w1"), (oh2, "w2"))):
                vr = f"v{r + 1}"
                link(TT(sm["mx"], sm[w], sm[vr], ALU.mult))
                link(TT(sm["ix"], sm[w], sm["mx"], ALU.subtract))
                link(v.tensor_copy(sm[w], sm["mx"]))
                if r == 0:
                    link(TT(cov, oh, col("ix", NE), ALU.mult))
                else:
                    link(TT(rtmp, oh, col("ix", NE), ALU.mult))
                    link(TT(cov, cov, rtmp, ALU.add))
            link(TT(sm["mx"], sm["v1"], sm["v2"], ALU.add))
            link(TS(sm["mx"], sm["mx"], -1.0, 2.0, ALU.mult, ALU.add))
            v.tensor_reduce(ovf[:, 0:1], sm["mx"], AX.X, ALU.add).then_inc(S["ovf_ready"], 1)
            tell(v.tensor_copy(flag_i[0:1, 0:1], ready(v, "flag")[0:1, 0:1]), "flag_ready")

            def ex_het(e, g, j):
                wait(v, "ex_tr", 2 * e + 2)
                wait(v, "ex_u", e - 1)
                v.tensor_copy(heT[j % 2][:, KT // 2:, :], bank[1][:, 0:4 * CAP].rearrange("p (k n) -> p k n", k=4))\
                    .then_inc(S["heT_d"], 1)

            def ex_hid(e, g, j):
                wait(v, "ex_u", e + 1)
                wait(v, "ex_sil", e + 1)
                wait(v, "ex_d1", e - 1)
                TT(hid[:, j % 2, :], sil[:, j % 2, :], bank[3 + 2 * (j % 2)][:, 0:JE * CAP], ALU.mult)\
                    .then_inc(S["ex_hid"], 1)

            def ex_y(e, g, j):
                wait(v, "ex_d1", e + 1)
                wait(v, f"st_y{j % 2}", 32 * g + 16 * (j // 2))
                v.tensor_copy(ysb[j % 2][0:CAP, HALF:D], bank[7][0:CAP, :]).then_inc(S["ex_yd"], 1)

            def trip(g, first=False, last=False):
                for j in range(UN):
                    e = g * UN + j
                    ex_hid(e, g, j)
                    if not (first and j == 0):
                        ex_y(e - 1, g if j else g - 1, (j - 1) % UN)
                    if not (last and j == UN - 1):
                        ex_het(e + 1, g if j < UN - 1 else g + 1, (j + 1) % UN)
                if last:
                    ex_y(e, g, UN - 1)

            ex_het(0, 0, 0)
            trip(0, first=True)
            with v.Fori(1, NE // UN - 1) as g:
                trip(g)
            trip(NE // UN - 1, last=True)

            v.wait_ge(S["flag_ready"], 1)
            fv = v.value_load(flag_i[0:1, 0:1], min_val=0, max_val=2 * T)
            with v.If(fv > 0):
                v.wait_ge(S["st_y0"], 16 * NE // 2)
                v.wait_ge(S["st_y1"], 16 * NE // 2)
                v.wait_ge(S["ex_d1"], NE)
                v.engine_nop().then_inc(S["ov_shift"], 1)
                v.engine_nop().then_inc(S["ov_hid"], 1)
                v.engine_nop().then_inc(S["ov_acc"], 1)
                with v.Fori(0, NE) as e:
                    for m in range(JE):
                        v.wait_ge(S["ov_gu"], 2 * (e * JE + m) + 2)
                        v.wait_ge(S["ov_sil"], e * JE + m + 1)
                        TT(ohid[:, m, :], osil, bank[1][:], ALU.mult).then_inc(S["ov_hid"], 1)
                    for c in range(NT):
                        for hf in range(NH2):
                            v.wait_ge(S["ov_d"], e * 2 * NT + c * NH2 + hf + 1)
                            xx = x1[:, c, hf * HALF:(hf + 1) * HALF]
                            ins = STT(out=xx, in0=bank[2][:], scalar=cov[:, c, 0:1], in1=xx, op0=ALU.mult, op1=ALU.add)
                            ins.then_inc(S["ov_acc"], 1)
                    v.tensor_copy(rtmp[:, :, 0:NE - 1], cov[:, :, 1:NE]).then_inc(S["ov_shift"], 1)
                    v.wait_ge(S["ov_shift"], e * 2 + 2)
                    v.tensor_copy(cov[:, :, 0:NE - 1], rtmp[:, :, 0:NE - 1]).then_inc(S["ov_shift"], 1)
                    v.wait_ge(S["ov_shift"], e * 2 + 3)
                v.wait_ge(S["ov_acc"], 2 * NT * NE + 1)
            v.engine_nop().then_inc(S["ov_over"], 1)

            v.wait_ge(S["ld_part2"], 64)
            for c in range(NT):
                v.wait_ge(S[f"ld_y{c}"], 32)
                for r in range(2):
                    ins = STT(out=x1[:, c, :], in0=gath[2 * c + r], scalar=sm[f"w{r + 1}"][:, c:c + 1], in1=x1[:, c, :],
                              op0=ALU.mult, op1=ALU.add)
                    if r == 0:
                        link(ins)
                    else:
                        ins.then_inc(S["x2_ready"], 1)
            for c in range(NT):
                v.wait_ge(S["rms3"], c + 1)
                link(v.reciprocal(sm["gm"][:, c:c + 1], sm["r3"][:, c:c + 1]))
                STT(out=x1[:, c, :], in0=x1[:, c, :], scalar=sm["gm"][:, c:c + 1], in1=gain3, op0=ALU.mult,
                    op1=ALU.mult).then_inc(S["out_ready"], 1)


_INS = ['x', 'norm_mix_gain', 'w_in', 'conv_dw_w', 'conv_dw_b', 'conv_ln_gain', 'conv_ln_bias', 'w_conv_out',
        'gdn_conv_w', 'gdn_a_log', 'gdn_dt_bias', 'gdn_norm_gain', 'w_gdn_out', 'w_out', 'norm_ffn_gain',
        'w_router_group', 'b_router_group', 'w_router_expert', 'b_router_expert', 'w_expert_gate', 'w_expert_up',
        'w_expert_down', 'final_norm_gain']
CAP = 96


def kernel(**inputs):
    import numpy as np
    import concourse.bacc as bacc
    from concourse.bass_utils import run_bass_kernel_spmd

    nc = bacc.Bacc("TRN2", target_bir_lowering=False, num_devices=1)
    arrays, args = {}, {}
    for name in _INS:
        v = np.ascontiguousarray(inputs[name])
        arrays[f"in_{name}_dram"] = v
        args[name] = nc.dram_tensor(f"in_{name}_dram", v.shape, mybir.dt.from_np(v.dtype), kind="ExternalInput").ap()
    shape = inputs["x"].shape
    out = nc.dram_tensor("out_0_dram", shape, F32, kind="ExternalOutput").ap()
    ne = inputs["w_router_expert"].shape[2]
    sorted_h = nc.dram_tensor("sorted_h", (ne * CAP, shape[2]), F32, kind="Internal").ap()
    sorted_y = nc.dram_tensor("sorted_y", (ne * CAP, shape[2]), F32, kind="Internal").ap()
    hybrid_layer(nc, args, out, sorted_h, sorted_y, CAP)
    r = run_bass_kernel_spmd(nc, [arrays], core_ids=[0])
    return r.results[0]["out_0_dram"]
```

```python
from contextlib import ExitStack

import concourse.bass as bass
from concourse import mybir

F32 = mybir.dt.float32
FR = mybir.dt.float32r
I32 = mybir.dt.int32
ACT = mybir.ActivationFunctionType
ALU = mybir.AluOpType
AX = mybir.AxisListType

P = 128
EPS = 1e-6
NEG = -1e30


class Signals:

    def __init__(self, nc, ctx):
        self.nc, self.ctx, self.sems, self.count = nc, ctx, {}, {}

    def __getitem__(self, name):
        if name not in self.sems:
            self.sems[name] = self.ctx.enter_context(self.nc.semaphore(name))
        return self.sems[name]

    def tell(self, ins, name, by=1):
        ins.then_inc(self[name], by)
        self.count[name] = self.count.get(name, 0) + by
        return self.count[name]


def hybrid_layer(nc, a, out, sorted_h, sorted_y, low_h, CAP):
    _, T, D = a["x"].shape
    KT = D // P
    NT = T // P
    CW = a["w_conv_out"].shape[1]
    TAPS = a["conv_dw_w"].shape[1]
    CF = CW // P
    H = a["gdn_a_log"].shape[1]
    VD = a["w_gdn_out"].shape[1]
    DK = VD // H
    NP = H // 2
    ST = a["gdn_conv_w"].shape[1]
    NG = a["w_router_group"].shape[2]
    NE = a["w_router_expert"].shape[2]
    EG = NE // NG
    DE = a["w_expert_gate"].shape[3]
    JE = DE // P
    HALF = 512
    NH2 = D // HALF
    WSLOT = KT * HALF
    ESLOT = 3 * KT * DE
    UN = 4
    LV = 7
    GRP = 4
    NR = NG + NE

    C_CONV, C_Q = 0, 2 * CW
    C_K, C_V, C_ZG = C_Q + VD, C_Q + 2 * VD, C_Q + 3 * VD
    C_AB = C_Q + 4 * VD
    C_GC, C_GD = C_AB + 2 * H, C_AB + 2 * H + D

    with ExitStack() as ctx:
        S = Signals(nc, ctx)
        tell = S.tell

        def wait(eng, name, n):
            if not isinstance(n, int) or n > 0:
                eng.wait_ge(S[name], n)

        top = [0]
        ARENA = 52800
        slot_idx = ctx.enter_context(nc.sbuf_tensor("slot_idx", [P, NT, 2, 2], I32))
        flag_i = ctx.enter_context(nc.sbuf_tensor("flag_i", [1, 1], I32))

        def take(n):
            top[0] += n
            assert top[0] <= ARENA, top[0]
            return top[0] - n

        def at(off, *shape):
            n = 1
            for s in shape:
                n *= s
            v = arena[:, off:off + n]
            if len(shape) == 1:
                return v
            names = "abcd"[:len(shape)]
            return v.rearrange(f"p ({' '.join(names)}) -> p {' '.join(names)}", **dict(zip(names[1:], shape[1:])))

        R_HT = take(KT * T)
        R_RING = take(3 * WSLOT)
        R_SIG = take(2 * KT * T)
        R_EXP = take(0)
        R_QK = take(2 * NP * T)
        R_VTOK = take(NT * VD)
        R_KDEC = take(NT * VD)
        R_QKT = take(H * T)
        R_U = take(H * T)
        R_ZG = take(NT * VD)
        assert top[0] - R_EXP >= 3 * ESLOT
        R_UP = take(CF * (T + TAPS - 1))
        R_ACC = take(CF * T)
        R_TMP = take(4 * T)

        def parts(name, off, *shape):
            n = 1
            for d in shape:
                n *= d
            with ExitStack() as below:
                if off > 0:
                    below.enter_context(nc.sbuf_tensor(f"{name}_below", [P, off], F32))
                v = below.enter_context(nc.sbuf_tensor(name, [P, n], FR))[:, :]
            names = "abcd"[:len(shape)]
            return v.rearrange(f"p ({' '.join(names)}) -> p {' '.join(names)}", **dict(zip(names[1:], shape[1:])))

        h_hi = parts("h_hi", R_HT, KT, T)
        h_lo = parts("h_lo", R_SIG + KT * T, KT, T)
        WP = KT * P
        NSL = 4
        o_parts = [R_RING + 2 * WSLOT, R_RING + 2 * WSLOT + 2 * WP, R_U, R_U + 2 * WP]
        w_hi = [parts(f"w_hi{i}", o, WP) for i, o in enumerate(o_parts)]
        w_lo = [parts(f"w_lo{i}", o + WP, WP) for i, o in enumerate(o_parts)]
        ab_hi = parts("ab_hi", R_ZG + D + T, KT, 2 * H)
        ab_lo = parts("ab_lo", R_ZG + D + T + KT * 2 * H, KT, 2 * H)
        arena = ctx.enter_context(nc.sbuf_tensor("arena", [P, ARENA], F32))

        x1 = at(R_HT, NT, D)
        xs = at(R_SIG, NT, D)
        dwstage = at(R_KDEC, CW)
        gcstage = at(R_VTOK, 3 * VD)
        abT = at(R_ZG + D, T)
        vT = at(R_SIG, NP, T)
        Tm = at(R_SIG, GRP, NT, P)
        Xm = at(R_SIG + GRP * T, GRP, NT, P)
        MT = at(R_SIG + 2 * GRP * T, GRP, NT, P)
        BT = at(R_SIG + 3 * GRP * T, GRP, NT, P)
        sig = [at(R_SIG, KT, T), at(R_QKT, KT, T)]
        yT = sig[0]
        kT = at(R_QK, NP, T)
        qT = at(R_QK + NP * T, NP, T)
        vtok = at(R_VTOK, NT, VD)
        kdec = at(R_KDEC, NT, VD)
        qkT = at(R_QKT, H, NT, P)
        NPAD = T + ST - 1
        pad = [at(R_QKT + i * NPAD, NPAD) for i in range(3)]
        cacc = [at(R_QKT + 3 * NPAD + i * T, T) for i in range(3)]
        U = at(R_U, H, NT, P)
        zgs = at(R_ZG, NT, VD)
        upad = at(R_UP, CF, T + TAPS - 1)
        oTc = [at(R_VTOK + c * VD, NP, P) for c in range(NT)]
        oT = vtok.rearrange("p c (f n) -> p f c n", f=NP)
        acc = at(R_ACC, CF, T)
        gb = [at(R_TMP + i * T, NT, P) for i in range(2)]
        dec = [at(R_TMP + (2 + i) * T, NT, P) for i in range(2)]
        sq = [at(R_TMP + i * T, NT, 2, DK) for i in range(2)]
        sgl = [at(R_TMP + (2 + i) * T, T) for i in range(2)]
        rbuf, vn, o_t, o_s = (at(R_TMP + i * T, T) for i in range(4))
        lnm, lnv = at(R_TMP, T), at(R_TMP + T, T)
        lsq = [at(R_TMP + (2 + i) * T, T) for i in range(2)]

        ident = at(take(P), P)
        triu = at(take(P), P)
        triu_s = at(take(P), P)
        negm = at(take(P), P)
        ones = at(take(P), P)
        mean_w = at(take(P), P)
        lmask = at(take(LV * P), LV, P)
        Sst = at(take(NP * P), NP, P)
        par = at(take(CF * (TAPS + 3) + 3 * NP * ST), CF * (TAPS + 3) + 3 * NP * ST)
        g1 = at(take(KT), KT)
        wab = at(take(KT * 2 * H), KT, 2 * H)
        absb = at(take(NT * 2 * H), NT, 2 * H)
        alog = at(take(H), H)
        dtb = at(take(H), H)
        gng = at(take(DK), DK)
        SC = NT * H

        def tok(n=1):
            return at(take(SC), NT, H)

        beta, gt, y_sp, sp_a, sp_b, gcum, glast, eg, egl, kds, nk, nq, rk, rq, brk, brk2 = (tok() for _ in range(16))
        gls = at(take(NT * NP), NT, NP)
        epsb = at(take(1), 1)
        epsb64 = at(take(1), 1)
        ssk = tok()
        ssq = tok()
        oss = at(take(NT * H), NT, H)
        ors = at(take(NT * H), NT, H)
        sm = {n: at(take(NT), NT) for n in ("ss1", "r1", "ss2", "r2", "ss3", "r3", "gm", "gs", "gp", "m1", "m2", "w1",
                                            "w2", "tt", "p1", "p2", "s1", "s2", "v1", "v2", "ix", "mx")}

        eslot = [R_EXP + i * ESLOT for i in (1, 0, 2)] + [R_RING]
        wg = [at(o, KT, DE) for o in eslot]
        wu = [at(o + KT * DE, KT, DE) for o in eslot]
        wd = [at(o + 2 * KT * DE, JE, D) for o in eslot]
        ysb = [at(R_RING + ESLOT + i * D, D) for i in range(2)]
        R_S2 = R_RING + 2 * WSLOT
        gain2 = at(R_S2, D)
        gain3 = at(R_S2 + D, D)
        wr = at(R_S2 + 2 * D, KT, NR)
        o2 = R_S2 + 2 * D + KT * NR
        heT = [at(o2 + i * KT * CAP, KT, CAP) for i in range(2)]
        assert o2 + 2 * KT * CAP <= R_RING + 3 * WSLOT
        hs = [at(R_SIG + i * D, D) for i in range(UN)]
        h2T = at(R_SIG + KT * T, KT, T)
        h2 = at(R_UP, NT, D)
        rt = R_TMP
        NRT = NT * NE

        def rte(i):
            return at(rt + i * NRT, NT, NE)

        lg = at(rt + 10 * NRT, NT, NR)
        le, oh1, oh2, pos, Mx, cov, rtmp, desc, iota_c = (rte(i) for i in range(9))
        rtmp2 = rte(9)
        ohg = at(rt + 10 * NRT + NT * NR, NT, NG)
        dg = at(rt + 10 * NRT + NT * NR + NT * NG, NT, NG)
        rbias = at(rt + 10 * NRT + NT * NR + 2 * NT * NG, NR)
        descg = at(rt + 10 * NRT + NT * NR + 2 * NT * NG + NR, NT, NG)
        ovf = at(rt + 10 * NRT + NT * NR + 3 * NT * NG + NR, 2)
        e0 = rt + 10 * NRT + NT * NR + 3 * NT * NG + NR + 2
        sil = at(rt, 2, JE * CAP)
        hid = at(e0, 2, JE * CAP)
        assert e0 + 2 * JE * CAP <= rt + 4 * T and 2 * JE * CAP <= 3 * NRT * 2, (e0 + 2 * JE * CAP - rt)
        osil = at(R_RING + ESLOT, T)
        ohid = at(R_SIG, JE, T)
        zero = at(R_ZG, D)
        gath = [at(R_EXP + i * D, D) for i in range(2 * NT)]

        bank = [ctx.enter_context(nc.psum_tensor(f"bank{i}", [P, 512], F32))[:, :] for i in range(8)]

        def bc(ap, shape):
            return ap.to_broadcast(shape)

        def heads(v):
            return v.rearrange("p (h d) -> p h d", h=H)

        def per_head(s, c):
            return bc(s[:, c, :].unsqueeze(2), [P, H, DK])

        jobs = {}

        win = a["w_in"][0].rearrange("(p k) n -> p k n", k=KT)
        chunks = [("k", win[:, :, C_K:C_K + VD]), ("q", win[:, :, C_Q:C_Q + VD]), ("v", win[:, :, C_V:C_V + VD]),
                  ("glu0", None), ("glu1", None), ("zg", win[:, :, C_ZG:C_ZG + VD]),
                  ("gc0", win[:, :, C_GC:C_GC + HALF]), ("gc1", win[:, :, C_GC + HALF:C_GC + D]),
                  ("gd0", win[:, :, C_GD:C_GD + HALF]), ("gd1", win[:, :, C_GD + HALF:C_GD + D]),
                  ("wco", a["w_conv_out"][0].rearrange("(f p) n -> p f n", p=P)),
                  ("wgo", a["w_gdn_out"][0].rearrange("(f p) n -> p f n", p=P)),
                  ("wo0", a["w_out"][0].rearrange("(k p) n -> p k n", p=P)[:, :, 0:HALF]),
                  ("wo1", a["w_out"][0].rearrange("(k p) n -> p k n", p=P)[:, :, HALF:D])]
        cidx = {n: i for i, (n, _) in enumerate(chunks)}
        NWIN = cidx["wco"]
        NPC = WSLOT // WP
        place, arrived = {}, {}
        for n in range(NWIN):
            loads = 16 * (n // 2 + 1) + (16 if n >= cidx["glu0"] else 0)
            place[n], arrived[n] = R_RING + (n % 2) * WSLOT, (f"ld_w{n % 2}", loads)
        place[cidx["wco"]], arrived[cidx["wco"]] = R_QK, ("ld_w2", 16)
        place[cidx["wgo"]], arrived[cidx["wgo"]] = R_RING, ("ld_w0", 16 * (NWIN // 2 + 2))
        place[cidx["wo0"]], arrived[cidx["wo0"]] = R_RING + WSLOT, ("ld_w1", 16 * (NWIN // 2 + 2))
        place[cidx["wo1"]], arrived[cidx["wo1"]] = R_U, ("ld_w2", 32)
        FIRST_GATE = cidx["gc0"] * NPC

        def pslot(s):
            return s % NSL if s < FIRST_GATE else s % 2

        def raw(s):
            w = at(place[s // NPC], KT, HALF)
            i = s % NPC
            if s // NPC == cidx["zg"]:
                return w[:, i * KT // NPC:(i + 1) * KT // NPC, :]
            return w[:, :, i * P:(i + 1) * P]

        def as_raw(v, s):
            return v.rearrange("p (k n) -> p k n", n=HALF if s // NPC == cidx["zg"] else P)

        def lo_done(s):
            return ("w_lo_v", s + 1) if s < NPC else ("w_lo_p", s - NPC + 1)

        def slot_user(s):
            if s < NSL:
                return None
            return s - NSL if s < FIRST_GATE else (s - 4 if s < FIRST_GATE + 2 else s - 2)

        block = ctx.enter_context(nc.Block())

        @block.tensor
        def _(pe):
            used = [None] * 8
            nxt = [0]
            held = []

            def begin(name, freed_by, b=None):
                if b is None:
                    if nxt[0] % 8 in held:
                        nxt[0] += 1
                    b = nxt[0] % 8
                    nxt[0] += 1
                if used[b] is not None:
                    wait(pe, *used[b])
                used[b] = freed_by
                jobs[name] = [b, None, None]
                return bank[b]

            def end(ins, name, fam):
                n = tell(ins, fam)
                jobs[name][1:] = [fam, n]

            wait(pe, "consts", 2)
            for k in range(KT):
                b = begin(("hT", k), ("h_lo", k + 1))
                for c in range(NT):
                    if k == 0:
                        wait(pe, "xs_ready", c + 1)
                    ins = pe.transpose(b[:, c * P:(c + 1) * P], xs[:, c, :].rearrange("p (q k) -> p k q", k=KT)[:, k, :],
                                       ident)
                end(ins, ("hT", k), "setup_mm")
            b = begin("par", ("setup_ready", 1))
            wait(pe, "ld_stage", 80)
            NS = TAPS + 3
            for i in range(CF):
                pe.transpose(b[:, i * NS:(i + 1) * NS], dwstage[0:NS, i * P:(i + 1) * P], ident[0:NS, 0:NS])
            for f in range(3 * NP):
                o = CF * NS + f * ST
                ins = pe.transpose(b[:, o:o + ST], gcstage[0:ST, f * P:(f + 1) * P], ident[0:ST, 0:ST])
            end(ins, "par", "setup_mm")

            def split_product(o, w_parts, x_parts, first, last):
                (wh, wl), (xh, xl) = w_parts, x_parts
                pe.matmul(o, wh, xh, start=first, stop=False)
                pe.matmul(o, wh, xl, start=False, stop=False)
                return pe.matmul(o, wl, xh, start=False, stop=last)

            b = begin("abT", ("h_hi", KT + 2))
            wait(pe, "h_lo", KT)
            wait(pe, "h_lo", KT + 1)
            for k in range(KT):
                ins = split_product(b[0:2 * H, :], (ab_hi[:, k, :], ab_lo[:, k, :]), (h_hi[:, k, :], h_lo[:, k, :]),
                                    k == 0, k == KT - 1)
            end(ins, "abT", "setup_mm")

            def proj(chunk, f, name, freed_by, fam):
                b = begin(name, freed_by)
                s = cidx[chunk] * NPC + f
                wait(pe, *lo_done(s))
                wh, wl = (as_raw(w[pslot(s)], s) for w in (w_hi, w_lo))
                for k in range(KT):
                    ins = split_product(b[:], (wh[:, k, :], wl[:, k, :]), (h_hi[:, k, :], h_lo[:, k, :]), k == 0,
                                        k == KT - 1)
                end(ins, name, fam)
                jobs[("w", s)] = (fam, S.count[fam])

            def tok_tr(src, p, name, freed_by, fam):
                b = begin(name, freed_by)
                for c in range(NT):
                    ins = pe.transpose(b[:, c * P:(c + 1) * P], src[:, p, c * P:(c + 1) * P], ident)
                end(ins, name, fam)

            for f in range(NP):
                proj("k", f, ("qkv", f), ("pad_ready", f + 1), "qkv_mm")
                if f == 0:
                    b = begin("ab", ("setup_ready", 2))
                    wait(pe, "h_hi", KT + 2)
                    for c in range(NT):
                        ins = pe.transpose(b[:, c * 2 * H:(c + 1) * 2 * H], abT[0:2 * H, c * P:(c + 1) * P],
                                           ident[0:2 * H, 0:2 * H])
                    end(ins, "ab", "setup_mm")
            b = begin("gcum", ("gcum_ready", 2))
            wait(pe, "g_ready", 1)
            wait(pe, "consts", 7)
            pe.matmul(b[:, 0:SC], triu, gt.rearrange("p a b -> p (a b)"), start=True, stop=True)
            ins = pe.matmul(b[:, SC:2 * SC], ones, gt.rearrange("p a b -> p (a b)"), start=True, stop=True)
            end(ins, "gcum", "setup_mm")
            for f in range(NP):
                proj("q", f, ("qkv", NP + f), ("pad_ready", NP + f + 1), "qkv_mm")
            for p in range(NP):
                wait(pe, "silu_ready", p + 1)
                tok_tr(kT, p, ("ktok", p), ("ktok_copied", p + 1), "tok_tr")
            for f in range(NP):
                proj("v", f, ("qkv", 2 * NP + f), ("pad_ready", 2 * NP + f + 1), "qkv_mm")
            for p in range(NP):
                wait(pe, "silu_ready", NP + p + 1)
                tok_tr(qT, p, ("qtok", p), ("sq_ready", NP + p + 1), "tok_tr")
            for f in range(CF):
                proj("glu0", 2 * f, ("ca", f), ("glu_ready", f + 1), "glu_mm")
                proj("glu0", 2 * f + 1, ("cb", f), ("glu_sig", f + 1), "glu_mm")
            for p in range(NP):
                wait(pe, "silu_ready", 2 * NP + p + 1)
                tok_tr(vT, p, ("vtok", p), ("vtok_ready", p + 1), "vtok_tr")
            zb = [begin(("zg", c), ("zg_silu", c + 1)) for c in range(NT)]
            for i in range(NPC):
                s = cidx["zg"] * NPC + i
                wait(pe, *lo_done(s))
                wh, wl = (as_raw(w[pslot(s)], s) for w in (w_hi, w_lo))
                for c in range(NT):
                    cs = slice(c * P, (c + 1) * P)
                    for kk in range(KT // NPC):
                        k = i * KT // NPC + kk
                        ins = split_product(zb[c][:], (h_hi[:, k, cs], h_lo[:, k, cs]), (wh[:, kk, :], wl[:, kk, :]),
                                            k == 0, k == KT - 1)
                    if i == NPC - 1:
                        end(ins, ("zg", c), "zg_mm")
                if i < NPC - 1:
                    jobs[("w", s)] = ("zg_mm", tell(ins, "zg_mm"))
            jobs[("w", s)] = ("zg_mm", S.count["zg_mm"])

            def prep(h):
                t, r = h // 2, slice(DK * (h % 2), DK * (h % 2) + DK)
                b = begin(("G", h), ("diff_ready", NT * (h + 1)))
                wait(pe, "gb_ready", h + 1)
                for c in range(NT):
                    ins = pe.matmul(b[:, c * P:(c + 1) * P], gb[h % 2][:, c, :], triu, start=True, stop=True)
                end(ins, ("G", h), "G_mm")
                b = begin(("KK", h), ("M_ready", NT * (h + 1)))
                for c in range(NT):
                    kc = kT[r, t, c * P:(c + 1) * P]
                    ins = pe.matmul(b[:, c * P:(c + 1) * P], kc, kc, start=True, stop=True)
                end(ins, ("KK", h), "gram_mm")
                b = begin(("QK", h), ("qk_ready", NT * (h + 1)))
                for c in range(NT):
                    ins = pe.matmul(b[:, c * P:(c + 1) * P], kT[r, t, c * P:(c + 1) * P], qT[r, t, c * P:(c + 1) * P],
                                    start=True, stop=True)
                end(ins, ("QK", h), "gram_mm")

            for grp in range(H // GRP):
                hh = range(grp * GRP, (grp + 1) * GRP)
                for h in hh:
                    prep(h)
                for h in hh:
                    b = begin(("T0", h), ("T_init", h + 1))
                    wait(pe, "U0_ready", h + 1)
                    for c in range(NT):
                        ins = pe.transpose(b[:, c * P:(c + 1) * P], U[:, h, c, :], ident)
                    end(ins, ("T0", h), "gram_mm")
                for lv in range(1, LV):
                    for h in hh:
                        q = h % GRP
                        n_lv = (grp * (LV - 1) + lv - 1) * GRP + q
                        b = begin(("X", h, lv), ("X_ready", n_lv + 1))
                        wait(pe, "BT_ready", n_lv + 1)
                        if lv == 1:
                            wait(pe, "T_init", h + 1)
                        else:
                            wait(pe, "T_ready", (grp * (LV - 2) + lv - 2) * GRP + q + 1)
                        for c in range(NT):
                            ins = pe.matmul(b[:, c * P:(c + 1) * P], BT[:, q, c, :], Tm[:, q, c, :], start=True,
                                            stop=True)
                        end(ins, ("X", h, lv), "X_mm")
                    for h in hh:
                        q = h % GRP
                        n_lv = (grp * (LV - 1) + lv - 1) * GRP + q
                        n_t = (grp * (LV - 2) + lv - 1) * GRP + q
                        last = lv == LV - 1
                        fb = ("U_ready", h + 1) if last else ("T_ready", n_t + 1)
                        b = begin(("D", h, lv), fb)
                        wait(pe, "X_ready", n_lv + 1)
                        if lv > 1:
                            wait(pe, "U_tr_ready", (grp * (LV - 2) + lv - 2) * GRP + q + 1)
                        for c in range(NT):
                            if last:
                                ins = pe.matmul(b[:, c * P:(c + 1) * P], Xm[:, q, c, :], U[:, h, c, :], start=True,
                                                stop=True)
                            else:
                                ins = pe.matmul(b[:, c * P:(c + 1) * P], U[:, h, c, :], Xm[:, q, c, :], start=True,
                                                stop=True)
                        end(ins, ("D", h, lv), "D_mm")
                    if lv == LV - 1:
                        continue
                    for h in hh:
                        q = h % GRP
                        n_t = (grp * (LV - 2) + lv - 1) * GRP + q
                        b = begin(("TT", h, lv), ("U_tr_ready", n_t + 1))
                        wait(pe, "T_ready", n_t + 1)
                        for c in range(NT):
                            ins = pe.transpose(b[:, c * P:(c + 1) * P], Tm[:, q, c, :], ident)
                        end(ins, ("TT", h, lv), "gram_mm")

            gates = [(g, m) for g in range(2) for m in range(KT)]

            def gate():
                g, m = gates.pop(0)
                if len(gates) == 2 * KT - 1:
                    wait(pe, "ld_hlo", 16)
                proj(f"g{'cd'[g]}{m // NP}", m % NP, ("gate", g, m), ("gate_ready", g * KT + m + 1), "gate_mm")

            def o_tr(c):
                b = begin(("oT", c), ("oT_ready", c + 1))
                wait(pe, "og_ready", c + 1)
                for p in range(NP):
                    ins = pe.transpose(b[:, p * P:(p + 1) * P], o_s[:, p * P:(p + 1) * P], ident)
                end(ins, ("oT", c), "oT_tr")

            for c in range(NT):
                cs = slice(c * P, (c + 1) * P)
                if c > 0:
                    b = begin(("KS", c), ("st_ready", 2 * c - 1))
                    wait(pe, "S_ready", 2 * c)
                    for p in range(NP):
                        ins = pe.matmul(b[:, p * P:(p + 1) * P], kT[:, p, cs], Sst[:, p, :], start=True, stop=True)
                    end(ins, ("KS", c), "scan_mm")
                    o_tr(c - 1)
                b = begin(("VN", c), ("vn_ready", c + 1))
                wait(pe, "U_ready", H)
                wait(pe, "vtok_ready", NP)
                wait(pe, "r_ready", c)
                for h in range(H):
                    rr = vtok[:, 0, :] if c == 0 else rbuf
                    ins = pe.matmul(b[:, h * DK:(h + 1) * DK], U[:, h, c, :], rr[:, h * DK:(h + 1) * DK], start=True,
                                    stop=True)
                end(ins, ("VN", c), "scan_mm")
                gate()
                if c > 0:
                    b = begin(("QS", c), ("st_ready", 2 * c))
                    for p in range(NP):
                        ins = pe.matmul(b[:, p * P:(p + 1) * P], qT[:, p, cs], Sst[:, p, :], start=True, stop=True)
                    end(ins, ("QS", c), "QS_mm")
                wait(pe, "vn_ready", c + 1)
                if c < NT - 1:
                    b = begin(("DS", c), ("S_ready", 2 * c + 2))
                    wait(pe, "kdec_ready", c + 1)
                    for p in range(NP):
                        ins = pe.matmul(b[:, p * P:(p + 1) * P], kdec[:, c, p * P:(p + 1) * P], vn[:, p * P:(p + 1) * P],
                                        start=True, stop=True)
                    end(ins, ("DS", c), "scan_mm")
                b = begin(("OV", c), ("ov_read", c + 1))
                wait(pe, "qk_ready", NT * H)
                for h in range(H):
                    ins = pe.matmul(b[:, h * DK:(h + 1) * DK], qkT[:, h, c, :], vn[:, h * DK:(h + 1) * DK], start=True,
                                    stop=True)
                end(ins, ("OV", c), "OV_mm")
                gate()
            b = begin("mean", ("xc_ready", CF))
            wait(pe, "dw_done", CF)
            for i in range(CF):
                ins = pe.matmul(b[:], mean_w, acc[:, i, :], start=(i == 0), stop=(i == CF - 1))
            end(ins, "mean", "scan_mm")
            o_tr(NT - 1)
            gate()
            gate()
            b = begin("var", ("sd_ready", 1))
            for i in range(CF):
                wait(pe, "lsq_ready", i + 1)
                ins = pe.matmul(b[:], mean_w, lsq[i % 2], start=(i == 0), stop=(i == CF - 1))
                tell(ins, "var_mm")
            jobs["var"][1:] = ["var_mm", CF]
            while gates:
                gate()

            n = cidx["wco"]
            wait(pe, *arrived[n])
            wait(pe, "u_ready", CF)
            wco = at(place[n], CF, D)
            for m in range(KT):
                b = begin(("yc", m), ("yc_ready", m + 1))
                for f in range(CF):
                    ins = pe.matmul(b[:], wco[:, f, m * P:(m + 1) * P], acc[:, f, :], start=(f == 0), stop=(f == CF - 1))
                end(ins, ("yc", m), "yc_mm")
            n = cidx["wgo"]
            wait(pe, *arrived[n])
            wait(pe, "oT_ready", NT)
            wgo = at(place[n], NP, D)
            for m in range(KT):
                b = begin(("yd", m), ("yd_ready", m + 1))
                for f in range(NP):
                    ins = pe.matmul(b[:], wgo[:, f, m * P:(m + 1) * P], oT[:, f, :, :], start=(f == 0), stop=(f == NP - 1))
                end(ins, ("yd", m), "yd_mm")
            def h2_tile(c):
                for half in range(2):
                    b = begin(("h2T", c, half), ("h2T_ready", 2 * c + half + 1))
                    wait(pe, "h2_ready", c + 1)
                    for k in range(4):
                        ins = pe.transpose(b[:, k * P:(k + 1) * P],
                                           h2[:, c, :].rearrange("p (q k) -> p k q", k=KT)[:, 4 * half + k, :], ident)
                    end(ins, ("h2T", c, half), "route_mm")

            def logits_tile(c):
                if c == 0:
                    begin("logits", ("routed", 1))
                    held.append(jobs["logits"][0])
                    wait(pe, "ld_part2", 64)
                b = bank[jobs["logits"][0]]
                wait(pe, "h2T_ready", 2 * c + 2)
                for k in range(KT):
                    ins = pe.matmul(b[:, c * NR:(c + 1) * NR], h2T[:, k, c * P:(c + 1) * P], wr[:, k, :],
                                    start=(k == 0), stop=(k == KT - 1))
                end(ins, "logits", "route_mm")

            for c in range(NT):
                for hf in range(NH2):
                    n = cidx[f"wo{hf}"]
                    if c == 0:
                        wait(pe, *arrived[n])
                    b = begin(("wo", c, hf), ("x1_ready", c * NH2 + hf + 1))
                    for m in range(KT):
                        if hf == 0 and c == 0:
                            wait(pe, "y_ready", m + 1)
                        ins = pe.matmul(b[:], yT[:, m, c * P:(c + 1) * P], at(place[n], KT, HALF)[:, m, :], start=(m == 0),
                                        stop=(m == KT - 1))
                    end(ins, ("wo", c, hf), "wo_mm")
                if c > 0:
                    h2_tile(c - 1)
                if c > 1:
                    logits_tile(c - 2)

            h2_tile(NT - 1)
            logits_tile(NT - 2)
            logits_tile(NT - 1)
            held.clear()
            b = begin("rank", ("routed", 2))
            wait(pe, "M_onehot", 1)
            for c in range(NT):
                for cc in range(c + 1):
                    ins = pe.matmul(b[:, c * NE:(c + 1) * NE], triu_s if cc == c else ones, Mx[:, cc, :],
                                    start=(cc == 0), stop=(cc == c))
            end(ins, "rank", "route_mm")
            b = begin("flag", ("flag_ready", 1))
            wait(pe, "ovf_ready", 1)
            ins = pe.matmul(b[0:1, 0:1], ones[:, 0:1], ovf[:, 0:1], start=True, stop=True)
            end(ins, "flag", "route_mm")
            for b in range(8):
                wait(pe, *used[b])

            def ex_tr(e, g, j):
                wait(pe, f"ld_h{j}", 16 * (g + 1))
                wait(pe, "heT_a", e)
                wait(pe, "heT_d", e)
                for k in range(KT):
                    o = bank[k // 4][:, (k % 4) * CAP:(k % 4 + 1) * CAP]
                    ins = pe.transpose(o, hs[j][0:CAP, :].rearrange("p (q k) -> p k q", k=KT)[:, k, :],
                                       ident[0:CAP, 0:CAP])
                    if k % 4 == 3:
                        ins.then_inc(S["ex_tr"], 1)

            def ex_gu(e, g, j):
                wait(pe, f"ld_e{j}", 48 * (g + 1))
                wait(pe, "heT_a", e + 1)
                wait(pe, "heT_d", e + 1)
                wait(pe, "ex_sil", e - 1)
                wait(pe, "ex_hid", e - 1)
                for w, bk in ((wg, 2 + 2 * (j % 2)), (wu, 3 + 2 * (j % 2))):
                    for m in range(JE):
                        for k in range(KT):
                            ins = pe.matmul(bank[bk][:, m * CAP:(m + 1) * CAP], w[j][:, k, m * P:(m + 1) * P],
                                            heT[j % 2][:, k, :], start=(k == 0), stop=(k == KT - 1))
                    ins.then_inc(S["ex_g" if w is wg else "ex_u"], 1)

            def ex_dn(e, g, j):
                wait(pe, "ex_hid", e + 1)
                wait(pe, "ex_ya", e)
                wait(pe, "ex_yd", e)
                for hf in range(NH2):
                    for m in range(JE):
                        ins = pe.matmul(bank[6 + hf][0:CAP, :], hid[:, j % 2, m * CAP:(m + 1) * CAP],
                                        wd[j][:, m, hf * HALF:(hf + 1) * HALF], start=(m == 0), stop=(m == JE - 1))
                    ins.then_inc(S["ex_d0" if hf == 0 else "ex_d1"], 1)

            def trip(g, first=False, last=False):
                for j in range(UN):
                    e = g * UN + j
                    ex_gu(e, g, j)
                    if not (last and j == UN - 1):
                        ex_tr(e + 1, g if j < UN - 1 else g + 1, (j + 1) % UN)
                    if not (first and j == 0):
                        ex_dn(e - 1, g if j else g - 1, (j - 1) % UN)
                if last:
                    ex_dn(e, g, UN - 1)

            NTRIP = NE // UN
            ex_tr(0, 0, 0)
            trip(0, first=True)
            with pe.Fori(1, NTRIP - 1) as g:
                trip(g)
            trip(NTRIP - 1, last=True)

            wait(pe, "flag_ready", 1)
            wait(pe, "ex_ya", NE)
            wait(pe, "ex_yd", NE)
            fv = pe.value_load(flag_i[0:1, 0:1], min_val=0, max_val=2 * T)
            with pe.If(fv > 0):
                with pe.Fori(0, NE) as e:
                    wait(pe, "ov_ld", 48 * e + 48)
                    for m in range(JE):
                        pe.wait_ge(S["ov_hid"], e * JE + m + 1)
                        for w, bk in ((wg, 0), (wu, 1)):
                            for k in range(KT):
                                ins = pe.matmul(bank[bk][:], w[0][:, k, m * P:(m + 1) * P], h2T[:, k, :],
                                                start=(k == 0), stop=(k == KT - 1))
                            ins.then_inc(S["ov_gu"], 1)
                    for c in range(NT):
                        for hf in range(NH2):
                            if c == 0 and hf == 0:
                                pe.wait_ge(S["ov_hid"], e * JE + JE + 1)
                            pe.wait_ge(S["ov_acc"], e * 2 * NT + c * NH2 + hf + 1)
                            for m in range(JE):
                                ins = pe.matmul(bank[2][:], ohid[:, m, c * P:(c + 1) * P],
                                                wd[0][:, m, hf * HALF:(hf + 1) * HALF], start=(m == 0),
                                                stop=(m == JE - 1))
                            ins.then_inc(S["ov_d"], 1)

        def ready(eng, name):
            b, fam, n = jobs[name]
            wait(eng, fam, n)
            return bank[b]

        @block.sync
        def _(sp):
            xv = a["x"][0].rearrange("(c p) d -> c p d", p=P)
            for c in range(NT):
                sp.dma_start(xs[:, c, :], xv[c]).then_inc(S[f"ld_x{c}"], 16)
            sp.dma_start(g1, a["norm_mix_gain"][0].rearrange("(p k) -> p k", k=KT)).then_inc(S["ld_small"], 16)
            sp.dma_start(dwstage[0:TAPS, :], a["conv_dw_w"][0]).then_inc(S["ld_stage"], 16)
            for i, n in enumerate(("conv_dw_b", "conv_ln_gain", "conv_ln_bias")):
                sp.dma_start(dwstage[TAPS + i:TAPS + i + 1, :], a[n]).then_inc(S["ld_stage"], 16)
            sp.dma_start(gcstage[0:ST, :], a["gdn_conv_w"][0]).then_inc(S["ld_stage"], 16)
            sp.dma_start(wab, win[:, :, C_AB:C_AB + 2 * H]).then_inc(S["ld_ab"], 16)

            def load(n):
                src = chunks[n][1]
                if src is None:
                    w = at(place[n], KT, 2, 2, P)
                    for side in range(2):
                        o = C_CONV + side * CW + (n - cidx["glu0"]) * 2 * P
                        sp.dma_start(w[:, :, :, side, :], win[:, :, o:o + 2 * P].rearrange("p k (f n) -> p k f n", n=P))\
                            .then_inc(S[arrived[n][0]], 16)
                    return
                sp.dma_start(at(place[n], src.shape[1], src.shape[2]), src).then_inc(S[arrived[n][0]], 16)

            load(0)
            load(1)
            for dst, name in ((alog, "gdn_a_log"), (dtb, "gdn_dt_bias"), (gng, "gdn_norm_gain")):
                sp.dma_start(dst, a[name][0].partition_broadcast(P)).then_inc(S["ld_small"], 16)
            zeros = list(range(NE * CAP // P))
            wait(sp, "consts", 7)
            for n in range(2, NWIN):
                if n == 4:
                    wait(sp, "h_lo", KT)
                    sp.dma_start(low_h, h_lo.rearrange("p k n -> p (k n)").bitcast(F32)).then_inc(S["st_hlo"], 16)
                for i in zeros[:8]:
                    sp.dma_start(sorted_h[i * P:(i + 1) * P, :], zero).then_inc(S["zeroed"], 16)
                zeros = zeros[8:]
                wait(sp, *lo_done((n - 1) * NPC - 1))
                load(n)
            wait(sp, *jobs[("QS", NT - 1)][1:])
            load(cidx["wco"])
            wait(sp, *lo_done((cidx["gd0"] + 1) * NPC - 1))
            load(cidx["wgo"])
            wait(sp, *lo_done((cidx["gd1"] + 1) * NPC - 1))
            load(cidx["wo0"])
            wait(sp, *arrived[cidx["wco"]])
            load(cidx["wo1"])
            wait(sp, "gate_mm", 2 * KT)
            for c in range(NT):
                sp.dma_start(x1[:, c, :], xv[c]).then_inc(S[f"ld_x{c}"], 16)
            wgd = a["w_expert_gate"][0].rearrange("(g j) (p k) n -> g j p k n", j=UN, k=KT)
            wud = a["w_expert_up"][0].rearrange("(g j) (p k) n -> g j p k n", j=UN, k=KT)
            wdd = a["w_expert_down"][0].rearrange("(g j) (m p) n -> g j p m n", j=UN, p=P)
            shv = sorted_h.rearrange("(g j s) n -> g j s n", j=UN, s=CAP)

            def expert(g, j):
                sp.dma_start(wg[j], wgd[g, j]).then_inc(S[f"ld_e{j}"], 16)
                sp.dma_start(wu[j], wud[g, j]).then_inc(S[f"ld_e{j}"], 16)
                sp.dma_start(wd[j], wdd[g, j]).then_inc(S[f"ld_e{j}"], 16)

            sp.dma_start(gain2, a["norm_ffn_gain"][0].partition_broadcast(P)).then_inc(S["ld_part2"], 16)
            sp.dma_start(gain3, a["final_norm_gain"].partition_broadcast(P)).then_inc(S["ld_part2"], 16)
            sp.dma_start(wr[:, :, 0:NG], a["w_router_group"][0].rearrange("(p k) n -> p k n", k=KT)).then_inc(S["ld_part2"], 16)
            sp.dma_start(wr[:, :, NG:NR], a["w_router_expert"][0].rearrange("(p k) n -> p k n", k=KT)).then_inc(S["ld_part2"], 16)
            wait(sp, "y_ready", KT)
            expert(0, 0)
            expert(0, 1)
            wait(sp, "wo_mm", 2 * NT)
            expert(0, 2)
            expert(0, 3)
            wait(sp, "scattered", 16 * 2 * NT)
            for j in range(UN):
                sp.dma_start(hs[j][0:CAP, :], shv[0, j]).then_inc(S[f"ld_h{j}"], 16)
            with sp.Fori(1, NE // UN) as g:
                for j in range(UN):
                    e = g * UN + j
                    sp.wait_ge(S["ex_tr"], 2 * (e - UN) + 2)
                    sp.dma_start(hs[j][0:CAP, :], shv[g, j]).then_inc(S[f"ld_h{j}"], 16)
                    sp.wait_ge(S["ex_d1"], e - UN + 1)
                    expert(g, j)

            wait(sp, "flag_ready", 1)
            fv = sp.value_load(flag_i[0:1, 0:1], min_val=0, max_val=2 * T)
            with sp.If(fv > 0):
                wait(sp, "ex_d1", NE)
                with sp.Fori(0, NE) as e:
                    sp.wait_ge(S["ov_shift"], 2 * e + 1)
                    sp.dma_start(wg[0], a["w_expert_gate"][0].rearrange("e (p k) n -> e p k n", k=KT)[e]).then_inc(S["ov_ld"], 16)
                    sp.dma_start(wu[0], a["w_expert_up"][0].rearrange("e (p k) n -> e p k n", k=KT)[e]).then_inc(S["ov_ld"], 16)
                    sp.dma_start(wd[0], a["w_expert_down"][0].rearrange("e (m p) n -> e p m n", p=P)[e]).then_inc(S["ov_ld"], 16)
            ov = out[0].rearrange("(c p) d -> c p d", p=P)
            for c in range(NT):
                wait(sp, "out_ready", c + 1)
                sp.dma_start(ov[c], x1[:, c, :]).then_inc(S["st_out"], 16)
            wait(sp, "st_out", 16 * NT)

        @block.gpsimd
        def _(gp):
            n_chain = [0]

            def link(ins):
                n_chain[0] += 1
                ins.then_inc(S["pool_chain"], 1)
                gp.wait_ge(S["pool_chain"], n_chain[0])

            link(gp.memset(ones, 1.0))
            gp.memset(mean_w, 1.0 / CW).then_inc(S["consts"], 1)

            def sel(dst, src, pattern, base, cm, op=ALU.is_ge, fill=0.0):
                return gp.affine_select(out=dst, in_=src, compare_op=op, fill=fill, base=base, pattern=pattern,
                                        channel_multiplier=cm)

            sel(ident, ones, [[1, P]], 0, -1, ALU.is_equal).then_inc(S["consts"], 1)
            sel(triu, ones, [[1, P]], 0, -1).then_inc(S["consts"], 1)
            sel(triu_s, ones, [[1, P]], -1, -1).then_inc(S["consts"], 1)
            link(gp.memset(negm, 0.0))
            sel(negm, negm, [[1, P]], 0, -1, fill=NEG).then_inc(S["consts"], 1)
            for lv in range(LV):
                s = 2 ** lv
                if 2 * s == P:
                    link(gp.tensor_copy(lmask[:, lv, :], ones))
                    continue
                s2 = 2 * s
                v = lmask[:, lv, :].rearrange("p (b s) -> p b s", s=s2)
                link(sel(v, ones.rearrange("p (b s) -> p b s", s=s2), [[-s2, P // s2], [0, s2]], 0, 1))
                link(sel(v, v, [[s2, P // s2], [0, s2]], s2 - 1, -1))
            gp.wait_ge(S["consts"], 5)
            for lv in range(LV - 1, 0, -1):
                link(gp.tensor_tensor(lmask[:, lv, :], lmask[:, lv, :], lmask[:, lv - 1, :], ALU.subtract))
            link(gp.tensor_tensor(lmask[:, 0, :], lmask[:, 0, :], ident, ALU.subtract))
            for lv in range(LV):
                link(gp.tensor_tensor(lmask[:, lv, :], lmask[:, lv, :], triu_s, ALU.mult))
            gp.memset(Sst, 0.0).then_inc(S["consts"], 1)
            for i in range(3):
                link(gp.memset(pad[i][:, 0:ST - 1], 0.0))
            gp.memset(zero, 0.0).then_inc(S["consts"], 1)
            for i in range(CF):
                gp.memset(upad[:, i, 0:TAPS - 1], 0.0).then_inc(S["upad_zero"], 1)

            def lo_part(s):
                gp.wait_ge(S["w_hi"], s + 1)
                gp.tensor_tensor(as_raw(w_lo[pslot(s)], s), raw(s), as_raw(w_hi[pslot(s)], s).bitcast(F32), ALU.subtract)\
                    .then_inc(S["w_lo_p"], 1)

            for s in range(NPC, 4 * NPC):
                lo_part(s)
            gp.wait_ge(S["g_ready"], 1)

            def gbc(h):
                if h >= 2:
                    wait(gp, "G_mm", h - 1)
                gp.tensor_copy(gb[h % 2], bc(gt[:, :, h:h + 1], [P, NT, P])).then_inc(S["gb_ready"], 1)

            wait(gp, "ktok_copied", NP)
            wait(gp, "kds_ready", 1)
            for c in range(NT):
                gp.tensor_tensor(heads(kdec[:, c, :]), heads(kdec[:, c, :]), per_head(kds, c), ALU.mult)\
                    .then_inc(S["kdec_ready"], 1)
            for s in range(4 * NPC, FIRST_GATE):
                lo_part(s)
            gp.wait_ge(S["ss_done"], 2 * NP)
            gp.wait_ge(S["glu_ready"], CF)
            gbc(0)
            gbc(1)
            gp.wait_ge(S["ld_small"], 64)
            for c in range(NT):
                wait(gp, "zg_silu", c + 1)
                gp.tensor_tensor(heads(zgs[:, c, :]), heads(zgs[:, c, :]),
                                 bc(gng.unsqueeze(1), [P, H, DK]), ALU.mult).then_inc(S["zg_ready"], 1)

            for s in range(FIRST_GATE, FIRST_GATE + 2):
                lo_part(s)

            def masked(h, lv, q, buf):
                return gp.tensor_tensor(buf, MT[:, q, :, :], bc(lmask[:, lv, :].unsqueeze(1), [P, NT, P]), ALU.mult)

            for grp in range(H // GRP):
                for q in range(GRP):
                    h = grp * GRP + q
                    if h + 2 < H:
                        gbc(h + 2)
                    wait(gp, "M_ready", NT * (h + 1))
                    if grp > 0:
                        wait(gp, "X_mm", grp * (LV - 1) * GRP)
                    link(masked(h, 0, q, U[:, h, :, :]))
                    gp.tensor_tensor(U[:, h, :, :], bc(ident.unsqueeze(1), [P, NT, P]), U[:, h, :, :],
                                     ALU.subtract).then_inc(S["U0_ready"], 1)
                for lv in range(1, LV):
                    for q in range(GRP):
                        h = grp * GRP + q
                        wait(gp, "X_mm", (grp * (LV - 1) + lv - 2) * GRP + q + 1 if lv > 1 else grp * (LV - 1) * GRP)
                        masked(h, lv, q, BT[:, q, :, :]).then_inc(S["BT_ready"], 1)

            wait(gp, "st_hlo", 16)
            wait(gp, "X_mm", H * (LV - 1))
            gp.wait_ge(S["BT_ready"], H * (LV - 1))
            gp.dma_start(h_lo.rearrange("p k n -> p (k n)"), low_h).then_inc(S["ld_hlo"], 16)
            for s in range(FIRST_GATE + 2, NWIN * NPC):
                lo_part(s)
            gp.wait_ge(S["u_ready"], CF)
            gp.wait_ge(S["og_ready"], NT)
            gp.wait_ge(S["oT_tr"], NT)
            gp.dma_start(rbias[:, 0:NG], a["b_router_group"][0].partition_broadcast(P)).then_inc(S["ld_rbias"], 16)
            gp.dma_start(rbias[:, NG:NR], a["b_router_expert"][0].partition_broadcast(P)).then_inc(S["ld_rbias"], 16)
            gp.iota(desc, [[0, NT], [-1, NE]], NE, 0, allow_small_or_imprecise_dtypes=True).then_inc(S["rconst"], 1)
            gp.iota(descg, [[0, NT], [-1, NG]], NG, 0, allow_small_or_imprecise_dtypes=True).then_inc(S["rconst"], 1)
            gp.iota(iota_c, [[0, NT], [CAP, NE]], 0, 0, allow_small_or_imprecise_dtypes=True).then_inc(S["rconst"], 1)
            gp.wait_ge(S["idx_ready"], 1)
            gp.wait_ge(S["zeroed"], 16 * (NE * CAP // P))
            for c in range(NT):
                for r in range(2):
                    gp.indirect_dma_start(out=sorted_h, out_offset=bass.IndirectOffsetOnAxis(ap=slot_idx[:, c, r, 0:1], axis=0),
                                          in_=h2[:, c, :], in_offset=None, bounds_check=NE * CAP - 1,
                                          oob_is_err=False).then_inc(S["scattered"], 16)
            syv = sorted_y.rearrange("(g j s) n -> g j s n", j=UN, s=CAP)
            with gp.Fori(0, NE // UN) as g:
                for j in range(UN):
                    e = g * UN + j
                    gp.wait_ge(S["ex_ya"], e + 1)
                    gp.wait_ge(S["ex_yd"], e + 1)
                    gp.dma_start(syv[g, j], ysb[j % 2][0:CAP, :]).then_inc(S[f"st_y{j % 2}"], 16)
            gp.wait_ge(S["st_y0"], 16 * NE // 2)
            gp.wait_ge(S["st_y1"], 16 * NE // 2)
            wait(gp, "ex_d1", NE)
            wait(gp, "ov_over", 1)
            for c in range(NT):
                for r in range(2):
                    gp.indirect_dma_start(out=gath[2 * c + r], out_offset=None, in_=sorted_y,
                                          in_offset=bass.IndirectOffsetOnAxis(ap=slot_idx[:, c, r, 1:2], axis=0),
                                          bounds_check=NE * CAP - 1, oob_is_err=False).then_inc(S[f"ld_y{c}"], 16)

        @block.scalar
        def _(act):
            def copy(dst, src, fam, **kw):
                return tell(act.activation(dst, src, ACT.Copy, **kw), fam)

            for c in range(NT):
                act.wait_ge(S[f"ld_x{c}"], 16)
                act.activation(at(R_QK + c * D, D), xs[:, c, :], ACT.Square,
                               accum_out=sm["ss1"][:, c:c + 1]).then_inc(S["ss"], 1)
            act.wait_ge(S["ss"], NT)
            act.wait_ge(S["eps_ready"], 1)
            act.activation(sm["ss1"], sm["ss1"], ACT.Sqrt, scale=1.0 / D, bias=epsb).then_inc(S["norms"], 1)
            act.wait_ge(S["ld_small"], 64)
            for k in range(KT):
                tell(act.activation(h_hi[:, k, :], ready(act, ("hT", k))[:], ACT.Copy, scale=g1[:, k:k + 1]), "h_hi")

            def hi_part(s):
                wait(act, *arrived[s // NPC])
                if slot_user(s) is not None:
                    wait(act, *jobs[("w", slot_user(s))])
                act.activation(as_raw(w_hi[pslot(s)], s), raw(s), ACT.Copy).then_inc(S["w_hi"], 1)

            act.wait_ge(S["ld_ab"], 16)
            act.activation(ab_hi, wab, ACT.Copy).then_inc(S["h_hi"], 1)
            for s in range(NSL):
                hi_part(s)
            tell(act.activation(abT[0:2 * H, :], ready(act, "abT")[0:2 * H, :], ACT.Copy), "h_hi")


            def softplus():
                act.wait_ge(S["ld_small"], 64)
                act.activation(alog, alog, ACT.Exp).then_inc(S["sp"], 1)
                act.wait_ge(S["y_sp"], 1)
                act.activation(sp_a, y_sp, ACT.Abs).then_inc(S["sp"], 1)
                act.wait_ge(S["sp"], 2)
                act.activation(sp_a, sp_a, ACT.Exp, scale=-1.0).then_inc(S["sp"], 1)
                act.wait_ge(S["sp"], 3)
                act.activation(sp_a, sp_a, ACT.Ln, bias=1.0).then_inc(S["sp"], 1)
                act.activation(beta, absb[:, :, 0:H], ACT.Sigmoid).then_inc(S["beta_ready"], 1)

            def pad_copy(f):
                src = ready(act, ("qkv", f))
                if f >= 3:
                    act.wait_ge(S["tap_done"], f - 2)
                tell(act.activation(pad[f % 3][:, ST - 1:], src[:], ACT.Copy), "pad_ready")
                hi_part(f + NSL)

            def silu_out(f):
                dst = (kT, qT, vT)[f // NP][:, f % NP, :]
                act.wait_ge(S["tap_done"], f + 1)
                tell(act.activation(dst, cacc[f % 3], ACT.Silu), "silu_ready")

            def squares(name, n):
                src = ready(act, name)
                if n >= 2:
                    act.wait_ge(S["ss_done"], n - 1)
                tell(act.activation(sq[n % 2], src.rearrange("p (c h d) -> p c h d", c=NT, h=2), ACT.Square), "sq_ready")
                return src

            for f in range(NP + 1):
                pad_copy(f)
                if f > 0:
                    silu_out(f - 1)
                if f == 1:
                    softplus()
            act.wait_ge(S["gcum_ready"], 2)
            act.wait_ge(S["gdiff"], 1)
            act.activation(eg, gcum, ACT.Exp).then_inc(S["exps"], 1)
            act.activation(kds, kds, ACT.Exp).then_inc(S["exps"], 1)
            act.activation(egl, glast, ACT.Exp).then_inc(S["exps"], 1)
            for f in range(NP + 1, 2 * NP):
                pad_copy(f)
                silu_out(f - 1)
            for p in range(NP):
                src = squares(("ktok", p), p)
                tell(act.activation(kdec[:, :, p * P:(p + 1) * P], src.rearrange("p (c n) -> p c n", c=NT), ACT.Copy),
                     "ktok_copied")
            act.wait_ge(S["ss_done"], NP)
            act.activation(nk, ssk, ACT.Sqrt, bias=epsb).then_inc(S["norms"], 1)
            for f in range(2 * NP, 3 * NP):
                pad_copy(f)
                silu_out(f - 1)
            silu_out(3 * NP - 1)
            for p in range(NP):
                squares(("qtok", p), NP + p)
            act.wait_ge(S["ss_done"], 2 * NP)
            act.activation(nq, ssq, ACT.Sqrt, scale=float(DK), bias=epsb64).then_inc(S["norms"], 1)
            for i in range(CF):
                src = ready(act, ("cb", i))
                if i >= 2:
                    act.wait_ge(S["glu_ready"], i - 1)
                tell(act.activation(sgl[i % 2], src[:], ACT.Sigmoid), "glu_sig")
                for j in range(2):
                    hi_part(3 * NPC + 2 * i + j + NSL)
            act.wait_ge(S["zeroed"], 16 * (NE * CAP // P))
            hi_part(FIRST_GATE)
            hi_part(FIRST_GATE + 1)
            for c in range(NT):
                tell(act.activation(zgs[:, c, :], ready(act, ("zg", c))[:], ACT.Silu), "zg_silu")

            for grp in range(H // GRP):
                hh = range(grp * GRP, (grp + 1) * GRP)
                for h in hh:
                    act.wait_ge(S["diff_ready"], NT * (h + 1))
                    act.activation(dec[h % 2], dec[h % 2], ACT.Exp).then_inc(S["dec_ready"], 1)
                for h in hh:
                    tell(act.activation(Tm[:, h % GRP, :, :], ready(act, ("T0", h)).rearrange("p (c n) -> p c n", c=NT),
                                        ACT.Copy), "T_init")
                for lv in range(1, LV):
                    for h in hh:
                        tell(act.activation(Xm[:, h % GRP, :, :],
                                            ready(act, ("X", h, lv)).rearrange("p (c n) -> p c n", c=NT), ACT.Copy),
                             "X_ready")
                    if lv < LV - 1:
                        for h in hh:
                            tell(act.activation(U[:, h, :, :],
                                                ready(act, ("TT", h, lv)).rearrange("p (c n) -> p c n", c=NT), ACT.Copy),
                                 "U_tr_ready")

            act.wait_ge(S["U_ready"], H)
            act.wait_ge(S["D_mm"], H * (LV - 1))
            gates = [(g, m) for g in range(2) for m in range(KT)]

            def gate(upto):
                while gates and len(gates) > 2 * KT - upto:
                    g, m = gates.pop(0)
                    tell(act.activation(sig[g][:, m, :], ready(act, ("gate", g, m))[:], ACT.Sigmoid), "gate_ready")
                    s = FIRST_GATE + 2 + g * KT + m
                    if s < NWIN * NPC:
                        hi_part(s)

            done = [0]

            def more(n):
                done[0] += n
                gate(done[0])

            for c in range(NT):
                more(2)
                act.wait_ge(S["o_ready"], c + 1)
                act.activation(rbuf, o_t, ACT.Square).then_inc(S["osq"], 1)
                act.wait_ge(S["oss"], c + 1)
                act.activation(ors[:, c, :], oss[:, c, :], ACT.Sqrt, scale=1.0 / DK, bias=epsb).then_inc(S["ors"], 1)
                src = ready(act, ("oT", c))
                tell(act.activation(oTc[c], src.rearrange("p (f n) -> p f n", f=NP), ACT.Copy),
                     "oT_ready")
            more(2)

            for i in range(CF):
                act.wait_ge(S["xc_ready"], i + 1)
                if i >= 2:
                    act.wait_ge(S["var_mm"], i - 1)
                act.activation(lsq[i % 2], acc[:, i, :], ACT.Square).then_inc(S["lsq_ready"], 1)
            tell(act.activation(lnv, ready(act, "var")[:], ACT.Sqrt, bias=epsb), "sd_ready")
            more(2)
            for i in range(CF):
                act.wait_ge(S["xn_ready"], i + 1)
                o = i * (TAPS + 3)
                act.activation(acc[:, i, :], acc[:, i, :], ACT.Silu, scale=par[:, o + TAPS + 1:o + TAPS + 2],
                               bias=par[:, o + TAPS + 2:o + TAPS + 3]).then_inc(S["u_ready"], 1)
            more(2 * KT)
            junk = at(o2, D)
            act.wait_ge(S["yc_mm"], KT)
            act.wait_ge(S["yd_ready"], KT)

            def h2T_copy(c):
                for half in range(2):
                    tell(act.activation(h2T[:, 4 * half:4 * half + 4, c * P:(c + 1) * P],
                                        ready(act, ("h2T", c, half)).rearrange("p (k n) -> p k n", k=4), ACT.Copy),
                         "h2T_ready")

            for c in range(NT):
                act.wait_ge(S["x1_ready"], NH2 * (c + 1))
                if c > 0:
                    act.wait_ge(S["ss"], NT + c)
                act.activation(junk, x1[:, c, :], ACT.Square, accum_out=sm["ss2"][:, c:c + 1]).then_inc(S["ss"], 1)
                act.wait_ge(S["ss"], NT + c + 1)
                act.activation(sm["ss2"][:, c:c + 1], sm["ss2"][:, c:c + 1], ACT.Sqrt, scale=1.0 / D,
                               bias=epsb).then_inc(S["rms2"], 1)
                if c > 0:
                    h2T_copy(c - 1)
            h2T_copy(NT - 1)
            act.wait_ge(S["route_dif"], 1)
            act.activation(dg, dg, ACT.Exp).then_inc(S["route_exp"], 1)
            act.wait_ge(S["route_dif"], 2)
            act.activation(sm["tt"], sm["tt"], ACT.Exp).then_inc(S["route_exp"], 1)

            def ex_act(e, g, j):
                wait(act, "ex_tr", 2 * e + 1)
                wait(act, "ex_u", e - 1)
                act.activation(heT[j % 2][:, 0:KT // 2, :], bank[0][:, 0:4 * CAP].rearrange("p (k n) -> p k n", k=4),
                               ACT.Copy).then_inc(S["heT_a"], 1)

            def ex_silu(e, g, j):
                wait(act, "ex_g", e + 1)
                wait(act, "ex_hid", e - 1)
                act.activation(sil[:, j % 2, :], bank[2 + 2 * (j % 2)][:, 0:JE * CAP], ACT.Silu).then_inc(S["ex_sil"], 1)

            def ex_y(e, g, j):
                wait(act, "ex_d0", e + 1)
                wait(act, f"st_y{j % 2}", 32 * g + 16 * (j // 2))
                act.activation(ysb[j % 2][0:CAP, 0:HALF], bank[6][0:CAP, :], ACT.Copy).then_inc(S["ex_ya"], 1)

            def trip(g, first=False, last=False):
                for j in range(UN):
                    e = g * UN + j
                    ex_silu(e, g, j)
                    if not (last and j == UN - 1):
                        ex_act(e + 1, g if j < UN - 1 else g + 1, (j + 1) % UN)
                    if not (first and j == 0):
                        ex_y(e - 1, g if j else g - 1, (j - 1) % UN)
                if last:
                    ex_y(e, g, UN - 1)

            act.wait_ge(S["idx_ready"], 1)
            ex_act(0, 0, 0)
            trip(0, first=True)
            with act.Fori(1, NE // UN - 1) as g:
                trip(g)
            trip(NE // UN - 1, last=True)

            act.wait_ge(S["flag_ready"], 1)
            fv = act.value_load(flag_i[0:1, 0:1], min_val=0, max_val=2 * T)
            with act.If(fv > 0):
                with act.Fori(0, NE) as e:
                    for m in range(JE):
                        act.wait_ge(S["ov_gu"], 2 * (e * JE + m) + 1)
                        act.wait_ge(S["ov_hid"], e * JE + m + 1)
                        act.activation(osil, bank[0][:], ACT.Silu).then_inc(S["ov_sil"], 1)
            for c in range(NT):
                act.wait_ge(S["x2_ready"], c + 1)
                if c > 0:
                    act.wait_ge(S["ss"], 2 * NT + c)
                act.activation(at(R_UP, D), x1[:, c, :], ACT.Square, accum_out=sm["ss3"][:, c:c + 1]).then_inc(S["ss"], 1)
                act.wait_ge(S["ss"], 2 * NT + c + 1)
                act.activation(sm["r3"][:, c:c + 1], sm["ss3"][:, c:c + 1], ACT.Sqrt, scale=1.0 / D,
                               bias=epsb).then_inc(S["rms3"], 1)

        @block.vector
        def _(v):
            n_chain = [0]

            def link(ins):
                n_chain[0] += 1
                ins.then_inc(S["dve_chain"], 1)
                v.wait_ge(S["dve_chain"], n_chain[0])

            TT, TS, STT = v.tensor_tensor, v.tensor_scalar, v.scalar_tensor_tensor
            link(v.memset(epsb, EPS))
            v.memset(epsb64, EPS * DK).then_inc(S["eps_ready"], 1)
            v.wait_ge(S["norms"], 1)
            link(v.reciprocal(sm["r1"], sm["ss1"]))
            for c in range(NT):
                TS(xs[:, c, :], xs[:, c, :], sm["r1"][:, c:c + 1], None, ALU.mult).then_inc(S["xs_ready"], 1)
            v.wait_ge(S["ld_small"], 64)
            for k in range(KT):
                src = ready(v, ("hT", k))
                v.wait_ge(S["h_hi"], k + 1)
                tell(STT(out=h_lo[:, k, :], in0=src[:], scalar=g1[:, k:k + 1], in1=h_hi[:, k, :].bitcast(F32),
                         op0=ALU.mult, op1=ALU.subtract), "h_lo")
            v.wait_ge(S["h_hi"], KT + 1)
            TT(ab_lo, wab, ab_hi.bitcast(F32), ALU.subtract).then_inc(S["h_lo"], 1)
            for s in range(NPC):
                v.wait_ge(S["w_hi"], s + 1)
                TT(as_raw(w_lo[pslot(s)], s), raw(s), as_raw(w_hi[pslot(s)], s).bitcast(F32), ALU.subtract)\
                    .then_inc(S["w_lo_v"], 1)
            NS = TAPS + 3
            tell(v.tensor_copy(par, ready(v, "par")[:, 0:par.shape[1]]), "setup_ready")
            def conv(f):
                ff = (NP, 0, 2 * NP)[f // NP] + f % NP
                w0 = CF * NS + ff * ST
                v.wait_ge(S["pad_ready"], f + 1)
                if f >= 3:
                    v.wait_ge(S["silu_ready"], f - 2)
                link(TS(cacc[f % 3], pad[f % 3][:, 0:T], par[:, w0:w0 + 1], None, ALU.mult))
                for t in range(1, ST):
                    ins = STT(out=cacc[f % 3], in0=pad[f % 3][:, t:t + T], scalar=par[:, w0 + t:w0 + t + 1],
                              in1=cacc[f % 3], op0=ALU.mult, op1=ALU.add)
                    if t < ST - 1:
                        link(ins)
                    else:
                        tell(ins, "tap_done")

            v.wait_ge(S["consts"], 7)
            v.wait_ge(S["setup_ready"], 1)
            conv(0)
            tell(v.tensor_copy(absb.rearrange("p a b -> p (a b)"), ready(v, "ab")[:, 0:NT * 2 * H]), "setup_ready")
            v.wait_ge(S["setup_ready"], 2)
            v.wait_ge(S["ld_small"], 64)
            tell(TT(y_sp, absb[:, :, H:2 * H], bc(dtb.unsqueeze(1), [P, NT, H]), ALU.add), "y_sp")
            v.wait_ge(S["y_sp"], 1)
            link(TS(sp_b, y_sp, 0.0, None, ALU.max))
            v.wait_ge(S["sp"], 4)
            link(TT(sp_b, sp_b, sp_a, ALU.add))
            v.wait_ge(S["sp"], 1)
            link(TS(sp_b, sp_b, -1.0, None, ALU.mult))
            TT(gt, sp_b, bc(alog.unsqueeze(1), [P, NT, H]), ALU.mult).then_inc(S["g_ready"], 1)

            def sumsq(n, dst, p):
                v.wait_ge(S["sq_ready"], n + 1)
                tell(v.tensor_reduce(dst[:, :, 2 * p:2 * p + 2], sq[n % 2], AX.X, ALU.add), "ss_done")

            for f in range(1, NP):
                conv(f)
            b = ready(v, "gcum")
            tell(v.tensor_copy(gcum.rearrange("p a b -> p (a b)"), b[:, 0:SC]), "gcum_ready")
            tell(v.tensor_copy(glast.rearrange("p a b -> p (a b)"), b[:, SC:2 * SC]), "gcum_ready")
            v.wait_ge(S["gcum_ready"], 2)
            tell(TT(kds, glast, gcum, ALU.subtract), "gdiff")
            for f in range(NP, 2 * NP):
                conv(f)
            for p in range(NP):
                sumsq(p, ssk, p)
            v.wait_ge(S["norms"], 2)
            v.wait_ge(S["exps"], 3)
            v.wait_ge(S["beta_ready"], 1)
            link(v.reciprocal(rk, nk))
            link(TT(brk, beta, rk, ALU.mult))
            TT(brk2, brk, rk, ALU.mult).then_inc(S["brk2"], 1)
            tell(TT(kds, kds, rk, ALU.mult), "kds_ready")
            for r in range(2):
                rs = slice(DK * r, DK * r + DK)
                link(v.tensor_copy(gls[rs, :, :], egl[rs, :, :].rearrange("p c (a r) -> p c r a", r=2)[:, :, r, :]))
            for f in range(2 * NP, 3 * NP):
                conv(f)
            for p in range(NP):
                sumsq(NP + p, ssq, p)
            v.wait_ge(S["norms"], 3)
            link(v.reciprocal(rq, nq))
            v.wait_ge(S["upad_zero"], CF)
            for i in range(CF):
                src = ready(v, ("ca", i))
                v.wait_ge(S["glu_sig"], i + 1)
                tell(TT(upad[:, i, TAPS - 1:], src[:], sgl[i % 2], ALU.mult), "glu_ready")
            for p in range(NP):
                src = ready(v, ("vtok", p))
                tell(TT(vtok[:, :, p * P:(p + 1) * P].rearrange("p c (h d) -> p c h d", h=2),
                        src.rearrange("p (c h d) -> p c h d", c=NT, h=2),
                        bc(nk[:, :, 2 * p:2 * p + 2].unsqueeze(3), [P, NT, 2, DK]), ALU.mult), "vtok_ready")

            taps = [(t, i) for t in range(TAPS) for i in range(CF)]
            n_tap = [0]

            def dw(n):
                for _ in range(n):
                    if not taps:
                        return
                    t, i = taps.pop(0)
                    o = i * NS
                    if t == 0:
                        ins = TS(acc[:, i, :], upad[:, i, 0:T], par[:, o:o + 1], par[:, o + TAPS:o + TAPS + 1], ALU.mult,
                                 ALU.add)
                    else:
                        v.wait_ge(S["dw_step"], n_tap[0] - CF + 1 if t < TAPS - 1 else n_tap[0])
                        ins = STT(out=acc[:, i, :], in0=upad[:, i, t:t + T], scalar=par[:, o + t:o + t + 1],
                                  in1=acc[:, i, :], op0=ALU.mult, op1=ALU.add)
                    if t == TAPS - 1:
                        ins.then_inc(S["dw_done"], 1)
                    else:
                        ins.then_inc(S["dw_step"], 1)
                        n_tap[0] += 1

            for grp in range(H // GRP):
                hh = range(grp * GRP, (grp + 1) * GRP)
                for h in hh:
                    g = ready(v, ("G", h))
                    if h >= 2:
                        v.wait_ge(S["M_ready"], NT * (h - 1))
                        v.wait_ge(S["qk_ready"], NT * (h - 1))
                    for c in range(NT):
                        tell(STT(out=dec[h % 2][:, c, :], in0=g[:, c * P:(c + 1) * P], scalar=gcum[:, c, h:h + 1], in1=negm,
                                 op0=ALU.subtract, op1=ALU.add), "diff_ready")
                    kk = ready(v, ("KK", h))
                    v.wait_ge(S["dec_ready"], h + 1)
                    v.wait_ge(S["brk2"], 1)
                    if grp > 0 and h % GRP == 0:
                        v.wait_ge(S["BT_ready"], (LV - 1) * GRP * grp)
                    if grp == 0 and h == 0:
                        v.wait_ge(S["vtok_tr"], NP)
                    for c in range(NT):
                        tell(STT(out=MT[:, h % GRP, c, :], in0=kk[:, c * P:(c + 1) * P], scalar=brk2[:, c, h:h + 1],
                                 in1=dec[h % 2][:, c, :], op0=ALU.mult, op1=ALU.mult), "M_ready")
                    qk = ready(v, ("QK", h))
                    for c in range(NT):
                        tell(STT(out=qkT[:, h, c, :], in0=qk[:, c * P:(c + 1) * P], scalar=rk[:, c, h:h + 1],
                                 in1=dec[h % 2][:, c, :], op0=ALU.mult, op1=ALU.mult), "qk_ready")
                for lv in range(1, LV):
                    for h in hh:
                        src = ready(v, ("D", h, lv)).rearrange("p (c n) -> p c n", c=NT)
                        if lv < LV - 1:
                            tell(TT(Tm[:, h % GRP, :, :], Tm[:, h % GRP, :, :], src, ALU.subtract), "T_ready")
                        else:
                            tell(TT(U[:, h, :, :], U[:, h, :, :], src, ALU.subtract), "U_ready")
                    dw(11)

            for c in range(NT):
                if c > 0:
                    src = ready(v, ("KS", c))
                    v.wait_ge(S["osq"], c)
                    v.wait_ge(S["oss"], c)
                    tell(TT(heads(rbuf), heads(src), per_head(eg, c), ALU.mult), "st_ready")
                    v.wait_ge(S["st_ready"], 2 * c - 1)
                    TT(rbuf, vtok[:, c, :], rbuf, ALU.subtract).then_inc(S["r_ready"], 1)
                src = ready(v, ("VN", c))
                if c > 0:
                    v.wait_ge(S["OV_mm"], c)
                tell(TT(heads(vn), heads(src), per_head(brk, c), ALU.mult), "vn_ready")
                if c > 0:
                    src = ready(v, ("QS", c))
                    tell(TT(heads(o_t), heads(src), per_head(eg, c), ALU.mult), "st_ready")
                if c < NT - 1:
                    src = ready(v, ("DS", c)).rearrange("p (a n) -> p a n", a=NP)
                    if c > 0:
                        v.wait_ge(S["QS_mm"], c)
                    for r in range(2):
                        rs = slice(DK * r, DK * r + DK)
                        dst = Sst[rs, :, DK * r:DK * r + DK]
                        if c > 0:
                            link(TT(dst, dst, bc(gls[rs, c, :].unsqueeze(2), [DK, NP, DK]), ALU.mult))
                            tell(TT(dst, dst, src[rs, :, DK * r:DK * r + DK], ALU.add), "S_ready")
                        else:
                            v.wait_ge(S["consts"], 7)
                            tell(v.tensor_copy(dst, src[rs, :, DK * r:DK * r + DK]), "S_ready")
                src = ready(v, ("OV", c))
                if c > 0:
                    v.wait_ge(S["st_ready"], 2 * c)
                    tell(TT(o_t, o_t, src[:], ALU.add), "ov_read")
                    v.wait_ge(S["ov_read"], c + 1)
                    ins = TT(heads(o_t), heads(o_t), per_head(rq, c), ALU.mult)
                    ins.then_inc(S["o_ready"], 1)
                else:
                    ins = TT(heads(o_t), heads(src), per_head(rq, c), ALU.mult)
                    tell(ins, "ov_read")
                    v.wait_ge(S["ov_read"], 1)
                    v.engine_nop().then_inc(S["o_ready"], 1)
                v.wait_ge(S["osq"], c + 1)
                v.tensor_reduce(oss[:, c, :], heads(rbuf), AX.X, ALU.add).then_inc(S["oss"], 1)
                v.wait_ge(S["ors"], c + 1)
                link(v.reciprocal(ors[:, c, :], ors[:, c, :]))
                v.wait_ge(S["zg_ready"], c + 1)
                v.wait_ge(S["o_ready"], c + 1)
                if c > 0:
                    v.wait_ge(S["oT_tr"], c)
                link(TT(heads(o_s), heads(o_t), per_head(ors, c), ALU.mult))
                TT(o_s, o_s, zgs[:, c, :], ALU.mult).then_inc(S["og_ready"], 1)

            m = ready(v, "mean")
            for i in range(CF):
                tell(TT(acc[:, i, :], acc[:, i, :], m[:], ALU.subtract), "xc_ready")
            for g in (0,):
                v.wait_ge(S["sd_ready"], 1)
                link(v.reciprocal(lnm, lnv))
                v.wait_ge(S["lsq_ready"], CF)
                for i in range(CF):
                    TT(acc[:, i, :], acc[:, i, :], lnm, ALU.mult).then_inc(S["xn_ready"], 1)
            v.wait_ge(S["gate_ready"], 2 * KT)
            for m_ in range(KT):
                src = ready(v, ("yc", m_))
                tell(TT(yT[:, m_, :], yT[:, m_, :], src[:], ALU.mult), "yc_ready")
            for m_ in range(KT):
                src = ready(v, ("yd", m_))
                tell(TT(sig[1][:, m_, :], sig[1][:, m_, :], src[:], ALU.mult), "yd_ready")
                v.wait_ge(S["yc_ready"], m_ + 1)
                v.wait_ge(S["yd_ready"], m_ + 1)
                TT(yT[:, m_, :], yT[:, m_, :], sig[1][:, m_, :], ALU.add).then_inc(S["y_ready"], 1)
            v.wait_ge(S["ld_part2"], 64)
            v.wait_ge(S["yc_mm"], KT)
            for c in range(NT):
                v.wait_ge(S[f"ld_x{c}"], 32)
                for hf in range(NH2):
                    src = ready(v, ("wo", c, hf))
                    xx = x1[:, c, hf * HALF:(hf + 1) * HALF]
                    tell(TT(xx, xx, src[:], ALU.add), "x1_ready")
                v.wait_ge(S["rms2"], c + 1)
                link(v.reciprocal(sm["r2"][:, c:c + 1], sm["ss2"][:, c:c + 1]))
                v.wait_ge(S["x1_ready"], NH2 * (c + 1))
                STT(out=h2[:, c, :], in0=x1[:, c, :], scalar=sm["r2"][:, c:c + 1], in1=gain2, op0=ALU.mult,
                    op1=ALU.mult).then_inc(S["h2_ready"], 1)

            v.wait_ge(S["ld_rbias"], 32)
            v.wait_ge(S["rconst"], 3)
            src = ready(v, "logits")
            tell(TT(lg, src[:, 0:NT * NR].rearrange("p (c n) -> p c n", c=NT), bc(rbias.unsqueeze(1), [P, NT, NR]),
                    ALU.add), "routed")
            v.wait_ge(S["routed"], 1)

            def col(s, n):
                return bc(sm[s].unsqueeze(2), [P, NT, n])

            def first_max(dst, x, n, dsc, mx):
                link(v.tensor_reduce(sm[mx], x, AX.X, ALU.max))
                link(TT(dst, x, col(mx, n), ALU.is_equal))
                link(TT(dst, dst, dsc, ALU.mult))
                link(v.tensor_reduce(sm["ix"], dst, AX.X, ALU.max))
                link(TT(dst, dst, col("ix", n), ALU.is_equal))

            glog, elog = lg[:, :, 0:NG], lg[:, :, NG:NR]
            first_max(ohg, glog, NG, descg, "gm")
            TT(dg, glog, col("gm", NG), ALU.subtract).then_inc(S["route_dif"], 1)
            link(TS(ohg, ohg, -NEG, NEG, ALU.mult, ALU.add))
            link(TT(le.rearrange("p c (g e) -> p c g e", g=NG), elog.rearrange("p c (g e) -> p c g e", g=NG),
                    bc(ohg.unsqueeze(3), [P, NT, NG, EG]), ALU.add))
            first_max(oh1, le, NE, desc, "m1")
            link(STT(out=rtmp, in0=oh1, scalar=4 * NEG, in1=le, op0=ALU.mult, op1=ALU.add))
            first_max(oh2, rtmp, NE, desc, "m2")
            TT(Mx, oh1, oh2, ALU.add).then_inc(S["M_onehot"], 1)
            TT(sm["tt"], sm["m2"], sm["m1"], ALU.subtract).then_inc(S["route_dif"], 1)
            v.wait_ge(S["route_exp"], 1)
            link(v.tensor_reduce(sm["gs"], dg, AX.X, ALU.add))
            v.wait_ge(S["route_exp"], 2)
            link(TS(sm["gp"], sm["tt"], 1.0, None, ALU.add))
            link(TT(sm["gp"], sm["gp"], sm["gs"], ALU.mult))
            link(v.reciprocal(sm["w1"], sm["gp"]))
            link(TT(sm["w2"], sm["w1"], sm["tt"], ALU.mult))
            src = ready(v, "rank")
            tell(v.tensor_copy(pos.rearrange("p a b -> p (a b)"), src[:, 0:NT * NE]), "routed")
            v.wait_ge(S["routed"], 2)
            v.wait_ge(S["M_onehot"], 1)
            for r, (oh, w) in enumerate(((oh1, "w1"), (oh2, "w2"))):
                pr, sr, vr = f"p{r + 1}", f"s{r + 1}", f"v{r + 1}"
                link(TT(rtmp, oh, pos, ALU.mult))
                link(v.tensor_reduce(sm[pr], rtmp, AX.X, ALU.add))
                link(TT(rtmp, oh, iota_c, ALU.mult))
                link(v.tensor_reduce(sm[sr], rtmp, AX.X, ALU.add))
                link(TS(sm[vr], sm[pr], float(CAP), None, ALU.is_lt))
                link(TT(sm[sr], sm[sr], sm[pr], ALU.add))
                link(TT(rtmp2[:, :, 0], sm[sr], sm[vr], ALU.mult))
                link(v.tensor_copy(slot_idx[:, :, r, 1], rtmp2[:, :, 0]))
                link(TS(rtmp2[:, :, 1], sm[vr], -1.0 * NE * CAP, 1.0 * NE * CAP, ALU.mult, ALU.add))
                link(TT(rtmp2[:, :, 1], rtmp2[:, :, 1], sm[sr], ALU.add))
                link(v.tensor_copy(slot_idx[:, :, r, 0], rtmp2[:, :, 1]))
            v.tensor_copy(ovf[:, 1:2], ones[:, 0:1]).then_inc(S["idx_ready"], 1)
            for r, (oh, w) in enumerate(((oh1, "w1"), (oh2, "w2"))):
                vr = f"v{r + 1}"
                link(TT(sm["mx"], sm[w], sm[vr], ALU.mult))
                link(TT(sm["ix"], sm[w], sm["mx"], ALU.subtract))
                link(v.tensor_copy(sm[w], sm["mx"]))
                if r == 0:
                    link(TT(cov, oh, col("ix", NE), ALU.mult))
                else:
                    link(TT(rtmp, oh, col("ix", NE), ALU.mult))
                    link(TT(cov, cov, rtmp, ALU.add))
            link(TT(sm["mx"], sm["v1"], sm["v2"], ALU.add))
            link(TS(sm["mx"], sm["mx"], -1.0, 2.0, ALU.mult, ALU.add))
            v.tensor_reduce(ovf[:, 0:1], sm["mx"], AX.X, ALU.add).then_inc(S["ovf_ready"], 1)
            tell(v.tensor_copy(flag_i[0:1, 0:1], ready(v, "flag")[0:1, 0:1]), "flag_ready")

            def ex_het(e, g, j):
                wait(v, "ex_tr", 2 * e + 2)
                wait(v, "ex_u", e - 1)
                v.tensor_copy(heT[j % 2][:, KT // 2:, :], bank[1][:, 0:4 * CAP].rearrange("p (k n) -> p k n", k=4))\
                    .then_inc(S["heT_d"], 1)

            def ex_hid(e, g, j):
                wait(v, "ex_u", e + 1)
                wait(v, "ex_sil", e + 1)
                wait(v, "ex_d1", e - 1)
                TT(hid[:, j % 2, :], sil[:, j % 2, :], bank[3 + 2 * (j % 2)][:, 0:JE * CAP], ALU.mult)\
                    .then_inc(S["ex_hid"], 1)

            def ex_y(e, g, j):
                wait(v, "ex_d1", e + 1)
                wait(v, f"st_y{j % 2}", 32 * g + 16 * (j // 2))
                v.tensor_copy(ysb[j % 2][0:CAP, HALF:D], bank[7][0:CAP, :]).then_inc(S["ex_yd"], 1)

            def trip(g, first=False, last=False):
                for j in range(UN):
                    e = g * UN + j
                    ex_hid(e, g, j)
                    if not (last and j == UN - 1):
                        ex_het(e + 1, g if j < UN - 1 else g + 1, (j + 1) % UN)
                    if not (first and j == 0):
                        ex_y(e - 1, g if j else g - 1, (j - 1) % UN)
                if last:
                    ex_y(e, g, UN - 1)

            ex_het(0, 0, 0)
            trip(0, first=True)
            with v.Fori(1, NE // UN - 1) as g:
                trip(g)
            trip(NE // UN - 1, last=True)

            v.wait_ge(S["flag_ready"], 1)
            fv = v.value_load(flag_i[0:1, 0:1], min_val=0, max_val=2 * T)
            with v.If(fv > 0):
                v.wait_ge(S["st_y0"], 16 * NE // 2)
                v.wait_ge(S["st_y1"], 16 * NE // 2)
                v.wait_ge(S["ex_d1"], NE)
                v.engine_nop().then_inc(S["ov_shift"], 1)
                v.engine_nop().then_inc(S["ov_hid"], 1)
                v.engine_nop().then_inc(S["ov_acc"], 1)
                with v.Fori(0, NE) as e:
                    for m in range(JE):
                        v.wait_ge(S["ov_gu"], 2 * (e * JE + m) + 2)
                        v.wait_ge(S["ov_sil"], e * JE + m + 1)
                        TT(ohid[:, m, :], osil, bank[1][:], ALU.mult).then_inc(S["ov_hid"], 1)
                    for c in range(NT):
                        for hf in range(NH2):
                            v.wait_ge(S["ov_d"], e * 2 * NT + c * NH2 + hf + 1)
                            xx = x1[:, c, hf * HALF:(hf + 1) * HALF]
                            ins = STT(out=xx, in0=bank[2][:], scalar=cov[:, c, 0:1], in1=xx, op0=ALU.mult, op1=ALU.add)
                            ins.then_inc(S["ov_acc"], 1)
                    v.tensor_copy(rtmp[:, :, 0:NE - 1], cov[:, :, 1:NE]).then_inc(S["ov_shift"], 1)
                    v.wait_ge(S["ov_shift"], e * 2 + 2)
                    v.tensor_copy(cov[:, :, 0:NE - 1], rtmp[:, :, 0:NE - 1]).then_inc(S["ov_shift"], 1)
                    v.wait_ge(S["ov_shift"], e * 2 + 3)
                v.wait_ge(S["ov_acc"], 2 * NT * NE + 1)
            v.engine_nop().then_inc(S["ov_over"], 1)

            v.wait_ge(S["ld_part2"], 64)
            for c in range(NT):
                v.wait_ge(S[f"ld_y{c}"], 32)
                for r in range(2):
                    ins = STT(out=x1[:, c, :], in0=gath[2 * c + r], scalar=sm[f"w{r + 1}"][:, c:c + 1], in1=x1[:, c, :],
                              op0=ALU.mult, op1=ALU.add)
                    if r == 0:
                        link(ins)
                    else:
                        ins.then_inc(S["x2_ready"], 1)
            for c in range(NT):
                v.wait_ge(S["rms3"], c + 1)
                link(v.reciprocal(sm["gm"][:, c:c + 1], sm["r3"][:, c:c + 1]))
                STT(out=x1[:, c, :], in0=x1[:, c, :], scalar=sm["gm"][:, c:c + 1], in1=gain3, op0=ALU.mult,
                    op1=ALU.mult).then_inc(S["out_ready"], 1)


_INS = ['x', 'norm_mix_gain', 'w_in', 'conv_dw_w', 'conv_dw_b', 'conv_ln_gain', 'conv_ln_bias', 'w_conv_out',
        'gdn_conv_w', 'gdn_a_log', 'gdn_dt_bias', 'gdn_norm_gain', 'w_gdn_out', 'w_out', 'norm_ffn_gain',
        'w_router_group', 'b_router_group', 'w_router_expert', 'b_router_expert', 'w_expert_gate', 'w_expert_up',
        'w_expert_down', 'final_norm_gain']
CAP = 96


def kernel(**inputs):
    import numpy as np
    import concourse.bacc as bacc
    from concourse.bass_utils import run_bass_kernel_spmd

    nc = bacc.Bacc("TRN2", target_bir_lowering=False, num_devices=1)
    arrays, args = {}, {}
    for name in _INS:
        v = np.ascontiguousarray(inputs[name])
        arrays[f"in_{name}_dram"] = v
        args[name] = nc.dram_tensor(f"in_{name}_dram", v.shape, mybir.dt.from_np(v.dtype), kind="ExternalInput").ap()
    shape = inputs["x"].shape
    out = nc.dram_tensor("out_0_dram", shape, F32, kind="ExternalOutput").ap()
    ne = inputs["w_router_expert"].shape[2]
    sorted_h = nc.dram_tensor("sorted_h", (ne * CAP, shape[2]), F32, kind="Internal").ap()
    sorted_y = nc.dram_tensor("sorted_y", (ne * CAP, shape[2]), F32, kind="Internal").ap()
    low_h = nc.dram_tensor("low_h", (P, shape[2] // P * shape[1]), F32, kind="Internal").ap()
    hybrid_layer(nc, args, out, sorted_h, sorted_y, low_h, CAP)
    r = run_bass_kernel_spmd(nc, [arrays], core_ids=[0])
    return r.results[0]["out_0_dram"]
```

```python
from contextlib import ExitStack

import concourse.bass as bass
from concourse import mybir

F32 = mybir.dt.float32
FR = mybir.dt.float32r
I32 = mybir.dt.int32
ACT = mybir.ActivationFunctionType
ALU = mybir.AluOpType
AX = mybir.AxisListType

P = 128
EPS = 1e-6
NEG = -1e30


class Signals:

    def __init__(self, nc, ctx):
        self.nc, self.ctx, self.sems, self.count = nc, ctx, {}, {}

    def __getitem__(self, name):
        if name not in self.sems:
            self.sems[name] = self.ctx.enter_context(self.nc.semaphore(name))
        return self.sems[name]

    def tell(self, ins, name, by=1):
        ins.then_inc(self[name], by)
        self.count[name] = self.count.get(name, 0) + by
        return self.count[name]


def hybrid_layer(nc, a, out, h2_rows, y_rows, low_h, CAP):
    _, T, D = a["x"].shape
    KT = D // P
    NT = T // P
    CW = a["w_conv_out"].shape[1]
    TAPS = a["conv_dw_w"].shape[1]
    CF = CW // P
    H = a["gdn_a_log"].shape[1]
    VD = a["w_gdn_out"].shape[1]
    DK = VD // H
    NP = H // 2
    ST = a["gdn_conv_w"].shape[1]
    NG = a["w_router_group"].shape[2]
    NE = a["w_router_expert"].shape[2]
    EG = NE // NG
    DE = a["w_expert_gate"].shape[3]
    JE = DE // P
    HALF = 512
    NH2 = D // HALF
    WSLOT = KT * HALF
    ESLOT = 3 * KT * DE
    UN = 4
    LV = 7
    GRP = 4
    HP = P // 2
    NR = NG + NE
    NZ = 2 * T // P
    NO_ROW = 4096.0

    C_CONV, C_Q = 0, 2 * CW
    C_K, C_V, C_ZG = C_Q + VD, C_Q + 2 * VD, C_Q + 3 * VD
    C_AB = C_Q + 4 * VD
    C_GC, C_GD = C_AB + 2 * H, C_AB + 2 * H + D

    with ExitStack() as ctx:
        S = Signals(nc, ctx)
        tell = S.tell

        def wait(eng, name, n):
            if not isinstance(n, int) or n > 0:
                eng.wait_ge(S[name], n)

        top = [0]
        ARENA = 52800
        row_idx = ctx.enter_context(nc.sbuf_tensor("row_idx", [P, 2, NE], I32))
        flag_i = ctx.enter_context(nc.sbuf_tensor("flag_i", [1, 1], I32))

        def take(n):
            top[0] += n
            assert top[0] <= ARENA, top[0]
            return top[0] - n

        def at(off, *shape):
            n = 1
            for s in shape:
                n *= s
            v = arena[:, off:off + n]
            if len(shape) == 1:
                return v
            names = "abcd"[:len(shape)]
            return v.rearrange(f"p ({' '.join(names)}) -> p {' '.join(names)}", **dict(zip(names[1:], shape[1:])))

        R_HT = take(KT * T)
        R_RING = take(3 * WSLOT)
        R_SIG = take(2 * KT * T)
        R_EXP = take(0)
        R_QK = take(2 * NP * T)
        R_VTOK = take(NT * VD)
        R_KDEC = take(NT * VD)
        R_QKT = take(H * T)
        R_U = take(H * T)
        R_ZG = take(NT * VD)
        assert top[0] - R_EXP >= 3 * ESLOT
        R_UP = take(CF * (T + TAPS - 1))
        R_ACC = take(CF * T)
        R_TMP = take(4 * T)

        def parts(name, off, *shape):
            n = 1
            for d in shape:
                n *= d
            with ExitStack() as below:
                if off > 0:
                    below.enter_context(nc.sbuf_tensor(f"{name}_below", [P, off], F32))
                v = below.enter_context(nc.sbuf_tensor(name, [P, n], FR))[:, :]
            names = "abcd"[:len(shape)]
            return v.rearrange(f"p ({' '.join(names)}) -> p {' '.join(names)}", **dict(zip(names[1:], shape[1:])))

        h_hi = parts("h_hi", R_HT, KT, T)
        h_lo = parts("h_lo", R_SIG + KT * T, KT, T)
        WP = KT * P
        NSL = 4
        o_parts = [R_RING + 2 * WSLOT, R_RING + 2 * WSLOT + 2 * WP, R_U, R_U + 2 * WP]
        w_hi = [parts(f"w_hi{i}", o, WP) for i, o in enumerate(o_parts)]
        w_lo = [parts(f"w_lo{i}", o + WP, WP) for i, o in enumerate(o_parts)]
        u_hi, u_lo = parts("u_hi", R_KDEC, CF, T), parts("u_lo", R_ACC, CF, T)
        o_hi, o_lo = parts("o_hi", R_UP, NP, T), parts("o_lo", R_VTOK, NT, NP, P)
        BP = CF * P
        b_hi = [parts(f"b_hi{i}", R_ZG + 2 * i * BP, CF, P) for i in range(2)]
        b_lo = [parts(f"b_lo{i}", R_ZG + (2 * i + 1) * BP, CF, P) for i in range(2)]
        ab_hi = parts("ab_hi", R_ZG + D + T, KT, 2 * H)
        ab_lo = parts("ab_lo", R_ZG + D + T + KT * 2 * H, KT, 2 * H)
        arena = ctx.enter_context(nc.sbuf_tensor("arena", [P, ARENA], F32))

        x1 = at(R_HT, NT, D)
        xs = at(R_SIG, NT, D)
        dwstage = at(R_KDEC, CW)
        gcstage = at(R_VTOK, 3 * VD)
        abT = at(R_ZG + D, T)
        vT = at(R_SIG, NP, T)
        Tm = at(R_SIG, GRP, NT, P)
        Xm = at(R_SIG + GRP * T, GRP, NT, P)
        MT = at(R_SIG + 2 * GRP * T, GRP, NT, P)
        BT = at(R_SIG + 3 * GRP * T, GRP, NT, P)
        sig = [at(R_SIG, KT, T), at(R_QKT, KT, T)]
        yT = sig[0]
        kT = at(R_QK, NP, T)
        qT = at(R_QK + NP * T, NP, T)
        vtok = at(R_VTOK, NT, VD)
        kdec = at(R_KDEC, NT, VD)
        qkT = at(R_QKT, H, NT, P)
        NPAD = T + ST - 1
        pad = [at(R_QKT + i * NPAD, NPAD) for i in range(3)]
        cacc = [at(R_QKT + 3 * NPAD + i * T, T) for i in range(3)]
        U = at(R_U, H, NT, P)
        zgs = at(R_ZG, NT, VD)
        upad = at(R_UP, CF, T + TAPS - 1)
        oTc = [at(R_VTOK + c * VD, NP, P) for c in range(NT)]
        oT = vtok.rearrange("p c (f n) -> p f c n", f=NP)
        acc = at(R_ACC, CF, T)
        gb = [at(R_TMP + i * T, NT, P) for i in range(2)]
        dec = [at(R_TMP + (2 + i) * T, NT, P) for i in range(2)]
        sq = [at(R_TMP + i * T, NT, 2, DK) for i in range(2)]
        sgl = [at(R_TMP + (2 + i) * T, T) for i in range(2)]
        rbuf, vn, o_t, o_s = (at(R_TMP + i * T, T) for i in range(4))
        lnm, lnv = at(R_TMP, T), at(R_TMP + T, T)
        lsq = [at(R_TMP + (2 + i) * T, T) for i in range(2)]

        ident = at(take(P), P)
        triu = at(take(P), P)
        triu_s = at(take(P), P)
        negm = at(take(P), P)
        ones = at(take(P), P)
        mean_w = at(take(P), P)
        lmask = at(take(LV * P), LV, P)
        Sst = at(take(NP * P), NP, P)
        par = at(take(CF * (TAPS + 3) + 3 * NP * ST), CF * (TAPS + 3) + 3 * NP * ST)
        g1 = at(take(KT), KT)
        wab = at(take(KT * 2 * H), KT, 2 * H)
        absb = at(take(NT * 2 * H), NT, 2 * H)
        alog = at(take(H), H)
        dtb = at(take(H), H)
        gng = at(take(DK), DK)
        SC = NT * H

        def tok(n=1):
            return at(take(SC), NT, H)

        beta, gt, y_sp, sp_a, sp_b, gcum, glast, eg, egl, kds, nk, nq, rk, rq, brk, brk2 = (tok() for _ in range(16))
        gls = at(take(NT * NP), NT, NP)
        epsb = at(take(1), 1)
        epsb64 = at(take(1), 1)
        ssk = tok()
        ssq = tok()
        oss = at(take(NT * H), NT, H)
        ors = at(take(NT * H), NT, H)
        sm = {n: at(take(NT), NT) for n in ("ss1", "r1", "ss2", "r2", "ss3", "r3", "gm", "gs", "gp", "m1", "m2", "w1",
                                            "w2", "tt", "p1", "p2", "s1", "s2", "v1", "v2", "ix", "mx")}

        eslot = [R_EXP + i * ESLOT for i in (1, 0, 2)] + [R_RING]
        wg = [at(o, KT, DE) for o in eslot]
        wu = [at(o + KT * DE, KT, DE) for o in eslot]
        wd = [at(o + 2 * KT * DE, JE, D) for o in eslot]
        ysb = [at(R_RING + ESLOT + i * D, D) for i in range(2)]
        R_S2 = R_RING + 2 * WSLOT
        gain2 = at(R_S2, D)
        gain3 = at(R_S2 + D, D)
        wr = at(R_S2 + 2 * D, KT, NR)
        NL = 64
        wr_wide = [at(R_S2 + 2 * D + k * NR, NL) for k in range(KT)]
        o2 = R_S2 + 2 * D + KT * NR + NL - NR
        heT = [at(o2 + i * KT * CAP, KT, CAP) for i in range(2)]
        assert o2 + 2 * KT * CAP <= R_RING + 3 * WSLOT
        hs = [at(R_SIG + i * D, D) for i in range(UN)]
        h2T = at(R_SIG + KT * T, KT, T)
        h2 = at(R_UP, NT, D)
        rt = R_TMP
        NRT = NT * NE

        def rte(i):
            return at(rt + i * NRT, NT, NE)

        lg = at(rt + 10 * NRT, NT, NR)
        le, oh1, oh2, pos, Mx, cov, rtmp, desc, rtmp2 = (rte(i) for i in range(9))
        rank_row = at(rt + 9 * NRT, CAP)
        code_c = at(rt + 9 * NRT + CAP, 2, 2, NT)
        assert CAP + 4 * NT <= NRT
        row_of = at(o2, 2, NT, CAP)
        codes = at(o2 + 2 * NT * CAP, 2, NT, 2, NE)
        assert 2 * NT * CAP + 4 * NRT <= 2 * KT * CAP
        ridx = at(R_UP + NT * D, 2, NE)
        assert NT * D + 2 * NE <= CF * (2 * T + TAPS - 1)
        ohg = at(rt + 10 * NRT + NT * NR, NT, NG)
        dg = at(rt + 10 * NRT + NT * NR + NT * NG, NT, NG)
        rbias = at(rt + 10 * NRT + NT * NR + 2 * NT * NG, NR)
        descg = at(rt + 10 * NRT + NT * NR + 2 * NT * NG + NR, NT, NG)
        ovf = at(rt + 10 * NRT + NT * NR + 3 * NT * NG + NR, 2)
        e0 = rt + 10 * NRT + NT * NR + 3 * NT * NG + NR + 2
        sil = at(rt, 2, JE * CAP)
        hid = at(e0, 2, JE * CAP)
        assert e0 + 2 * JE * CAP <= rt + 4 * T and 2 * JE * CAP <= 3 * NRT * 2, (e0 + 2 * JE * CAP - rt)
        osil = at(R_RING + ESLOT, T)
        ohid = at(R_SIG, JE, T)
        zero = at(R_ZG, D)
        gath = [at(R_EXP + 2 * c * D, 2, D) for c in range(NT)]

        bank = [ctx.enter_context(nc.psum_tensor(f"bank{i}", [P, 512], F32))[:, :] for i in range(8)]

        def bc(ap, shape):
            return ap.to_broadcast(shape)

        def heads(v):
            return v.rearrange("p (h d) -> p h d", h=H)

        def per_head(s, c):
            return bc(s[:, c, :].unsqueeze(2), [P, H, DK])

        jobs = {}

        win = a["w_in"][0].rearrange("(p k) n -> p k n", k=KT)
        chunks = [("k", win[:, :, C_K:C_K + VD]), ("q", win[:, :, C_Q:C_Q + VD]), ("v", win[:, :, C_V:C_V + VD]),
                  ("glu0", None), ("glu1", None), ("zg", win[:, :, C_ZG:C_ZG + VD]),
                  ("gc0", win[:, :, C_GC:C_GC + HALF]), ("gc1", win[:, :, C_GC + HALF:C_GC + D]),
                  ("gd0", win[:, :, C_GD:C_GD + HALF]), ("gd1", win[:, :, C_GD + HALF:C_GD + D]),
                  ("wco", a["w_conv_out"][0].rearrange("(f p) n -> p f n", p=P)),
                  ("wgo", a["w_gdn_out"][0].rearrange("(f p) n -> p f n", p=P)),
                  ("wo0", a["w_out"][0].rearrange("(k p) n -> p k n", p=P)[:, :, 0:HALF]),
                  ("wo1", a["w_out"][0].rearrange("(k p) n -> p k n", p=P)[:, :, HALF:D])]
        cidx = {n: i for i, (n, _) in enumerate(chunks)}
        NWIN = cidx["wco"]
        NPC = WSLOT // WP
        place, arrived = {}, {}
        for n in range(NWIN):
            loads = 16 * (n // 2 + 1) + (16 if n >= cidx["glu0"] else 0)
            place[n], arrived[n] = R_RING + (n % 2) * WSLOT, (f"ld_w{n % 2}", loads)
        place[cidx["wco"]], arrived[cidx["wco"]] = R_QK, ("ld_w2", 16)
        place[cidx["wgo"]], arrived[cidx["wgo"]] = R_RING, ("ld_w0", 16 * (NWIN // 2 + 2))
        place[cidx["wo0"]], arrived[cidx["wo0"]] = R_RING + WSLOT, ("ld_w1", 16 * (NWIN // 2 + 2))
        place[cidx["wo1"]], arrived[cidx["wo1"]] = R_U, ("ld_w2", 32)
        FIRST_GATE = cidx["gc0"] * NPC

        def pslot(s):
            return s % NSL if s < FIRST_GATE else s % 2

        def raw(s):
            w = at(place[s // NPC], KT, HALF)
            i = s % NPC
            if s // NPC == cidx["zg"]:
                return w[:, i * KT // NPC:(i + 1) * KT // NPC, :]
            return w[:, :, i * P:(i + 1) * P]

        def as_raw(v, s):
            return v.rearrange("p (k n) -> p k n", n=HALF if s // NPC == cidx["zg"] else P)

        LAST_PIECE = NWIN * NPC - 1

        def branch_raw(i):
            w = at(place[cidx["wco" if i < KT else "wgo"]], CF, D)
            return w[:, :, (i % KT) * P:(i % KT + 1) * P]

        def lo_done(s):
            return ("w_lo_v", s + 1) if s < NPC else ("w_lo_p", s - NPC + 1)

        def slot_user(s):
            if s < NSL:
                return None
            return s - NSL if s < FIRST_GATE else (s - 4 if s < FIRST_GATE + 2 else s - 2)

        block = ctx.enter_context(nc.Block())

        @block.tensor
        def _(pe):
            used = [None] * 8
            nxt = [0]
            held = []

            def begin(name, freed_by, b=None):
                if b is None:
                    while nxt[0] % 8 in held:
                        nxt[0] += 1
                    b = nxt[0] % 8
                    nxt[0] += 1
                if used[b] is not None:
                    wait(pe, *used[b])
                used[b] = freed_by
                jobs[name] = [b, None, None]
                return bank[b]

            def end(ins, name, fam):
                n = tell(ins, fam)
                jobs[name][1:] = [fam, n]

            wait(pe, "consts", 2)
            for k in range(KT):
                b = begin(("hT", k), ("h_lo", k + 1))
                for c in range(NT):
                    if k == 0:
                        wait(pe, "xs_ready", c + 1)
                    ins = pe.transpose(b[:, c * P:(c + 1) * P], xs[:, c, :].rearrange("p (q k) -> p k q", k=KT)[:, k, :],
                                       ident)
                end(ins, ("hT", k), "setup_mm")
            b = begin("par", ("setup_ready", 1))
            wait(pe, "ld_stage", 80)
            NS = TAPS + 3
            for i in range(CF):
                pe.transpose(b[:, i * NS:(i + 1) * NS], dwstage[0:NS, i * P:(i + 1) * P], ident[0:NS, 0:NS])
            for f in range(3 * NP):
                o = CF * NS + f * ST
                ins = pe.transpose(b[:, o:o + ST], gcstage[0:ST, f * P:(f + 1) * P], ident[0:ST, 0:ST])
            end(ins, "par", "setup_mm")

            def split_product(o, w_parts, x_parts, first, last):
                (wh, wl), (xh, xl) = w_parts, x_parts
                pe.matmul(o, wh, xh, start=first, stop=False)
                pe.matmul(o, wh, xl, start=False, stop=False)
                return pe.matmul(o, wl, xh, start=False, stop=last)

            b = begin("abT", ("h_hi", KT + 2))
            wait(pe, "h_lo", KT)
            wait(pe, "h_lo", KT + 1)
            for k in range(KT):
                ins = split_product(b[0:2 * H, :], (ab_hi[:, k, :], ab_lo[:, k, :]), (h_hi[:, k, :], h_lo[:, k, :]),
                                    k == 0, k == KT - 1)
            end(ins, "abT", "setup_mm")

            def proj(chunk, f, name, freed_by, fam):
                b = begin(name, freed_by)
                s = cidx[chunk] * NPC + f
                wait(pe, *lo_done(s))
                wh, wl = (as_raw(w[pslot(s)], s) for w in (w_hi, w_lo))
                for k in range(KT):
                    ins = split_product(b[:], (wh[:, k, :], wl[:, k, :]), (h_hi[:, k, :], h_lo[:, k, :]), k == 0,
                                        k == KT - 1)
                end(ins, name, fam)
                jobs[("w", s)] = (fam, S.count[fam])

            def tok_tr(src, p, name, freed_by, fam):
                b = begin(name, freed_by)
                for c in range(NT):
                    ins = pe.transpose(b[:, c * P:(c + 1) * P], src[:, p, c * P:(c + 1) * P], ident)
                end(ins, name, fam)

            for f in range(NP):
                proj("k", f, ("qkv", f), ("pad_ready", f + 1), "qkv_mm")
                if f == 0:
                    b = begin("ab", ("setup_ready", 2))
                    wait(pe, "h_hi", KT + 2)
                    for c in range(NT):
                        ins = pe.transpose(b[:, c * 2 * H:(c + 1) * 2 * H], abT[0:2 * H, c * P:(c + 1) * P],
                                           ident[0:2 * H, 0:2 * H])
                    end(ins, "ab", "setup_mm")
            b = begin("gcum", ("gcum_ready", 2))
            wait(pe, "g_ready", 1)
            wait(pe, "consts", 7)
            pe.matmul(b[:, 0:SC], triu, gt.rearrange("p a b -> p (a b)"), start=True, stop=True)
            ins = pe.matmul(b[:, SC:2 * SC], ones, gt.rearrange("p a b -> p (a b)"), start=True, stop=True)
            end(ins, "gcum", "setup_mm")
            for f in range(NP):
                proj("q", f, ("qkv", NP + f), ("pad_ready", NP + f + 1), "qkv_mm")
            for p in range(NP):
                wait(pe, "silu_ready", p + 1)
                tok_tr(kT, p, ("ktok", p), ("ktok_copied", p + 1), "tok_tr")
            for f in range(NP):
                proj("v", f, ("qkv", 2 * NP + f), ("pad_ready", 2 * NP + f + 1), "qkv_mm")
            for p in range(NP):
                wait(pe, "silu_ready", NP + p + 1)
                tok_tr(qT, p, ("qtok", p), ("sq_ready", NP + p + 1), "tok_tr")
            for f in range(CF):
                proj("glu0", 2 * f, ("ca", f), ("glu_ready", f + 1), "glu_mm")
                proj("glu0", 2 * f + 1, ("cb", f), ("glu_sig", f + 1), "glu_mm")
            for p in range(NP):
                wait(pe, "silu_ready", 2 * NP + p + 1)
                tok_tr(vT, p, ("vtok", p), ("vtok_ready", p + 1), "vtok_tr")
            zb = []

            def zg_piece(i):
                if i == 0:
                    zb.extend(begin(("zg", c), ("zg_silu", c + 1)) for c in range(NT))
                    held.extend(jobs[("zg", c)][0] for c in range(NT))
                s = cidx["zg"] * NPC + i
                wait(pe, *lo_done(s))
                wh, wl = (as_raw(w[pslot(s)], s) for w in (w_hi, w_lo))
                for c in range(NT):
                    cs = slice(c * P, (c + 1) * P)
                    for kk in range(KT // NPC):
                        k = i * KT // NPC + kk
                        ins = split_product(zb[c][:], (h_hi[:, k, cs], h_lo[:, k, cs]), (wh[:, kk, :], wl[:, kk, :]),
                                            k == 0, k == KT - 1)
                    if i == NPC - 1:
                        end(ins, ("zg", c), "zg_mm")
                if i < NPC - 1:
                    tell(ins, "zg_mm")
                else:
                    held.clear()
                jobs[("w", s)] = ("zg_mm", S.count["zg_mm"])

            def prep(h):
                t, r = h // 2, slice(DK * (h % 2), DK * (h % 2) + DK)
                b = begin(("G", h), ("diff_ready", NT * (h + 1)))
                wait(pe, "gb_ready", h + 1)
                for c in range(NT):
                    ins = pe.matmul(b[:, c * P:(c + 1) * P], gb[h % 2][:, c, :], triu, start=True, stop=True)
                end(ins, ("G", h), "G_mm")
                b = begin(("KK", h), ("M_ready", NT * (h + 1)))
                for c in range(NT):
                    kc = kT[r, t, c * P:(c + 1) * P]
                    ins = pe.matmul(b[:, c * P:(c + 1) * P], kc, kc, start=True, stop=True)
                end(ins, ("KK", h), "gram_mm")
                b = begin(("QK", h), ("qk_ready", NT * (h + 1)))
                for c in range(NT):
                    ins = pe.matmul(b[:, c * P:(c + 1) * P], kT[r, t, c * P:(c + 1) * P], qT[r, t, c * P:(c + 1) * P],
                                    start=True, stop=True)
                end(ins, ("QK", h), "gram_mm")

            for grp in range(H // GRP):
                hh = range(grp * GRP, (grp + 1) * GRP)
                for h in hh:
                    prep(h)
                    if grp == 0:
                        for i in ((0,), (1, 2), (), (3,))[h]:
                            zg_piece(i)
                for h in hh:
                    b = begin(("T0", h), ("T_init", h + 1))
                    wait(pe, "U0_ready", h + 1)
                    for c in range(NT):
                        ins = pe.transpose(b[:, c * P:(c + 1) * P], U[:, h, c, :], ident)
                    end(ins, ("T0", h), "gram_mm")
                for lv in range(1, LV):
                    for h in hh:
                        q = h % GRP
                        n_lv = (grp * (LV - 1) + lv - 1) * GRP + q
                        b = begin(("X", h, lv), ("X_ready", n_lv + 1))
                        wait(pe, "BT_ready", n_lv + 1)
                        if lv == 1:
                            wait(pe, "T_init", h + 1)
                        else:
                            wait(pe, "T_ready", (grp * (LV - 2) + lv - 2) * GRP + q + 1)
                        for c in range(NT):
                            if lv == LV - 1:
                                ins = pe.matmul(b[HP:P, c * P:c * P + HP], BT[0:HP, q, c, HP:P], Tm[0:HP, q, c, 0:HP],
                                                start=True, stop=True)
                            else:
                                ins = pe.matmul(b[:, c * P:(c + 1) * P], BT[:, q, c, :], Tm[:, q, c, :], start=True,
                                                stop=True)
                        end(ins, ("X", h, lv), "X_mm")
                    for h in hh:
                        q = h % GRP
                        n_lv = (grp * (LV - 1) + lv - 1) * GRP + q
                        n_t = (grp * (LV - 2) + lv - 1) * GRP + q
                        last = lv == LV - 1
                        fb = ("U_ready", h + 1) if last else ("T_ready", n_t + 1)
                        b = begin(("D", h, lv), fb)
                        wait(pe, "X_ready", n_lv + 1)
                        if lv > 1:
                            wait(pe, "U_tr_ready", (grp * (LV - 2) + lv - 2) * GRP + q + 1)
                        for c in range(NT):
                            if last:
                                ins = pe.matmul(b[0:HP, c * P + HP:(c + 1) * P], Xm[HP:P, q, c, 0:HP],
                                                U[HP:P, h, c, HP:P], start=True, stop=True)
                            else:
                                ins = pe.matmul(b[:, c * P:(c + 1) * P], U[:, h, c, :], Xm[:, q, c, :], start=True,
                                                stop=True)
                        end(ins, ("D", h, lv), "D_mm")
                    if lv == LV - 1:
                        continue
                    for h in hh:
                        q = h % GRP
                        n_t = (grp * (LV - 2) + lv - 1) * GRP + q
                        b = begin(("TT", h, lv), ("U_tr_ready", n_t + 1))
                        wait(pe, "T_ready", n_t + 1)
                        for c in range(NT):
                            ins = pe.transpose(b[:, c * P:(c + 1) * P], Tm[:, q, c, :], ident)
                        end(ins, ("TT", h, lv), "gram_mm")

            gates = [(g, m) for g in range(2) for m in range(KT)]

            def gate():
                g, m = gates.pop(0)
                if len(gates) == 2 * KT - 1:
                    wait(pe, "ld_hlo", 16)
                proj(f"g{'cd'[g]}{m // NP}", m % NP, ("gate", g, m), ("gate_ready", g * KT + m + 1), "gate_mm")

            def o_tr(c):
                b = begin(("oT", c), ("oT_ready", c + 1))
                wait(pe, "og_ready", c + 1)
                for p in range(NP):
                    ins = pe.transpose(b[:, p * P:(p + 1) * P], o_s[:, p * P:(p + 1) * P], ident)
                end(ins, ("oT", c), "oT_tr")

            for c in range(NT):
                cs = slice(c * P, (c + 1) * P)
                if c > 0:
                    b = begin(("KS", c), ("st_ready", 2 * c - 1))
                    wait(pe, "S_ready", 2 * c)
                    for p in range(NP):
                        ins = pe.matmul(b[:, p * P:(p + 1) * P], kT[:, p, cs], Sst[:, p, :], start=True, stop=True)
                    end(ins, ("KS", c), "scan_mm")
                b = begin(("VN", c), ("vn_ready", c + 1))
                wait(pe, "U_ready", H)
                wait(pe, "vtok_ready", NP)
                wait(pe, "r_ready", c)
                for h in range(H):
                    rr = vtok[:, 0, :] if c == 0 else rbuf
                    ins = pe.matmul(b[:, h * DK:(h + 1) * DK], U[:, h, c, :], rr[:, h * DK:(h + 1) * DK], start=True,
                                    stop=True)
                end(ins, ("VN", c), "scan_mm")
                gate()
                if c > 0:
                    b = begin(("QS", c), ("st_ready", 2 * c))
                    for p in range(NP):
                        ins = pe.matmul(b[:, p * P:(p + 1) * P], qT[:, p, cs], Sst[:, p, :], start=True, stop=True)
                    end(ins, ("QS", c), "QS_mm")
                wait(pe, "vn_ready", c + 1)
                if c < NT - 1:
                    b = begin(("DS", c), ("S_ready", 2 * c + 2))
                    wait(pe, "kdec_ready", c + 1)
                    for p in range(NP):
                        ins = pe.matmul(b[:, p * P:(p + 1) * P], kdec[:, c, p * P:(p + 1) * P], vn[:, p * P:(p + 1) * P],
                                        start=True, stop=True)
                    end(ins, ("DS", c), "scan_mm")
                b = begin(("OV", c), ("ov_read", c + 1))
                wait(pe, "qk_ready", NT * H)
                for h in range(H):
                    ins = pe.matmul(b[:, h * DK:(h + 1) * DK], qkT[:, h, c, :], vn[:, h * DK:(h + 1) * DK], start=True,
                                    stop=True)
                end(ins, ("OV", c), "OV_mm")
                if c > 0:
                    o_tr(c - 1)
                gate()
            b = begin("mean", ("xc_ready", CF))
            wait(pe, "dw_done", CF)
            for i in range(CF):
                ins = pe.matmul(b[:], mean_w, acc[:, i, :], start=(i == 0), stop=(i == CF - 1))
            end(ins, "mean", "scan_mm")
            o_tr(NT - 1)
            gate()
            gate()
            b = begin("var", ("sd_ready", 1))
            for i in range(CF):
                wait(pe, "lsq_ready", i + 1)
                ins = pe.matmul(b[:], mean_w, lsq[i % 2], start=(i == 0), stop=(i == CF - 1))
                tell(ins, "var_mm")
            jobs["var"][1:] = ["var_mm", CF]
            while gates:
                gate()

            n = cidx["wco"]
            wait(pe, *arrived[n])
            wait(pe, "br_lo", CF)
            for m in range(KT):
                b = begin(("yc", m), ("yc_ready", m + 1))
                wait(pe, "b_lo", m + 1)
                for f in range(CF):
                    ins = split_product(b[:], (b_hi[m % 2][:, f, :], b_lo[m % 2][:, f, :]),
                                        (u_hi[:, f, :], u_lo[:, f, :]), f == 0, f == CF - 1)
                end(ins, ("yc", m), "yc_mm")
            n = cidx["wgo"]
            wait(pe, *arrived[n])
            wait(pe, "br_lo", CF + 1)
            for m in range(KT):
                b = begin(("yd", m), ("yd_ready", m + 1))
                wait(pe, "b_lo", KT + m + 1)
                for f in range(NP):
                    ins = split_product(b[:], (b_hi[m % 2][:, f, :], b_lo[m % 2][:, f, :]),
                                        (o_hi[:, f, :], o_lo[:, :, f, :]), f == 0, f == NP - 1)
                end(ins, ("yd", m), "yd_mm")
            def h2_tile(c):
                for half in range(2):
                    b = begin(("h2T", c, half), ("h2T_ready", 2 * c + half + 1))
                    wait(pe, "h2_ready", c + 1)
                    for k in range(4):
                        ins = pe.transpose(b[:, k * P:(k + 1) * P],
                                           h2[:, c, :].rearrange("p (q k) -> p k q", k=KT)[:, 4 * half + k, :], ident)
                    end(ins, ("h2T", c, half), "route_mm")

            def logits_tile(c):
                if c == 0:
                    begin("logits", ("routed", 1))
                    held.append(jobs["logits"][0])
                    wait(pe, "ld_part2", 64)
                    wait(pe, "rconst", 1)
                b = bank[jobs["logits"][0]]
                wait(pe, "h2T_ready", 2 * c + 2)
                for k in range(KT):
                    ins = pe.matmul(b[:, c * NL:(c + 1) * NL], h2T[:, k, c * P:(c + 1) * P], wr_wide[k],
                                    start=(k == 0), stop=(k == KT - 1))
                end(ins, "logits", "route_mm")

            for c in range(NT):
                for hf in range(NH2):
                    n = cidx[f"wo{hf}"]
                    if c == 0:
                        wait(pe, *arrived[n])
                    b = begin(("wo", c, hf), ("x1_ready", c * NH2 + hf + 1))
                    for m in range(KT):
                        if hf == 0 and c == 0:
                            wait(pe, "y_ready", m + 1)
                        ins = pe.matmul(b[:], yT[:, m, c * P:(c + 1) * P], at(place[n], KT, HALF)[:, m, :], start=(m == 0),
                                        stop=(m == KT - 1))
                    end(ins, ("wo", c, hf), "wo_mm")
                if c > 0:
                    h2_tile(c - 1)
                if c > 1:
                    logits_tile(c - 2)

            h2_tile(NT - 1)
            logits_tile(NT - 2)
            logits_tile(NT - 1)
            held.clear()
            b = begin("rank", ("routed", 2))
            wait(pe, "M_onehot", 1)
            hot = Mx.rearrange("p c n -> p (c n)")
            pe.matmul(b[:, 0:NT * NE], triu_s, hot, start=True, stop=False)
            for d in range(1, NT):
                ins = pe.matmul(b[:, d * NE:NT * NE], ones, hot[:, 0:(NT - d) * NE], start=False, stop=(d == NT - 1))
            end(ins, "rank", "route_mm")
            b = begin("rows", ("idx_ready", 1))
            wait(pe, "M_onehot", 2)
            for i in range(2 * NT):
                ins = pe.matmul(b[0:CAP, 0:2 * NE], row_of[:, i // NT, i % NT, :],
                                codes[:, i // NT, i % NT, :, :].rearrange("p a b -> p (a b)"), start=(i == 0),
                                stop=(i == 2 * NT - 1))
            end(ins, "rows", "route_mm")
            b = begin("flag", ("flag_ready", 1))
            wait(pe, "ovf_ready", 1)
            ins = pe.matmul(b[0:1, 0:1], ones[:, 0:1], ovf[:, 0:1], start=True, stop=True)
            end(ins, "flag", "route_mm")
            for b in range(8):
                wait(pe, *used[b])

            def ex_tr(e, g, j):
                wait(pe, f"ld_h{j}", 16 * (g + 1))
                wait(pe, "heT_a", e)
                wait(pe, "heT_d", e)
                for k in range(KT):
                    o = bank[k // 4][:, (k % 4) * CAP:(k % 4 + 1) * CAP]
                    ins = pe.transpose(o, hs[j][0:CAP, :].rearrange("p (q k) -> p k q", k=KT)[:, k, :],
                                       ident[0:CAP, 0:CAP])
                    if k % 4 == 3:
                        ins.then_inc(S["ex_tr"], 1)

            def ex_gu(e, g, j):
                wait(pe, f"ld_e{j}", 48 * (g + 1))
                wait(pe, "heT_a", e + 1)
                wait(pe, "heT_d", e + 1)
                wait(pe, "ex_sil", e - 1)
                wait(pe, "ex_hid", e - 1)
                for w, bk in ((wg, 2 + 2 * (j % 2)), (wu, 3 + 2 * (j % 2))):
                    for m in range(JE):
                        for k in range(KT):
                            ins = pe.matmul(bank[bk][:, m * CAP:(m + 1) * CAP], w[j][:, k, m * P:(m + 1) * P],
                                            heT[j % 2][:, k, :], start=(k == 0), stop=(k == KT - 1))
                    ins.then_inc(S["ex_g" if w is wg else "ex_u"], 1)

            def ex_dn(e, g, j):
                wait(pe, "ex_hid", e + 1)
                wait(pe, "ex_ya", e)
                wait(pe, "ex_yd", e)
                for hf in range(NH2):
                    for m in range(JE):
                        ins = pe.matmul(bank[6 + hf][0:CAP, :], hid[:, j % 2, m * CAP:(m + 1) * CAP],
                                        wd[j][:, m, hf * HALF:(hf + 1) * HALF], start=(m == 0), stop=(m == JE - 1))
                    ins.then_inc(S["ex_d0" if hf == 0 else "ex_d1"], 1)

            def trip(g, first=False, last=False):
                for j in range(UN):
                    e = g * UN + j
                    ex_gu(e, g, j)
                    if not (last and j == UN - 1):
                        ex_tr(e + 1, g if j < UN - 1 else g + 1, (j + 1) % UN)
                    if not (first and j == 0):
                        ex_dn(e - 1, g if j else g - 1, (j - 1) % UN)
                if last:
                    ex_dn(e, g, UN - 1)

            NTRIP = NE // UN
            ex_tr(0, 0, 0)
            trip(0, first=True)
            with pe.Fori(1, NTRIP - 1) as g:
                trip(g)
            trip(NTRIP - 1, last=True)

            wait(pe, "flag_ready", 1)
            wait(pe, "ex_ya", NE)
            wait(pe, "ex_yd", NE)
            fv = pe.value_load(flag_i[0:1, 0:1], min_val=0, max_val=2 * T)
            with pe.If(fv > 0):
                with pe.Fori(0, NE) as e:
                    wait(pe, "ov_ld", 48 * e + 48)
                    for m in range(JE):
                        pe.wait_ge(S["ov_hid"], e * JE + m + 1)
                        for w, bk in ((wg, 0), (wu, 1)):
                            for k in range(KT):
                                ins = pe.matmul(bank[bk][:], w[0][:, k, m * P:(m + 1) * P], h2T[:, k, :],
                                                start=(k == 0), stop=(k == KT - 1))
                            ins.then_inc(S["ov_gu"], 1)
                    for c in range(NT):
                        for hf in range(NH2):
                            if c == 0 and hf == 0:
                                pe.wait_ge(S["ov_hid"], e * JE + JE + 1)
                            pe.wait_ge(S["ov_acc"], e * 2 * NT + c * NH2 + hf + 1)
                            for m in range(JE):
                                ins = pe.matmul(bank[2][:], ohid[:, m, c * P:(c + 1) * P],
                                                wd[0][:, m, hf * HALF:(hf + 1) * HALF], start=(m == 0),
                                                stop=(m == JE - 1))
                            ins.then_inc(S["ov_d"], 1)

        def ready(eng, name):
            b, fam, n = jobs[name]
            wait(eng, fam, n)
            return bank[b]

        @block.sync
        def _(sp):
            xv = a["x"][0].rearrange("(c p) d -> c p d", p=P)
            for c in range(NT):
                sp.dma_start(xs[:, c, :], xv[c]).then_inc(S[f"ld_x{c}"], 16)
            sp.dma_start(g1, a["norm_mix_gain"][0].rearrange("(p k) -> p k", k=KT)).then_inc(S["ld_small"], 16)
            for dst, name in ((alog, "gdn_a_log"), (dtb, "gdn_dt_bias"), (gng, "gdn_norm_gain")):
                sp.dma_start(dst, a[name][0].partition_broadcast(P)).then_inc(S["ld_small"], 16)
            sp.dma_start(dwstage[0:TAPS, :], a["conv_dw_w"][0]).then_inc(S["ld_stage"], 16)
            for i, n in enumerate(("conv_dw_b", "conv_ln_gain", "conv_ln_bias")):
                sp.dma_start(dwstage[TAPS + i:TAPS + i + 1, :], a[n]).then_inc(S["ld_stage"], 16)
            sp.dma_start(gcstage[0:ST, :], a["gdn_conv_w"][0]).then_inc(S["ld_stage"], 16)
            sp.dma_start(wab, win[:, :, C_AB:C_AB + 2 * H]).then_inc(S["ld_ab"], 16)

            def load(n):
                src = chunks[n][1]
                if src is None:
                    w = at(place[n], KT, 2, 2, P)
                    for side in range(2):
                        o = C_CONV + side * CW + (n - cidx["glu0"]) * 2 * P
                        sp.dma_start(w[:, :, :, side, :], win[:, :, o:o + 2 * P].rearrange("p k (f n) -> p k f n", n=P))\
                            .then_inc(S[arrived[n][0]], 16)
                    return
                sp.dma_start(at(place[n], src.shape[1], src.shape[2]), src).then_inc(S[arrived[n][0]], 16)

            load(0)
            load(1)
            zeros = list(range(NZ))
            wait(sp, "consts", 7)
            for n in range(2, NWIN):
                if n == 4:
                    wait(sp, "h_lo", KT)
                    sp.dma_start(low_h, h_lo.rearrange("p k n -> p (k n)").bitcast(F32)).then_inc(S["st_hlo"], 16)
                for i in zeros[:3]:
                    sp.dma_start(y_rows[i * P:(i + 1) * P, :], zero).then_inc(S["zeroed"], 16)
                zeros = zeros[3:]
                wait(sp, *lo_done((n - 1) * NPC - 1))
                load(n)
            wait(sp, *jobs[("QS", NT - 1)][1:])
            load(cidx["wco"])
            wait(sp, *lo_done((cidx["gd0"] + 1) * NPC - 1))
            load(cidx["wgo"])
            wait(sp, *lo_done((cidx["gd1"] + 1) * NPC - 1))
            load(cidx["wo0"])
            wait(sp, *arrived[cidx["wco"]])
            load(cidx["wo1"])
            wait(sp, "gate_mm", 2 * KT)
            for c in range(NT):
                sp.dma_start(x1[:, c, :], xv[c]).then_inc(S[f"ld_x{c}"], 16)
            wgd = a["w_expert_gate"][0].rearrange("(g j) (p k) n -> g j p k n", j=UN, k=KT)
            wud = a["w_expert_up"][0].rearrange("(g j) (p k) n -> g j p k n", j=UN, k=KT)
            wdd = a["w_expert_down"][0].rearrange("(g j) (m p) n -> g j p m n", j=UN, p=P)

            def expert(g, j):
                sp.dma_start(wg[j], wgd[g, j]).then_inc(S[f"ld_e{j}"], 16)
                sp.dma_start(wu[j], wud[g, j]).then_inc(S[f"ld_e{j}"], 16)
                sp.dma_start(wd[j], wdd[g, j]).then_inc(S[f"ld_e{j}"], 16)

            sp.dma_start(gain2, a["norm_ffn_gain"][0].partition_broadcast(P)).then_inc(S["ld_part2"], 16)
            sp.dma_start(gain3, a["final_norm_gain"].partition_broadcast(P)).then_inc(S["ld_part2"], 16)
            sp.dma_start(wr[:, :, 0:NG], a["w_router_group"][0].rearrange("(p k) n -> p k n", k=KT)).then_inc(S["ld_part2"], 16)
            sp.dma_start(wr[:, :, NG:NR], a["w_router_expert"][0].rearrange("(p k) n -> p k n", k=KT)).then_inc(S["ld_part2"], 16)
            wait(sp, "y_ready", KT)
            expert(0, 0)
            expert(0, 1)
            for c in range(NT):
                wait(sp, "h2_ready", c + 1)
                sp.dma_start(h2_rows[c * P:(c + 1) * P, :], h2[:, c, :]).then_inc(S["st_h2"], 16)
            wait(sp, "wo_mm", 2 * NT)
            expert(0, 2)
            expert(0, 3)
            with sp.Fori(1, NE // UN) as g:
                for j in range(UN):
                    e = g * UN + j
                    sp.wait_ge(S["ex_d1"], e - UN + 1)
                    expert(g, j)

            wait(sp, "flag_ready", 1)
            fv = sp.value_load(flag_i[0:1, 0:1], min_val=0, max_val=2 * T)
            with sp.If(fv > 0):
                wait(sp, "ex_d1", NE)
                with sp.Fori(0, NE) as e:
                    sp.wait_ge(S["ov_shift"], 2 * e + 1)
                    sp.dma_start(wg[0], a["w_expert_gate"][0].rearrange("e (p k) n -> e p k n", k=KT)[e]).then_inc(S["ov_ld"], 16)
                    sp.dma_start(wu[0], a["w_expert_up"][0].rearrange("e (p k) n -> e p k n", k=KT)[e]).then_inc(S["ov_ld"], 16)
                    sp.dma_start(wd[0], a["w_expert_down"][0].rearrange("e (m p) n -> e p m n", p=P)[e]).then_inc(S["ov_ld"], 16)
            wait(sp, "st_y0", 16 * NE // 2)
            wait(sp, "st_y1", 16 * NE // 2)
            wait(sp, "ex_d1", NE)
            wait(sp, "ov_over", 1)
            for c in range(NT):
                sp.dma_start(gath[c], y_rows.rearrange("(r c p) d -> c p r d", r=2, p=P)[c]).then_inc(S[f"ld_x{c}"], 16)
            ov = out[0].rearrange("(c p) d -> c p d", p=P)
            for c in range(NT):
                wait(sp, "out_ready", c + 1)
                sp.dma_start(ov[c], x1[:, c, :]).then_inc(S["st_out"], 16)
            wait(sp, "st_out", 16 * NT)

        @block.gpsimd
        def _(gp):
            n_chain = [0]

            def link(ins):
                n_chain[0] += 1
                ins.then_inc(S["pool_chain"], 1)
                gp.wait_ge(S["pool_chain"], n_chain[0])

            link(gp.memset(ones, 1.0))
            gp.memset(mean_w, 1.0 / CW).then_inc(S["consts"], 1)

            def sel(dst, src, pattern, base, cm, op=ALU.is_ge, fill=0.0):
                return gp.affine_select(out=dst, in_=src, compare_op=op, fill=fill, base=base, pattern=pattern,
                                        channel_multiplier=cm)

            sel(ident, ones, [[1, P]], 0, -1, ALU.is_equal).then_inc(S["consts"], 1)
            sel(triu, ones, [[1, P]], 0, -1).then_inc(S["consts"], 1)
            sel(triu_s, ones, [[1, P]], -1, -1).then_inc(S["consts"], 1)
            link(gp.memset(negm, 0.0))
            sel(negm, negm, [[1, P]], 0, -1, fill=NEG).then_inc(S["consts"], 1)
            for lv in range(LV):
                s = 2 ** lv
                if 2 * s == P:
                    link(gp.tensor_copy(lmask[:, lv, :], ones))
                    continue
                s2 = 2 * s
                v = lmask[:, lv, :].rearrange("p (b s) -> p b s", s=s2)
                link(sel(v, ones.rearrange("p (b s) -> p b s", s=s2), [[-s2, P // s2], [0, s2]], 0, 1))
                link(sel(v, v, [[s2, P // s2], [0, s2]], s2 - 1, -1))
            gp.wait_ge(S["consts"], 5)
            for lv in range(LV - 1, 0, -1):
                link(gp.tensor_tensor(lmask[:, lv, :], lmask[:, lv, :], lmask[:, lv - 1, :], ALU.subtract))
            link(gp.tensor_tensor(lmask[:, 0, :], lmask[:, 0, :], ident, ALU.subtract))
            for lv in range(LV):
                link(gp.tensor_tensor(lmask[:, lv, :], lmask[:, lv, :], triu_s, ALU.mult))
            gp.memset(Sst, 0.0).then_inc(S["consts"], 1)
            for i in range(3):
                link(gp.memset(pad[i][:, 0:ST - 1], 0.0))
            gp.memset(zero, 0.0).then_inc(S["consts"], 1)
            for i in range(CF):
                gp.memset(upad[:, i, 0:TAPS - 1], 0.0).then_inc(S["upad_zero"], 1)

            def lo_part(s):
                gp.wait_ge(S["w_hi"], s + 1)
                gp.tensor_tensor(as_raw(w_lo[pslot(s)], s), raw(s), as_raw(w_hi[pslot(s)], s).bitcast(F32), ALU.subtract)\
                    .then_inc(S["w_lo_p"], 1)

            for s in range(NPC, 4 * NPC):
                lo_part(s)
            wait(gp, "ktok_copied", NP)
            wait(gp, "kds_ready", 2)
            for c in range(NT):
                gp.tensor_tensor(heads(kdec[:, c, :]), heads(kdec[:, c, :]), per_head(kds, c), ALU.mult)\
                    .then_inc(S["kdec_ready"], 1)
            for s in range(4 * NPC, FIRST_GATE):
                lo_part(s)
            def masked(h, lv, q, buf):
                return gp.tensor_tensor(buf, MT[:, q, :, :], bc(lmask[:, lv, :].unsqueeze(1), [P, NT, P]), ALU.mult)

            for grp in range(H // GRP):
                for q in range(GRP):
                    h = grp * GRP + q
                    wait(gp, "M_ready", NT * (h + 1))
                    wait(gp, "zg_mm", NPC - 1)
                    masked(h, 0, q, U[:, h, :, :]).then_inc(S["U0_mask"], 1)
                if grp == 0:
                    wait(gp, "zg_mm", NPC - 1 + NT)
                for lv in range(1, LV):
                    for q in range(GRP):
                        h = grp * GRP + q
                        wait(gp, "X_mm", (grp * (LV - 1) + lv - 2) * GRP + q + 1 if lv > 1 else grp * (LV - 1) * GRP)
                        masked(h, lv, q, BT[:, q, :, :]).then_inc(S["BT_ready"], 1)
                    if grp == 0 and lv == 1:
                        for s in range(FIRST_GATE, FIRST_GATE + 2):
                            lo_part(s)
                    if grp == 0 and lv == 2:
                        gp.wait_ge(S["ld_small"], 64)
                        for c in range(NT):
                            wait(gp, "zg_silu", c + 1)
                            gp.tensor_tensor(heads(zgs[:, c, :]), heads(zgs[:, c, :]),
                                             bc(gng.unsqueeze(1), [P, H, DK]), ALU.mult).then_inc(S["zg_ready"], 1)

            wait(gp, "st_hlo", 16)
            wait(gp, "X_mm", H * (LV - 1))
            gp.wait_ge(S["BT_ready"], H * (LV - 1))
            gp.dma_start(h_lo.rearrange("p k n -> p (k n)"), low_h).then_inc(S["ld_hlo"], 16)
            for s in range(FIRST_GATE + 2, LAST_PIECE):
                lo_part(s)
            for i in range(CF):
                gp.wait_ge(S["br_hi"], i + 1)
                gp.tensor_tensor(u_lo[:, i, :], acc[:, i, :], u_hi[:, i, :].bitcast(F32), ALU.subtract)\
                    .then_inc(S["br_lo"], 1)
                if i == 1:
                    lo_part(LAST_PIECE)
            gp.wait_ge(S["br_hi"], CF + 1)
            gp.tensor_tensor(o_lo, vtok.rearrange("p c (f n) -> p c f n", f=NP),
                             o_hi.bitcast(F32).rearrange("p f (c n) -> p c f n", c=NT), ALU.subtract).then_inc(S["br_lo"], 1)
            for i in range(2 * KT):
                gp.wait_ge(S["b_hi"], i + 1)
                gp.tensor_tensor(b_lo[i % 2], branch_raw(i), b_hi[i % 2].bitcast(F32), ALU.subtract)\
                    .then_inc(S["b_lo"], 1)
            gp.wait_ge(S["u_ready"], CF)
            gp.wait_ge(S["og_ready"], NT)
            wait(gp, "gate_mm", 2 * KT)
            gp.wait_ge(S["oT_tr"], NT)
            gp.dma_start(rbias[:, 0:NG], a["b_router_group"][0].partition_broadcast(P)).then_inc(S["ld_rbias"], 16)
            gp.dma_start(rbias[:, NG:NR], a["b_router_expert"][0].partition_broadcast(P)).then_inc(S["ld_rbias"], 16)
            gp.memset(at(o2 - (NL - NR), NL - NR), 0.0).then_inc(S["rconst"], 1)
            gp.iota(desc, [[0, NT], [-1, NE]], NE, 0, allow_small_or_imprecise_dtypes=True).then_inc(S["rconst"], 1)
            gp.iota(descg, [[0, NT], [-1, NG]], NG, 0, allow_small_or_imprecise_dtypes=True).then_inc(S["rconst"], 1)
            gp.iota(rank_row, [[1, CAP]], 0, 0, allow_small_or_imprecise_dtypes=True).then_inc(S["rconst"], 1)
            gp.iota(code_c[:, 0, :, :], [[0, 2], [P, NT]], 1, 1, allow_small_or_imprecise_dtypes=True)\
                .then_inc(S["rconst"], 1)
            gp.iota(code_c[:, 1, :, :], [[T, 2], [P, NT]], 1, 1, allow_small_or_imprecise_dtypes=True)\
                .then_inc(S["rconst"], 1)

            gp.wait_ge(S["idx_ready"], 1)
            gp.wait_ge(S["st_h2"], 16 * NT)
            gp.wait_ge(S["zeroed"], 16 * NZ)

            def gather(e):
                if e >= UN:
                    wait(gp, "ex_tr", 2 * (e - UN) + 2)
                gp.indirect_dma_start(out=hs[e % UN][0:CAP, :], out_offset=None, in_=h2_rows,
                                      in_offset=bass.IndirectOffsetOnAxis(ap=row_idx[0:CAP, 0, e:e + 1], axis=0),
                                      bounds_check=T - 1, oob_is_err=False).then_inc(S[f"ld_h{e % UN}"], 16)

            def scatter(e):
                gp.wait_ge(S["ex_ya"], e + 1)
                gp.wait_ge(S["ex_yd"], e + 1)
                gp.indirect_dma_start(out=y_rows, in_=ysb[e % 2][0:CAP, :], in_offset=None,
                                      out_offset=bass.IndirectOffsetOnAxis(ap=row_idx[0:CAP, 1, e:e + 1], axis=0),
                                      bounds_check=2 * T - 1, oob_is_err=False).then_inc(S[f"st_y{e % 2}"], 16)

            for e in range(UN - 1):
                gather(e)
            for e in range(NE):
                if e + UN - 1 < NE:
                    gather(e + UN - 1)
                scatter(e)

        @block.scalar
        def _(act):
            def copy(dst, src, fam, **kw):
                return tell(act.activation(dst, src, ACT.Copy, **kw), fam)

            for c in range(NT):
                act.wait_ge(S[f"ld_x{c}"], 16)
                act.activation(at(R_QK + c * D, D), xs[:, c, :], ACT.Square,
                               accum_out=sm["ss1"][:, c:c + 1]).then_inc(S["ss"], 1)
                act.wait_ge(S["ss"], c + 1)
                if c == 0:
                    act.wait_ge(S["eps_ready"], 1)
                act.activation(sm["ss1"][:, c:c + 1], sm["ss1"][:, c:c + 1], ACT.Sqrt, scale=1.0 / D,
                               bias=epsb).then_inc(S["norms"], 1)
            act.wait_ge(S["ld_small"], 64)
            for k in range(KT):
                tell(act.activation(h_hi[:, k, :], ready(act, ("hT", k))[:], ACT.Copy, scale=g1[:, k:k + 1]), "h_hi")

            def hi_part(s):
                wait(act, *arrived[s // NPC])
                if slot_user(s) is not None:
                    wait(act, *jobs[("w", slot_user(s))])
                act.activation(as_raw(w_hi[pslot(s)], s), raw(s), ACT.Copy).then_inc(S["w_hi"], 1)

            act.wait_ge(S["ld_ab"], 16)
            act.activation(ab_hi, wab, ACT.Copy).then_inc(S["h_hi"], 1)
            for s in range(NSL):
                hi_part(s)
            tell(act.activation(abT[0:2 * H, :], ready(act, "abT")[0:2 * H, :], ACT.Copy), "h_hi")


            def softplus():
                act.wait_ge(S["ld_small"], 64)
                act.activation(alog, alog, ACT.Exp).then_inc(S["sp"], 1)
                act.wait_ge(S["y_sp"], 1)
                act.activation(sp_a, y_sp, ACT.Abs).then_inc(S["sp"], 1)
                act.wait_ge(S["sp"], 2)
                act.activation(sp_a, sp_a, ACT.Exp, scale=-1.0).then_inc(S["sp"], 1)
                act.wait_ge(S["sp"], 3)
                act.activation(sp_a, sp_a, ACT.Ln, bias=1.0).then_inc(S["sp"], 1)
                act.activation(beta, absb[:, :, 0:H], ACT.Sigmoid).then_inc(S["beta_ready"], 1)

            def pad_copy(f):
                src = ready(act, ("qkv", f))
                if f >= 3:
                    act.wait_ge(S["tap_done"], f - 2)
                tell(act.activation(pad[f % 3][:, ST - 1:], src[:], ACT.Copy), "pad_ready")
                hi_part(f + NSL)

            def silu_out(f):
                dst = (kT, qT, vT)[f // NP][:, f % NP, :]
                act.wait_ge(S["tap_done"], f + 1)
                tell(act.activation(dst, cacc[f % 3], ACT.Silu), "silu_ready")

            def squares(name, n):
                src = ready(act, name)
                if n >= 2:
                    act.wait_ge(S["ss_done"], n - 1)
                tell(act.activation(sq[n % 2], src.rearrange("p (c h d) -> p c h d", c=NT, h=2), ACT.Square), "sq_ready")
                return src

            for f in range(NP + 1):
                pad_copy(f)
                if f > 0:
                    silu_out(f - 1)
                if f == 1:
                    softplus()
            act.wait_ge(S["gcum_ready"], 3)
            act.activation(eg, gcum, ACT.Exp).then_inc(S["exps"], 1)
            act.activation(kds, kds, ACT.Exp).then_inc(S["exps"], 1)
            act.activation(egl, glast, ACT.Exp).then_inc(S["exps"], 1)
            for f in range(NP + 1, 2 * NP):
                pad_copy(f)
                silu_out(f - 1)
            for p in range(NP):
                src = squares(("ktok", p), p)
                tell(act.activation(kdec[:, :, p * P:(p + 1) * P], src.rearrange("p (c n) -> p c n", c=NT), ACT.Copy),
                     "ktok_copied")
            act.wait_ge(S["ss_done"], NP)
            act.activation(nk, ssk, ACT.Sqrt, bias=epsb).then_inc(S["norms"], 1)
            for f in range(2 * NP, 3 * NP):
                pad_copy(f)
                silu_out(f - 1)
            silu_out(3 * NP - 1)
            for p in range(NP):
                squares(("qtok", p), NP + p)
            act.wait_ge(S["ss_done"], 2 * NP)
            act.activation(nq, ssq, ACT.Sqrt, scale=float(DK), bias=epsb64).then_inc(S["norms"], 1)
            for i in range(CF):
                src = ready(act, ("cb", i))
                if i >= 2:
                    act.wait_ge(S["glu_ready"], i - 1)
                tell(act.activation(sgl[i % 2], src[:], ACT.Sigmoid), "glu_sig")
                for j in range(2):
                    hi_part(3 * NPC + 2 * i + j + NSL)
            def gbc(h):
                if h >= 2:
                    wait(act, "G_mm", h - 1)
                act.activation(gb[h % 2], bc(gt[:, :, h:h + 1], [P, NT, P]), ACT.Copy).then_inc(S["gb_ready"], 1)

            act.wait_ge(S["ss_done"], 2 * NP)
            act.wait_ge(S["glu_ready"], CF)
            act.wait_ge(S["g_ready"], 1)
            gbc(0)
            gbc(1)
            for grp in range(H // GRP):
                hh = range(grp * GRP, (grp + 1) * GRP)
                for h in hh:
                    act.wait_ge(S["diff_ready"], NT * (h + 1))
                    act.activation(dec[h % 2], dec[h % 2], ACT.Exp).then_inc(S["dec_ready"], 1)
                    if h + 2 < H:
                        gbc(h + 2)
                if grp == 0:
                    hi_part(FIRST_GATE)
                    hi_part(FIRST_GATE + 1)
                    act.wait_ge(S["zeroed"], 16 * NZ)
                    for c in range(NT):
                        tell(act.activation(zgs[:, c, :], ready(act, ("zg", c))[:], ACT.Silu), "zg_silu")
                for h in hh:
                    tell(act.activation(Tm[:, h % GRP, :, :], ready(act, ("T0", h)).rearrange("p (c n) -> p c n", c=NT),
                                        ACT.Copy), "T_init")
                for lv in range(1, LV):
                    for h in hh:
                        rows, cols = (slice(0, P), slice(0, P)) if lv < LV - 1 else (slice(HP, P), slice(0, HP))
                        src = ready(act, ("X", h, lv)).rearrange("p (c n) -> p c n", c=NT)
                        tell(act.activation(Xm[rows, h % GRP, :, cols], src[rows, :, cols], ACT.Copy), "X_ready")
                    if lv < LV - 1:
                        for h in hh:
                            tell(act.activation(U[:, h, :, :],
                                                ready(act, ("TT", h, lv)).rearrange("p (c n) -> p c n", c=NT), ACT.Copy),
                                 "U_tr_ready")

            act.wait_ge(S["U_ready"], H)
            act.wait_ge(S["D_mm"], H * (LV - 1))
            gates = [(g, m) for g in range(2) for m in range(KT)]

            def gate(upto):
                while gates and len(gates) > 2 * KT - upto:
                    g, m = gates.pop(0)
                    tell(act.activation(sig[g][:, m, :], ready(act, ("gate", g, m))[:], ACT.Sigmoid), "gate_ready")
                    s = FIRST_GATE + 2 + g * KT + m
                    if s < LAST_PIECE:
                        hi_part(s)

            done = [0]

            def more(n):
                done[0] += n
                gate(done[0])

            def oT_copy(c):
                tell(act.activation(oTc[c], ready(act, ("oT", c)).rearrange("p (f n) -> p f n", f=NP), ACT.Copy),
                     "oT_ready")

            for c in range(NT):
                more(1)
                act.wait_ge(S["o_ready"], c + 1)
                if c > 0:
                    act.wait_ge(S["oT_tr"], c)
                act.activation(o_s, o_t, ACT.Square).then_inc(S["osq"], 1)
                act.wait_ge(S["oss"], c + 1)
                act.activation(ors[:, c, :], oss[:, c, :], ACT.Sqrt, scale=1.0 / DK, bias=epsb).then_inc(S["ors"], 1)
                if c > 0:
                    oT_copy(c - 1)
                more(1)
            oT_copy(NT - 1)
            more(2)

            for i in range(CF):
                act.wait_ge(S["xc_ready"], i + 1)
                if i >= 2:
                    act.wait_ge(S["var_mm"], i - 1)
                act.activation(lsq[i % 2], acc[:, i, :], ACT.Square).then_inc(S["lsq_ready"], 1)
            tell(act.activation(lnv, ready(act, "var")[:], ACT.Sqrt, bias=epsb), "sd_ready")
            more(3)
            for i in range(CF):
                act.wait_ge(S["xn_ready"], i + 1)
                o = i * (TAPS + 3)
                act.activation(acc[:, i, :], acc[:, i, :], ACT.Silu, scale=par[:, o + TAPS + 1:o + TAPS + 2],
                               bias=par[:, o + TAPS + 2:o + TAPS + 3]).then_inc(S["u_ready"], 1)
                act.wait_ge(S["u_ready"], i + 1)
                act.activation(u_hi[:, i, :], acc[:, i, :], ACT.Copy).then_inc(S["br_hi"], 1)
                if i == 1:
                    hi_part(LAST_PIECE)
            act.wait_ge(S["oT_ready"], NT)
            act.activation(o_hi.rearrange("p f (c n) -> p f c n", c=NT), oT, ACT.Copy).then_inc(S["br_hi"], 1)

            def branch_hi(i):
                wait(act, *arrived[cidx["wco" if i < KT else "wgo"]])
                if i >= 2:
                    wait(act, "yc_mm" if i - 2 < KT else "yd_mm", (i - 2) % KT + 1)
                act.activation(b_hi[i % 2], branch_raw(i), ACT.Copy).then_inc(S["b_hi"], 1)

            more(1)
            branch_hi(0)
            branch_hi(1)
            more(2 * KT)
            for i in range(2, 2 * KT):
                branch_hi(i)
            junk = at(o2, D)
            act.wait_ge(S["yc_mm"], KT)
            act.wait_ge(S["yd_ready"], KT)

            def h2T_copy(c):
                for half in range(2):
                    tell(act.activation(h2T[:, 4 * half:4 * half + 4, c * P:(c + 1) * P],
                                        ready(act, ("h2T", c, half)).rearrange("p (k n) -> p k n", k=4), ACT.Copy),
                         "h2T_ready")

            for c in range(NT):
                act.wait_ge(S["x1_ready"], NH2 * (c + 1))
                if c > 0:
                    act.wait_ge(S["ss"], NT + c)
                act.activation(junk, x1[:, c, :], ACT.Square, accum_out=sm["ss2"][:, c:c + 1]).then_inc(S["ss"], 1)
                act.wait_ge(S["ss"], NT + c + 1)
                act.activation(sm["ss2"][:, c:c + 1], sm["ss2"][:, c:c + 1], ACT.Sqrt, scale=1.0 / D,
                               bias=epsb).then_inc(S["rms2"], 1)
                if c > 0:
                    h2T_copy(c - 1)
            h2T_copy(NT - 1)
            act.wait_ge(S["route_dif"], 1)
            act.activation(dg, dg, ACT.Exp).then_inc(S["route_exp"], 1)
            act.wait_ge(S["route_dif"], 2)
            act.activation(sm["tt"], sm["tt"], ACT.Exp).then_inc(S["route_exp"], 1)

            def ex_act(e, g, j):
                wait(act, "ex_tr", 2 * e + 1)
                wait(act, "ex_u", e - 1)
                act.activation(heT[j % 2][:, 0:KT // 2, :], bank[0][:, 0:4 * CAP].rearrange("p (k n) -> p k n", k=4),
                               ACT.Copy).then_inc(S["heT_a"], 1)

            def ex_silu(e, g, j):
                wait(act, "ex_g", e + 1)
                wait(act, "ex_hid", e - 1)
                act.activation(sil[:, j % 2, :], bank[2 + 2 * (j % 2)][:, 0:JE * CAP], ACT.Silu).then_inc(S["ex_sil"], 1)

            def ex_y(e, g, j):
                wait(act, "ex_d0", e + 1)
                wait(act, f"st_y{j % 2}", 32 * g + 16 * (j // 2))
                act.activation(ysb[j % 2][0:CAP, 0:HALF], bank[6][0:CAP, :], ACT.Copy).then_inc(S["ex_ya"], 1)

            def trip(g, first=False, last=False):
                for j in range(UN):
                    e = g * UN + j
                    ex_silu(e, g, j)
                    if not (last and j == UN - 1):
                        ex_act(e + 1, g if j < UN - 1 else g + 1, (j + 1) % UN)
                    if not (first and j == 0):
                        ex_y(e - 1, g if j else g - 1, (j - 1) % UN)
                if last:
                    ex_y(e, g, UN - 1)

            act.wait_ge(S["idx_ready"], 1)
            ex_act(0, 0, 0)
            trip(0, first=True)
            with act.Fori(1, NE // UN - 1) as g:
                trip(g)
            trip(NE // UN - 1, last=True)

            act.wait_ge(S["flag_ready"], 1)
            fv = act.value_load(flag_i[0:1, 0:1], min_val=0, max_val=2 * T)
            with act.If(fv > 0):
                with act.Fori(0, NE) as e:
                    for m in range(JE):
                        act.wait_ge(S["ov_gu"], 2 * (e * JE + m) + 1)
                        act.wait_ge(S["ov_hid"], e * JE + m + 1)
                        act.activation(osil, bank[0][:], ACT.Silu).then_inc(S["ov_sil"], 1)
            for c in range(NT):
                act.wait_ge(S["x2_ready"], c + 1)
                if c > 0:
                    act.wait_ge(S["ss"], 2 * NT + c)
                act.activation(at(R_UP, D), x1[:, c, :], ACT.Square, accum_out=sm["ss3"][:, c:c + 1]).then_inc(S["ss"], 1)
                act.wait_ge(S["ss"], 2 * NT + c + 1)
                act.activation(sm["r3"][:, c:c + 1], sm["ss3"][:, c:c + 1], ACT.Sqrt, scale=1.0 / D,
                               bias=epsb).then_inc(S["rms3"], 1)

        @block.vector
        def _(v):
            n_chain = [0]

            def link(ins):
                n_chain[0] += 1
                ins.then_inc(S["dve_chain"], 1)
                v.wait_ge(S["dve_chain"], n_chain[0])

            TT, TS, STT = v.tensor_tensor, v.tensor_scalar, v.scalar_tensor_tensor
            link(v.memset(epsb, EPS))
            v.memset(epsb64, EPS * DK).then_inc(S["eps_ready"], 1)
            for c in range(NT):
                v.wait_ge(S["norms"], c + 1)
                link(v.reciprocal(sm["r1"][:, c:c + 1], sm["ss1"][:, c:c + 1]))
                TS(xs[:, c, :], xs[:, c, :], sm["r1"][:, c:c + 1], None, ALU.mult).then_inc(S["xs_ready"], 1)
            v.wait_ge(S["ld_small"], 64)
            for k in range(KT):
                src = ready(v, ("hT", k))
                v.wait_ge(S["h_hi"], k + 1)
                tell(STT(out=h_lo[:, k, :], in0=src[:], scalar=g1[:, k:k + 1], in1=h_hi[:, k, :].bitcast(F32),
                         op0=ALU.mult, op1=ALU.subtract), "h_lo")
            v.wait_ge(S["h_hi"], KT + 1)
            TT(ab_lo, wab, ab_hi.bitcast(F32), ALU.subtract).then_inc(S["h_lo"], 1)
            for s in range(NPC):
                v.wait_ge(S["w_hi"], s + 1)
                TT(as_raw(w_lo[pslot(s)], s), raw(s), as_raw(w_hi[pslot(s)], s).bitcast(F32), ALU.subtract)\
                    .then_inc(S["w_lo_v"], 1)
            NS = TAPS + 3
            tell(v.tensor_copy(par, ready(v, "par")[:, 0:par.shape[1]]), "setup_ready")
            def conv(f):
                ff = (NP, 0, 2 * NP)[f // NP] + f % NP
                w0 = CF * NS + ff * ST
                v.wait_ge(S["pad_ready"], f + 1)
                if f >= 3:
                    v.wait_ge(S["silu_ready"], f - 2)
                link(TS(cacc[f % 3], pad[f % 3][:, 0:T], par[:, w0:w0 + 1], None, ALU.mult))
                for t in range(1, ST):
                    ins = STT(out=cacc[f % 3], in0=pad[f % 3][:, t:t + T], scalar=par[:, w0 + t:w0 + t + 1],
                              in1=cacc[f % 3], op0=ALU.mult, op1=ALU.add)
                    if t < ST - 1:
                        link(ins)
                    else:
                        tell(ins, "tap_done")

            v.wait_ge(S["consts"], 7)
            v.wait_ge(S["setup_ready"], 1)
            conv(0)
            tell(v.tensor_copy(absb.rearrange("p a b -> p (a b)"), ready(v, "ab")[:, 0:NT * 2 * H]), "setup_ready")
            v.wait_ge(S["setup_ready"], 2)
            v.wait_ge(S["ld_small"], 64)
            tell(TT(y_sp, absb[:, :, H:2 * H], bc(dtb.unsqueeze(1), [P, NT, H]), ALU.add), "y_sp")
            v.wait_ge(S["y_sp"], 1)
            link(TS(sp_b, y_sp, 0.0, None, ALU.max))
            v.wait_ge(S["sp"], 4)
            link(TT(sp_b, sp_b, sp_a, ALU.add))
            v.wait_ge(S["sp"], 1)
            link(TS(sp_b, sp_b, -1.0, None, ALU.mult))
            TT(gt, sp_b, bc(alog.unsqueeze(1), [P, NT, H]), ALU.mult).then_inc(S["g_ready"], 1)

            def sumsq(n, dst, p):
                v.wait_ge(S["sq_ready"], n + 1)
                tell(v.tensor_reduce(dst[:, :, 2 * p:2 * p + 2], sq[n % 2], AX.X, ALU.add), "ss_done")

            for f in range(1, NP):
                conv(f)
            b = ready(v, "gcum")
            tell(v.tensor_copy(gcum.rearrange("p a b -> p (a b)"), b[:, 0:SC]), "gcum_ready")
            tell(v.tensor_copy(glast.rearrange("p a b -> p (a b)"), b[:, SC:2 * SC]), "gcum_ready")
            v.wait_ge(S["gcum_ready"], 2)
            tell(TT(kds, glast, gcum, ALU.subtract), "gcum_ready")
            for f in range(NP, 2 * NP):
                conv(f)
            for p in range(NP):
                sumsq(p, ssk, p)
            v.wait_ge(S["norms"], NT + 1)
            v.wait_ge(S["exps"], 3)
            v.wait_ge(S["beta_ready"], 1)
            link(v.reciprocal(rk, nk))
            link(TT(brk, beta, rk, ALU.mult))
            tell(TT(brk2, brk, rk, ALU.mult), "kds_ready")
            tell(TT(kds, kds, rk, ALU.mult), "kds_ready")
            for r in range(2):
                rs = slice(DK * r, DK * r + DK)
                link(v.tensor_copy(gls[rs, :, :], egl[rs, :, :].rearrange("p c (a r) -> p c r a", r=2)[:, :, r, :]))
            for f in range(2 * NP, 3 * NP):
                conv(f)
            for p in range(NP):
                sumsq(NP + p, ssq, p)
            v.wait_ge(S["norms"], NT + 2)
            link(v.reciprocal(rq, nq))
            v.wait_ge(S["upad_zero"], CF)
            for i in range(CF):
                src = ready(v, ("ca", i))
                v.wait_ge(S["glu_sig"], i + 1)
                tell(TT(upad[:, i, TAPS - 1:], src[:], sgl[i % 2], ALU.mult), "glu_ready")
            for p in range(NP):
                src = ready(v, ("vtok", p))
                tell(TT(vtok[:, :, p * P:(p + 1) * P].rearrange("p c (h d) -> p c h d", h=2),
                        src.rearrange("p (c h d) -> p c h d", c=NT, h=2),
                        bc(nk[:, :, 2 * p:2 * p + 2].unsqueeze(3), [P, NT, 2, DK]), ALU.mult), "vtok_ready")

            taps = [(t, i) for t in range(TAPS) for i in range(CF)]
            n_tap = [0]

            def dw(n):
                for _ in range(n):
                    if not taps:
                        return
                    t, i = taps.pop(0)
                    o = i * NS
                    if t == 0:
                        ins = TS(acc[:, i, :], upad[:, i, 0:T], par[:, o:o + 1], par[:, o + TAPS:o + TAPS + 1], ALU.mult,
                                 ALU.add)
                    else:
                        v.wait_ge(S["dw_step"], n_tap[0] - CF + 1 if t < TAPS - 1 else n_tap[0])
                        ins = STT(out=acc[:, i, :], in0=upad[:, i, t:t + T], scalar=par[:, o + t:o + t + 1],
                                  in1=acc[:, i, :], op0=ALU.mult, op1=ALU.add)
                    if t == TAPS - 1:
                        ins.then_inc(S["dw_done"], 1)
                    else:
                        ins.then_inc(S["dw_step"], 1)
                        n_tap[0] += 1

            def first_inverse(h):
                v.wait_ge(S["U0_mask"], h + 1)
                TT(U[:, h, :, :], bc(ident.unsqueeze(1), [P, NT, P]), U[:, h, :, :], ALU.subtract)\
                    .then_inc(S["U0_ready"], 1)

            for grp in range(H // GRP):
                hh = range(grp * GRP, (grp + 1) * GRP)
                for h in hh:
                    g = ready(v, ("G", h))
                    if h >= 2:
                        v.wait_ge(S["M_ready"], NT * (h - 1))
                        v.wait_ge(S["qk_ready"], NT * (h - 1))
                    for c in range(NT):
                        tell(STT(out=dec[h % 2][:, c, :], in0=g[:, c * P:(c + 1) * P], scalar=gcum[:, c, h:h + 1], in1=negm,
                                 op0=ALU.subtract, op1=ALU.add), "diff_ready")
                    kk = ready(v, ("KK", h))
                    v.wait_ge(S["dec_ready"], h + 1)
                    v.wait_ge(S["kds_ready"], 2)
                    if grp > 0 and h % GRP == 0:
                        v.wait_ge(S["BT_ready"], (LV - 1) * GRP * grp)
                    if grp == 0:
                        if h == 0:
                            v.wait_ge(S["vtok_tr"], NP)
                            v.wait_ge(S["st_hlo"], 16)
                        v.wait_ge(S["zg_mm"], h // 2 + 1)
                    for c in range(NT):
                        tell(STT(out=MT[:, h % GRP, c, :], in0=kk[:, c * P:(c + 1) * P], scalar=brk2[:, c, h:h + 1],
                                 in1=dec[h % 2][:, c, :], op0=ALU.mult, op1=ALU.mult), "M_ready")
                    qk = ready(v, ("QK", h))
                    for c in range(NT):
                        tell(STT(out=qkT[:, h, c, :], in0=qk[:, c * P:(c + 1) * P], scalar=rk[:, c, h:h + 1],
                                 in1=dec[h % 2][:, c, :], op0=ALU.mult, op1=ALU.mult), "qk_ready")
                    if h % GRP > 0:
                        first_inverse(h - 1)
                    if grp == 0:
                        dw(5)
                first_inverse(grp * GRP + GRP - 1)
                for lv in range(1, LV):
                    for h in hh:
                        src = ready(v, ("D", h, lv)).rearrange("p (c n) -> p c n", c=NT)
                        if lv < LV - 1:
                            tell(TT(Tm[:, h % GRP, :, :], Tm[:, h % GRP, :, :], src, ALU.subtract), "T_ready")
                        else:
                            u = U[0:HP, h, :, HP:P]
                            tell(TT(u, u, src[0:HP, :, HP:P], ALU.subtract), "U_ready")
                    dw(9 if lv < LV - 1 else 2)

            def output(c):
                v.wait_ge(S["ors"], c + 1)
                link(v.reciprocal(ors[:, c, :], ors[:, c, :]))
                v.wait_ge(S["zg_ready"], c + 1)
                v.wait_ge(S["o_ready"], c + 1)
                v.wait_ge(S["oss"], c + 1)
                link(TT(heads(o_s), heads(o_t), per_head(ors, c), ALU.mult))
                TT(o_s, o_s, zgs[:, c, :], ALU.mult).then_inc(S["og_ready"], 1)

            for c in range(NT):
                if c > 0:
                    src = ready(v, ("KS", c))
                    tell(TT(heads(rbuf), heads(src), per_head(eg, c), ALU.mult), "st_ready")
                    v.wait_ge(S["st_ready"], 2 * c - 1)
                    TT(rbuf, vtok[:, c, :], rbuf, ALU.subtract).then_inc(S["r_ready"], 1)
                src = ready(v, ("VN", c))
                if c > 0:
                    v.wait_ge(S["OV_mm"], c)
                tell(TT(heads(vn), heads(src), per_head(brk, c), ALU.mult), "vn_ready")
                if c > 0:
                    output(c - 1)
                if c > 0:
                    src = ready(v, ("QS", c))
                    tell(TT(heads(o_t), heads(src), per_head(eg, c), ALU.mult), "st_ready")
                if c < NT - 1:
                    src = ready(v, ("DS", c)).rearrange("p (a n) -> p a n", a=NP)
                    if c > 0:
                        v.wait_ge(S["QS_mm"], c)
                    for r in range(2):
                        rs = slice(DK * r, DK * r + DK)
                        dst = Sst[rs, :, DK * r:DK * r + DK]
                        if c > 0:
                            link(TT(dst, dst, bc(gls[rs, c, :].unsqueeze(2), [DK, NP, DK]), ALU.mult))
                            tell(TT(dst, dst, src[rs, :, DK * r:DK * r + DK], ALU.add), "S_ready")
                        else:
                            v.wait_ge(S["consts"], 7)
                            tell(v.tensor_copy(dst, src[rs, :, DK * r:DK * r + DK]), "S_ready")
                src = ready(v, ("OV", c))
                if c > 0:
                    v.wait_ge(S["st_ready"], 2 * c)
                    tell(TT(o_t, o_t, src[:], ALU.add), "ov_read")
                    v.wait_ge(S["ov_read"], c + 1)
                    ins = TT(heads(o_t), heads(o_t), per_head(rq, c), ALU.mult)
                    ins.then_inc(S["o_ready"], 1)
                else:
                    ins = TT(heads(o_t), heads(src), per_head(rq, c), ALU.mult)
                    tell(ins, "ov_read")
                    v.wait_ge(S["ov_read"], 1)
                    v.engine_nop().then_inc(S["o_ready"], 1)
                dw(4 if c < NT - 1 else len(taps))
                v.wait_ge(S["osq"], c + 1)
                v.tensor_reduce(oss[:, c, :], heads(o_s), AX.X, ALU.add).then_inc(S["oss"], 1)
            output(NT - 1)

            m = ready(v, "mean")
            for i in range(CF):
                tell(TT(acc[:, i, :], acc[:, i, :], m[:], ALU.subtract), "xc_ready")
            v.wait_ge(S["sd_ready"], 1)
            link(v.reciprocal(lnm, lnv))
            v.wait_ge(S["lsq_ready"], CF)
            for i in range(CF):
                TT(acc[:, i, :], acc[:, i, :], lnm, ALU.mult).then_inc(S["xn_ready"], 1)
            v.wait_ge(S["gate_ready"], 2 * KT)
            for m_ in range(KT):
                src = ready(v, ("yc", m_))
                tell(TT(yT[:, m_, :], yT[:, m_, :], src[:], ALU.mult), "yc_ready")
            for m_ in range(KT):
                src = ready(v, ("yd", m_))
                tell(TT(sig[1][:, m_, :], sig[1][:, m_, :], src[:], ALU.mult), "yd_ready")
                v.wait_ge(S["yc_ready"], m_ + 1)
                v.wait_ge(S["yd_ready"], m_ + 1)
                TT(yT[:, m_, :], yT[:, m_, :], sig[1][:, m_, :], ALU.add).then_inc(S["y_ready"], 1)
            v.wait_ge(S["ld_part2"], 64)
            v.wait_ge(S["yc_mm"], KT)
            for c in range(NT):
                v.wait_ge(S[f"ld_x{c}"], 32)
                for hf in range(NH2):
                    src = ready(v, ("wo", c, hf))
                    xx = x1[:, c, hf * HALF:(hf + 1) * HALF]
                    tell(TT(xx, xx, src[:], ALU.add), "x1_ready")
                v.wait_ge(S["rms2"], c + 1)
                link(v.reciprocal(sm["r2"][:, c:c + 1], sm["ss2"][:, c:c + 1]))
                v.wait_ge(S["x1_ready"], NH2 * (c + 1))
                STT(out=h2[:, c, :], in0=x1[:, c, :], scalar=sm["r2"][:, c:c + 1], in1=gain2, op0=ALU.mult,
                    op1=ALU.mult).then_inc(S["h2_ready"], 1)

            v.wait_ge(S["ld_rbias"], 32)
            v.wait_ge(S["rconst"], 6)
            src = ready(v, "logits")
            tell(TT(lg, src[:, 0:NT * NL].rearrange("p (c n) -> p c n", c=NT)[:, :, 0:NR], bc(rbias.unsqueeze(1), [P, NT, NR]),
                    ALU.add), "routed")
            v.wait_ge(S["routed"], 1)

            def col(s, n):
                return bc(sm[s].unsqueeze(2), [P, NT, n])

            def first_max(dst, x, n, dsc, mx):
                link(v.tensor_reduce(sm[mx], x, AX.X, ALU.max))
                link(TT(dst, x, col(mx, n), ALU.is_equal))
                link(TT(dst, dst, dsc, ALU.mult))
                link(v.tensor_reduce(sm["ix"], dst, AX.X, ALU.max))
                link(TT(dst, dst, col("ix", n), ALU.is_equal))

            glog, elog = lg[:, :, 0:NG], lg[:, :, NG:NR]
            first_max(ohg, glog, NG, descg, "gm")
            TT(dg, glog, col("gm", NG), ALU.subtract).then_inc(S["route_dif"], 1)
            link(TS(ohg, ohg, -NEG, NEG, ALU.mult, ALU.add))
            link(TT(le.rearrange("p c (g e) -> p c g e", g=NG), elog.rearrange("p c (g e) -> p c g e", g=NG),
                    bc(ohg.unsqueeze(3), [P, NT, NG, EG]), ALU.add))
            first_max(oh1, le, NE, desc, "m1")
            link(STT(out=rtmp, in0=oh1, scalar=4 * NEG, in1=le, op0=ALU.mult, op1=ALU.add))
            first_max(oh2, rtmp, NE, desc, "m2")
            TT(Mx, oh1, oh2, ALU.add).then_inc(S["M_onehot"], 1)
            for r, oh in enumerate((oh1, oh2)):
                for q in range(2):
                    TT(codes[:, r, :, q, :], oh, bc(code_c[:, q, r, :].unsqueeze(2), [P, NT, NE]), ALU.mult)\
                        .then_inc(S["codes"], 1)
            TT(sm["tt"], sm["m2"], sm["m1"], ALU.subtract).then_inc(S["route_dif"], 1)
            v.wait_ge(S["route_exp"], 1)
            link(v.tensor_reduce(sm["gs"], dg, AX.X, ALU.add))
            v.wait_ge(S["route_exp"], 2)
            link(TS(sm["gp"], sm["tt"], 1.0, None, ALU.add))
            link(TT(sm["gp"], sm["gp"], sm["gs"], ALU.mult))
            link(v.reciprocal(sm["w1"], sm["gp"]))
            link(TT(sm["w2"], sm["w1"], sm["tt"], ALU.mult))
            src = ready(v, "rank")
            tell(v.tensor_copy(pos.rearrange("p a b -> p (a b)"), src[:, 0:NT * NE]), "routed")
            v.wait_ge(S["routed"], 2)
            v.wait_ge(S["M_onehot"], 1)
            v.wait_ge(S["codes"], 4)
            for r, oh in enumerate((oh1, oh2)):
                tmp, pr = (rtmp, rtmp2)[r], f"p{r + 1}"
                link(TT(tmp, oh, pos, ALU.mult))
                link(v.tensor_reduce(sm[pr], tmp, AX.X, ALU.add))
                for c in range(NT):
                    ins = TS(row_of[:, r, c, :], rank_row, sm[pr][:, c:c + 1], None, ALU.is_equal)
                    if c == NT - 1:
                        ins.then_inc(S["M_onehot"], 1) if r == 1 else link(ins)
                    else:
                        link(ins)
            TS(sm["v1"], sm["p1"], float(CAP), None, ALU.is_lt).then_inc(S["codes"], 1)
            TS(sm["v2"], sm["p2"], float(CAP), None, ALU.is_lt).then_inc(S["codes"], 1)
            src = ready(v, "rows")
            o = src[0:CAP, 0:2 * NE].rearrange("p (a b) -> p a b", a=2)
            link(TS(ridx[0:CAP], o, 0.0, NO_ROW, ALU.is_equal, ALU.mult))
            link(STT(out=ridx[0:CAP], in0=o, scalar=-1.0, in1=ridx[0:CAP], op0=ALU.add, op1=ALU.add))
            v.tensor_copy(row_idx[0:CAP, :, :], ridx[0:CAP]).then_inc(S["idx_ready"], 1)
            link(v.tensor_copy(ovf[:, 1:2], ones[:, 0:1]))
            v.wait_ge(S["codes"], 6)
            for r, (oh, w) in enumerate(((oh1, "w1"), (oh2, "w2"))):
                vr = f"v{r + 1}"
                link(TT(sm["mx"], sm[w], sm[vr], ALU.mult))
                link(TT(sm["ix"], sm[w], sm["mx"], ALU.subtract))
                link(v.tensor_copy(sm[w], sm["mx"]))
                if r == 0:
                    link(TT(cov, oh, col("ix", NE), ALU.mult))
                else:
                    link(TT(rtmp, oh, col("ix", NE), ALU.mult))
                    link(TT(cov, cov, rtmp, ALU.add))
            link(TT(sm["mx"], sm["v1"], sm["v2"], ALU.add))
            link(TS(sm["mx"], sm["mx"], -1.0, 2.0, ALU.mult, ALU.add))
            v.tensor_reduce(ovf[:, 0:1], sm["mx"], AX.X, ALU.add).then_inc(S["ovf_ready"], 1)
            tell(v.tensor_copy(flag_i[0:1, 0:1], ready(v, "flag")[0:1, 0:1]), "flag_ready")

            def ex_het(e, g, j):
                wait(v, "ex_tr", 2 * e + 2)
                wait(v, "ex_u", e - 1)
                v.tensor_copy(heT[j % 2][:, KT // 2:, :], bank[1][:, 0:4 * CAP].rearrange("p (k n) -> p k n", k=4))\
                    .then_inc(S["heT_d"], 1)

            def ex_hid(e, g, j):
                wait(v, "ex_u", e + 1)
                wait(v, "ex_sil", e + 1)
                wait(v, "ex_d1", e - 1)
                TT(hid[:, j % 2, :], sil[:, j % 2, :], bank[3 + 2 * (j % 2)][:, 0:JE * CAP], ALU.mult)\
                    .then_inc(S["ex_hid"], 1)

            def ex_y(e, g, j):
                wait(v, "ex_d1", e + 1)
                wait(v, f"st_y{j % 2}", 32 * g + 16 * (j // 2))
                v.tensor_copy(ysb[j % 2][0:CAP, HALF:D], bank[7][0:CAP, :]).then_inc(S["ex_yd"], 1)

            def trip(g, first=False, last=False):
                for j in range(UN):
                    e = g * UN + j
                    ex_hid(e, g, j)
                    if not (last and j == UN - 1):
                        ex_het(e + 1, g if j < UN - 1 else g + 1, (j + 1) % UN)
                    if not (first and j == 0):
                        ex_y(e - 1, g if j else g - 1, (j - 1) % UN)
                if last:
                    ex_y(e, g, UN - 1)

            ex_het(0, 0, 0)
            trip(0, first=True)
            with v.Fori(1, NE // UN - 1) as g:
                trip(g)
            trip(NE // UN - 1, last=True)

            v.wait_ge(S["flag_ready"], 1)
            fv = v.value_load(flag_i[0:1, 0:1], min_val=0, max_val=2 * T)
            with v.If(fv > 0):
                v.wait_ge(S["st_y0"], 16 * NE // 2)
                v.wait_ge(S["st_y1"], 16 * NE // 2)
                v.wait_ge(S["ex_d1"], NE)
                v.engine_nop().then_inc(S["ov_shift"], 1)
                v.engine_nop().then_inc(S["ov_hid"], 1)
                v.engine_nop().then_inc(S["ov_acc"], 1)
                with v.Fori(0, NE) as e:
                    for m in range(JE):
                        v.wait_ge(S["ov_gu"], 2 * (e * JE + m) + 2)
                        v.wait_ge(S["ov_sil"], e * JE + m + 1)
                        TT(ohid[:, m, :], osil, bank[1][:], ALU.mult).then_inc(S["ov_hid"], 1)
                    for c in range(NT):
                        for hf in range(NH2):
                            v.wait_ge(S["ov_d"], e * 2 * NT + c * NH2 + hf + 1)
                            xx = x1[:, c, hf * HALF:(hf + 1) * HALF]
                            ins = STT(out=xx, in0=bank[2][:], scalar=cov[:, c, 0:1], in1=xx, op0=ALU.mult, op1=ALU.add)
                            ins.then_inc(S["ov_acc"], 1)
                    v.tensor_copy(rtmp[:, :, 0:NE - 1], cov[:, :, 1:NE]).then_inc(S["ov_shift"], 1)
                    v.wait_ge(S["ov_shift"], e * 2 + 2)
                    v.tensor_copy(cov[:, :, 0:NE - 1], rtmp[:, :, 0:NE - 1]).then_inc(S["ov_shift"], 1)
                    v.wait_ge(S["ov_shift"], e * 2 + 3)
                v.wait_ge(S["ov_acc"], 2 * NT * NE + 1)
            v.engine_nop().then_inc(S["ov_over"], 1)

            v.wait_ge(S["ld_part2"], 64)

            def final(c):
                v.wait_ge(S["rms3"], c + 1)
                link(v.reciprocal(sm["gm"][:, c:c + 1], sm["r3"][:, c:c + 1]))
                STT(out=x1[:, c, :], in0=x1[:, c, :], scalar=sm["gm"][:, c:c + 1], in1=gain3, op0=ALU.mult,
                    op1=ALU.mult).then_inc(S["out_ready"], 1)

            for c in range(NT):
                v.wait_ge(S[f"ld_x{c}"], 48)
                for r in range(2):
                    ins = STT(out=x1[:, c, :], in0=gath[c][:, r, :], scalar=sm[f"w{r + 1}"][:, c:c + 1], in1=x1[:, c, :],
                              op0=ALU.mult, op1=ALU.add)
                    if r == 0:
                        link(ins)
                    else:
                        ins.then_inc(S["x2_ready"], 1)
                if c > 0:
                    final(c - 1)
            final(NT - 1)


_INS = ['x', 'norm_mix_gain', 'w_in', 'conv_dw_w', 'conv_dw_b', 'conv_ln_gain', 'conv_ln_bias', 'w_conv_out',
        'gdn_conv_w', 'gdn_a_log', 'gdn_dt_bias', 'gdn_norm_gain', 'w_gdn_out', 'w_out', 'norm_ffn_gain',
        'w_router_group', 'b_router_group', 'w_router_expert', 'b_router_expert', 'w_expert_gate', 'w_expert_up',
        'w_expert_down', 'final_norm_gain']
CAP = 96


def kernel(**inputs):
    import numpy as np
    import concourse.bacc as bacc
    from concourse.bass_utils import run_bass_kernel_spmd

    nc = bacc.Bacc("TRN2", target_bir_lowering=False, num_devices=1)
    arrays, args = {}, {}
    for name in _INS:
        v = np.ascontiguousarray(inputs[name])
        arrays[f"in_{name}_dram"] = v
        args[name] = nc.dram_tensor(f"in_{name}_dram", v.shape, mybir.dt.from_np(v.dtype), kind="ExternalInput").ap()
    shape = inputs["x"].shape
    out = nc.dram_tensor("out_0_dram", shape, F32, kind="ExternalOutput").ap()
    h2_rows = nc.dram_tensor("h2_rows", (shape[1], shape[2]), F32, kind="Internal").ap()
    y_rows = nc.dram_tensor("y_rows", (2 * shape[1], shape[2]), F32, kind="Internal").ap()
    low_h = nc.dram_tensor("low_h", (P, shape[2] // P * shape[1]), F32, kind="Internal").ap()
    hybrid_layer(nc, args, out, h2_rows, y_rows, low_h, CAP)
    r = run_bass_kernel_spmd(nc, [arrays], core_ids=[0])
    return r.results[0]["out_0_dram"]
```
